# Optimizing a Trainium2 kernel written in Bass

```python
import math
import jax
import jax.numpy as jnp
from jax import lax
import numpy as np
import jax, jax.numpy as jnp

D_MODEL = 1024
BATCH = 1
SEQ = 512
DEPTH = 1

CHUNK = 64
EPS = 1e-6
NEG_INF = -1e30
ATT_HEADS = 8
ATT_HEAD_DIM = 64
ATT_WIDTH = ATT_HEADS * ATT_HEAD_DIM
LEFT_CHUNKS = 8
BAND_CHUNKS = LEFT_CHUNKS + 1
BAND = BAND_CHUNKS * CHUNK
REL_MAX = 128
REL_BUCKETS = (CHUNK - 1) + REL_MAX + 1
SSM_WIDTH = D_MODEL - ATT_WIDTH
SSM_GROUP = 16
SSM_GROUPS = SSM_WIDTH // SSM_GROUP
SSM_STATE = 64
MIX_WIDTH = ATT_WIDTH + SSM_WIDTH
IN_WIDTH = 3 * ATT_WIDTH + SSM_WIDTH
MEM_LEN = 256
MEM_HEADS = 4
MEM_HEAD_DIM = D_MODEL // MEM_HEADS
PEER_HEADS = 8
PEER_KEYS = 128
PEER_EXPERTS = PEER_KEYS * PEER_KEYS
PEER_TOPK = 16
PEER_QDIM = 256
PEER_BLOCK = 128


def _rmsnorm(x, g):
    xf = x.astype(jnp.float32)
    y = xf * lax.rsqrt(jnp.mean(xf * xf, axis=-1, keepdims=True) + EPS)
    return (y * g.astype(jnp.float32)).astype(x.dtype)

def _band_bias(rel_bias):
    qi = jnp.arange(CHUNK)
    kj = jnp.arange(BAND)
    dist = LEFT_CHUNKS * CHUNK + qi[:, None] - kj[None, :]
    bucket = jnp.clip(dist, -(CHUNK - 1), REL_MAX) + (CHUNK - 1)
    return rel_bias[:, bucket]

def _chunked_attention(q, k, v, rel_bias):
    bsz, seq = q.shape[0], q.shape[1]
    nc = seq // CHUNK
    shp = (bsz, nc, CHUNK, ATT_HEADS, ATT_HEAD_DIM)
    qc = q.reshape(shp)
    pad = ((0, 0), (LEFT_CHUNKS, 0), (0, 0), (0, 0), (0, 0))
    kp = jnp.pad(k.reshape(shp), pad)
    vp = jnp.pad(v.reshape(shp), pad)
    idx = jnp.arange(nc)[:, None] + jnp.arange(BAND_CHUNKS)[None, :]
    band_shp = (bsz, nc, BAND, ATT_HEADS, ATT_HEAD_DIM)
    kb = kp[:, idx].reshape(band_shp)
    vb = vp[:, idx].reshape(band_shp)
    s = jnp.einsum('bnqhd,bnkhd->bhnqk', qc, kb).astype(jnp.float32) * (ATT_HEAD_DIM ** -0.5)
    s = s + _band_bias(rel_bias).astype(jnp.float32)[None, :, None]
    key_chunk = jnp.arange(nc)[:, None] - LEFT_CHUNKS + (jnp.arange(BAND) // CHUNK)[None, :]
    s = jnp.where((key_chunk >= 0)[None, None, :, None, :], s, NEG_INF)
    p = jax.nn.softmax(s, axis=-1).astype(v.dtype)
    o = jnp.einsum('bhnqk,bnkhd->bnqhd', p, vb)
    return o.reshape(bsz, seq, ATT_WIDTH)

def _complex_affine_combine(c1, c2):
    a1r, a1i, b1r, b1i = c1
    a2r, a2i, b2r, b2i = c2
    ar = a2r * a1r - a2i * a1i
    ai = a2r * a1i + a2i * a1r
    br = a2r * b1r - a2i * b1i + b2r
    bi = a2r * b1i + a2i * b1r + b2i
    return (ar, ai, br, bi)

def _s5_mixer(u, lam_re, lam_im, log_step, b_re, b_im, c_re, c_im, d_skip, w_glu, b_glu):
    bsz, seq = u.shape[0], u.shape[1]
    uf = u.astype(jnp.float32).reshape(bsz, seq, SSM_GROUPS, SSM_GROUP)
    step = jnp.exp(log_step.astype(jnp.float32))[:, None]
    lr = lam_re.astype(jnp.float32)
    li = lam_im.astype(jnp.float32)
    mag = jnp.exp(lr * step)
    ar = mag * jnp.cos(li * step)
    ai = mag * jnp.sin(li * step)
    zr = ar - 1.0
    den = lr * lr + li * li
    fr = (zr * lr + ai * li) / den
    fi = (ai * lr - zr * li) / den
    br = b_re.astype(jnp.float32)
    bi = b_im.astype(jnp.float32)
    bbr = fr[..., None] * br - fi[..., None] * bi
    bbi = fr[..., None] * bi + fi[..., None] * br
    bu_r = jnp.einsum('blgc,gpc->blgp', uf, bbr)
    bu_i = jnp.einsum('blgc,gpc->blgp', uf, bbi)
    a_r = jnp.broadcast_to(ar, bu_r.shape)
    a_i = jnp.broadcast_to(ai, bu_i.shape)
    _, _, xr, xi = lax.associative_scan(_complex_affine_combine, (a_r, a_i, bu_r, bu_i), axis=1)
    y = (jnp.einsum('blgp,gcp->blgc', xr, c_re.astype(jnp.float32))
         - jnp.einsum('blgp,gcp->blgc', xi, c_im.astype(jnp.float32))
         + d_skip.astype(jnp.float32) * uf)
    y = jax.nn.gelu(y.reshape(bsz, seq, SSM_WIDTH), approximate=False)
    y = y * jax.nn.sigmoid(y @ w_glu.astype(jnp.float32) + b_glu.astype(jnp.float32))
    return y.astype(u.dtype)

def _memory_attention(hn, memn, w_q, w_k, w_v, q_g, k_g, w_o):
    bsz, seq = hn.shape[0], hn.shape[1]
    m = memn.shape[1]
    q = _rmsnorm((hn @ w_q).reshape(bsz, seq, MEM_HEADS, MEM_HEAD_DIM), q_g)
    k = _rmsnorm((memn @ w_k).reshape(bsz, m, MEM_HEADS, MEM_HEAD_DIM), k_g)
    v = (memn @ w_v).reshape(bsz, m, MEM_HEADS, MEM_HEAD_DIM)
    s = jnp.einsum('blhd,bmhd->bhlm', q, k).astype(jnp.float32) * (MEM_HEAD_DIM ** -0.5)
    p = jax.nn.softmax(s, axis=-1).astype(v.dtype)
    o = jnp.einsum('bhlm,bmhd->blhd', p, v).reshape(bsz, seq, D_MODEL)
    return o @ w_o

def _peer_ffn(hn, w_q, sub_keys, u_tab, v_tab):
    bsz, seq, d = hn.shape
    tokens = hn.reshape(-1, PEER_BLOCK, d)

    def block(xb):
        q = (xb @ w_q).reshape(PEER_BLOCK, PEER_HEADS, 2, PEER_QDIM // 2)
        s = jnp.einsum('thsd,hsnd->thsn', q, sub_keys).astype(jnp.float32)
        sv, si = lax.top_k(s, PEER_TOPK)
        cand = (sv[:, :, 0, :, None] + sv[:, :, 1, None, :]).reshape(PEER_BLOCK, PEER_HEADS, -1)
        cidx = (si[:, :, 0, :, None] * PEER_KEYS + si[:, :, 1, None, :]).reshape(PEER_BLOCK, PEER_HEADS, -1)
        top, pos = lax.top_k(cand, PEER_TOPK)
        e = jnp.take_along_axis(cidx, pos, axis=-1)
        g = jax.nn.softmax(top, axis=-1)
        act = jax.nn.gelu(jnp.einsum('thkd,td->thk', u_tab[e], xb), approximate=False)
        w = (g * act).astype(xb.dtype)
        return jnp.einsum('thk,thkd->td', w, v_tab[e])

    return lax.map(block, tokens).reshape(bsz, seq, d)

def first_inputs(seed: int = 0) -> dict:
    key = jax.random.key(seed)
    ks = iter(jax.random.split(key, 40))

    def nrm(shape, scale):
        return scale * jax.random.normal(next(ks), shape, jnp.float32)

    def gain(n):
        return 1.0 + nrm((DEPTH, n), 0.02)

    x = nrm((BATCH, SEQ, D_MODEL), 1.0)
    mem = nrm((BATCH, MEM_LEN, D_MODEL), 1.0)
    norm_mix_g = gain(D_MODEL)
    w_in = nrm((DEPTH, D_MODEL, IN_WIDTH), D_MODEL ** -0.5)
    att_q_g = gain(ATT_HEAD_DIM)
    att_k_g = gain(ATT_HEAD_DIM)
    rel_bias = nrm((DEPTH, ATT_HEADS, REL_BUCKETS), 0.5)
    ssm_lam_re = -0.5 + nrm((DEPTH, SSM_GROUPS, SSM_STATE), 0.01)
    ssm_lam_im = math.pi * jnp.arange(SSM_STATE, dtype=jnp.float32) + nrm((DEPTH, SSM_GROUPS, SSM_STATE), 0.01)
    ssm_log_step = jax.random.uniform(next(ks), (DEPTH, SSM_GROUPS), jnp.float32, math.log(1e-3), math.log(1e-1))
    ssm_b_re = nrm((DEPTH, SSM_GROUPS, SSM_STATE, SSM_GROUP), (2 * SSM_GROUP) ** -0.5)
    ssm_b_im = nrm((DEPTH, SSM_GROUPS, SSM_STATE, SSM_GROUP), (2 * SSM_GROUP) ** -0.5)
    ssm_c_re = nrm((DEPTH, SSM_GROUPS, SSM_GROUP, SSM_STATE), (2 * SSM_STATE) ** -0.5)
    ssm_c_im = nrm((DEPTH, SSM_GROUPS, SSM_GROUP, SSM_STATE), (2 * SSM_STATE) ** -0.5)
    ssm_d = nrm((DEPTH, SSM_GROUPS, SSM_GROUP), 1.0)
    ssm_w_glu = nrm((DEPTH, SSM_WIDTH, SSM_WIDTH), SSM_WIDTH ** -0.5)
    ssm_b_glu = nrm((DEPTH, SSM_WIDTH), 0.01)
    att_out_g = gain(ATT_WIDTH)
    ssm_out_g = gain(SSM_WIDTH)
    w_out = nrm((DEPTH, MIX_WIDTH, D_MODEL), MIX_WIDTH ** -0.5)
    norm_mem_g = gain(D_MODEL)
    norm_memkv_g = gain(D_MODEL)
    w_mem_q = nrm((DEPTH, D_MODEL, D_MODEL), D_MODEL ** -0.5)
    w_mem_k = nrm((DEPTH, D_MODEL, D_MODEL), D_MODEL ** -0.5)
    w_mem_v = nrm((DEPTH, D_MODEL, D_MODEL), D_MODEL ** -0.5)
    mem_q_g = gain(MEM_HEAD_DIM)
    mem_k_g = gain(MEM_HEAD_DIM)
    w_mem_o = nrm((DEPTH, D_MODEL, D_MODEL), D_MODEL ** -0.5)
    norm_peer_g = gain(D_MODEL)
    w_peer_q = nrm((DEPTH, D_MODEL, PEER_HEADS * PEER_QDIM), D_MODEL ** -0.5)
    peer_keys = nrm((DEPTH, PEER_HEADS, 2, PEER_KEYS, PEER_QDIM // 2), (PEER_QDIM // 2) ** -0.5)
    peer_u = nrm((DEPTH, PEER_EXPERTS, D_MODEL), D_MODEL ** -0.5)
    peer_v = nrm((DEPTH, PEER_EXPERTS, D_MODEL), PEER_HEADS ** -0.5)
    return {'x': x, 'mem': mem, 'norm_mix_g': norm_mix_g, 'w_in': w_in,
            'att_q_g': att_q_g, 'att_k_g': att_k_g, 'rel_bias': rel_bias,
            'ssm_lam_re': ssm_lam_re, 'ssm_lam_im': ssm_lam_im, 'ssm_log_step': ssm_log_step,
            'ssm_b_re': ssm_b_re, 'ssm_b_im': ssm_b_im, 'ssm_c_re': ssm_c_re, 'ssm_c_im': ssm_c_im,
            'ssm_d': ssm_d, 'ssm_w_glu': ssm_w_glu, 'ssm_b_glu': ssm_b_glu,
            'att_out_g': att_out_g, 'ssm_out_g': ssm_out_g, 'w_out': w_out,
            'norm_mem_g': norm_mem_g, 'norm_memkv_g': norm_memkv_g,
            'w_mem_q': w_mem_q, 'w_mem_k': w_mem_k, 'w_mem_v': w_mem_v,
            'mem_q_g': mem_q_g, 'mem_k_g': mem_k_g, 'w_mem_o': w_mem_o,
            'norm_peer_g': norm_peer_g, 'w_peer_q': w_peer_q, 'peer_keys': peer_keys,
            'peer_u': peer_u, 'peer_v': peer_v}

def first_block(x, mem, norm_mix_g, w_in, att_q_g, att_k_g, rel_bias,
              ssm_lam_re, ssm_lam_im, ssm_log_step, ssm_b_re, ssm_b_im, ssm_c_re, ssm_c_im,
              ssm_d, ssm_w_glu, ssm_b_glu, att_out_g, ssm_out_g, w_out,
              norm_mem_g, norm_memkv_g, w_mem_q, w_mem_k, w_mem_v, mem_q_g, mem_k_g, w_mem_o,
              norm_peer_g, w_peer_q, peer_keys, peer_u, peer_v):
    bsz, seq = x.shape[0], x.shape[1]
    h = x
    for l in range(DEPTH):
        proj = _rmsnorm(h, norm_mix_g[l]) @ w_in[l]
        q = proj[..., :ATT_WIDTH].reshape(bsz, seq, ATT_HEADS, ATT_HEAD_DIM)
        k = proj[..., ATT_WIDTH:2 * ATT_WIDTH].reshape(bsz, seq, ATT_HEADS, ATT_HEAD_DIM)
        v = proj[..., 2 * ATT_WIDTH:3 * ATT_WIDTH].reshape(bsz, seq, ATT_HEADS, ATT_HEAD_DIM)
        u = proj[..., 3 * ATT_WIDTH:]
        att = _chunked_attention(_rmsnorm(q, att_q_g[l]), _rmsnorm(k, att_k_g[l]), v, rel_bias[l])
        ssm = _s5_mixer(u, ssm_lam_re[l], ssm_lam_im[l], ssm_log_step[l], ssm_b_re[l], ssm_b_im[l],
                        ssm_c_re[l], ssm_c_im[l], ssm_d[l], ssm_w_glu[l], ssm_b_glu[l])
        mixed = jnp.concatenate([_rmsnorm(att, att_out_g[l]), _rmsnorm(ssm, ssm_out_g[l])], axis=-1)
        h = h + mixed @ w_out[l]
        h = h + _memory_attention(_rmsnorm(h, norm_mem_g[l]), _rmsnorm(mem, norm_memkv_g[l]),
                                  w_mem_q[l], w_mem_k[l], w_mem_v[l], mem_q_g[l], mem_k_g[l], w_mem_o[l])
        h = h + _peer_ffn(_rmsnorm(h, norm_peer_g[l]), w_peer_q[l], peer_keys[l], peer_u[l], peer_v[l])
    return h


HEAD_DIM = 64
ROPE_THETA = 10000.0
NEG_INF_2 = -1e30

DIL_GROUPS = ((128, 1), (512, 4), (2048, 16))
N_DIL_GROUPS = 3
DIL_HEADS_PER_GROUP = 4
DIL_HEADS = N_DIL_GROUPS * DIL_HEADS_PER_GROUP
DIL_WIDTH = DIL_HEADS * HEAD_DIM
DIL_OUT = DIL_HEADS_PER_GROUP * HEAD_DIM

DIFF_HEADS = D_MODEL // (2 * HEAD_DIM)
DIFF_QK_WIDTH = DIFF_HEADS * 2 * HEAD_DIM
DIFF_V_WIDTH = DIFF_HEADS * 2 * HEAD_DIM
DIFF_Q_BLOCK = 128

N_BRANCHES = 2
GATE_WIDTH = N_BRANCHES * D_MODEL
IN_WIDTH_2 = 3 * DIL_WIDTH + 2 * DIFF_QK_WIDTH + DIFF_V_WIDTH + GATE_WIDTH
IN_SPLITS = (DIL_WIDTH, 2 * DIL_WIDTH, 3 * DIL_WIDTH,
             3 * DIL_WIDTH + DIFF_QK_WIDTH,
             3 * DIL_WIDTH + 2 * DIFF_QK_WIDTH,
             3 * DIL_WIDTH + 2 * DIFF_QK_WIDTH + DIFF_V_WIDTH)

PEER_N_KEYS = 128
PEER_N_EXPERTS = PEER_N_KEYS * PEER_N_KEYS
PEER_QUERY_DIM = 256
PEER_HALF = PEER_QUERY_DIM // 2
PEER_CHUNK = 128


def rms_norm(x, g):
    xf = x.astype(jnp.float32)
    y = xf * lax.rsqrt(jnp.mean(xf * xf, axis=-1, keepdims=True) + EPS)
    return (y * g.astype(jnp.float32)).astype(x.dtype)

def rope(x, positions):
    hd = x.shape[-1]
    inv_freq = 1.0 / (ROPE_THETA ** (jnp.arange(0, hd, 2, dtype=jnp.float32) / hd))
    ang = positions.astype(jnp.float32)[:, :, None, None] * inv_freq
    cos, sin = jnp.cos(ang), jnp.sin(ang)
    xf = x.astype(jnp.float32)
    x1, x2 = xf[..., : hd // 2], xf[..., hd // 2:]
    return jnp.concatenate([x1 * cos - x2 * sin, x2 * cos + x1 * sin], axis=-1).astype(x.dtype)

def dilated_window_attention(q, k, v, window, dilation):
    b, s, h, hd = q.shape
    m = window // (2 * dilation)
    blk = m
    L = s // dilation
    nb = -(-L // blk)
    Lp = nb * blk

    def to_res(t):
        return t.reshape(b, L, dilation, h, hd).transpose(0, 2, 3, 1, 4)

    qr = jnp.pad(to_res(q), ((0, 0), (0, 0), (0, 0), (0, Lp - L), (0, 0)))
    kpad = ((0, 0), (0, 0), (0, 0), (blk, Lp - L + blk), (0, 0))
    kp = jnp.pad(to_res(k), kpad)
    vp = jnp.pad(to_res(v), kpad)
    qb = qr.reshape(b, dilation, h, nb, blk, hd)

    def band(t):
        tb = t.reshape(b, dilation, h, nb + 2, blk, hd)
        return jnp.concatenate([tb[:, :, :, :-2], tb[:, :, :, 1:-1], tb[:, :, :, 2:]], axis=4)

    kb, vb = band(kp), band(vp)
    scores = jnp.einsum('brhnqc,brhnkc->brhnqk', qb, kb).astype(jnp.float32) * (hd ** -0.5)
    qi = jnp.arange(nb)[:, None, None] * blk + jnp.arange(blk)[None, :, None]
    ki = jnp.arange(nb)[:, None, None] * blk - blk + jnp.arange(3 * blk)[None, None, :]
    mask = (jnp.abs(ki - qi) <= m) & (ki >= 0) & (ki < L)
    scores = jnp.where(mask, scores, NEG_INF_2)
    lse = jax.nn.logsumexp(scores, axis=-1)
    p = jnp.exp(scores - lse[..., None])
    out = jnp.einsum('brhnqk,brhnkc->brhnqc', p.astype(v.dtype), vb)
    out = out.reshape(b, dilation, h, Lp, hd)[:, :, :, :L]
    out = out.transpose(0, 3, 1, 2, 4).reshape(b, s, h, hd)
    lse = lse.reshape(b, dilation, h, Lp)[..., :L].transpose(0, 3, 1, 2).reshape(b, s, h)
    return out, lse

def differential_attention(q1, q2, k1, k2, v, lam):
    b, s, h, hd = q1.shape
    nqb = s // DIFF_Q_BLOCK
    scale = hd ** -0.5

    def blockify(t):
        return t.reshape(b, nqb, DIFF_Q_BLOCK, h, hd).transpose(1, 0, 2, 3, 4)

    def one_block(qs):
        qa, qb = qs
        s1 = jnp.einsum('bqhc,bkhc->bhqk', qa, k1).astype(jnp.float32) * scale
        s2 = jnp.einsum('bqhc,bkhc->bhqk', qb, k2).astype(jnp.float32) * scale
        a = jax.nn.softmax(s1, axis=-1) - lam * jax.nn.softmax(s2, axis=-1)
        return jnp.einsum('bhqk,bkhc->bqhc', a.astype(v.dtype), v)

    out = lax.map(one_block, (blockify(q1), blockify(q2)))
    return out.transpose(1, 0, 2, 3, 4).reshape(b, s, h, 2 * hd)

def peer_ffn(h, w_query, sub_keys, expert_u, expert_v):
    b, s, d = h.shape
    tokens = h.reshape((b * s) // PEER_CHUNK, PEER_CHUNK, d)

    def chunk(xc):
        q = (xc @ w_query).reshape(PEER_CHUNK, PEER_HEADS, 2, PEER_HALF)
        s1 = jnp.einsum('thc,hnc->thn', q[:, :, 0], sub_keys[:, 0]).astype(jnp.float32)
        s2 = jnp.einsum('thc,hnc->thn', q[:, :, 1], sub_keys[:, 1]).astype(jnp.float32)
        v1, i1 = lax.top_k(s1, PEER_TOPK)
        v2, i2 = lax.top_k(s2, PEER_TOPK)
        cand = (v1[..., :, None] + v2[..., None, :]).reshape(PEER_CHUNK, PEER_HEADS, PEER_TOPK * PEER_TOPK)
        top, ci = lax.top_k(cand, PEER_TOPK)
        e1 = jnp.take_along_axis(i1, ci // PEER_TOPK, axis=-1)
        e2 = jnp.take_along_axis(i2, ci % PEER_TOPK, axis=-1)
        eidx = e1 * PEER_N_KEYS + e2
        gate = jax.nn.softmax(top, axis=-1)
        u = expert_u[eidx]
        vv = expert_v[eidx]
        act = jax.nn.gelu(jnp.einsum('td,thkd->thk', xc, u).astype(jnp.float32), approximate=False)
        wts = (gate * act).astype(xc.dtype)
        return jnp.einsum('thk,thkd->td', wts, vv)

    return lax.map(chunk, tokens).reshape(b, s, d)

def hybrid_layer(x, c, positions, lam_init, w_ada, b_ada, norm1_g, w_in, b_gate,
                 qn_a, kn_a, w_proj_a, qn_b, kn_b, lam_q1, lam_k1, lam_q2, lam_k2,
                 subln_g, w_proj_b, w_out, norm2_g, w_query, sub_keys, expert_u, expert_v):
    b, s, d = x.shape
    mod = jax.nn.silu(c) @ w_ada + b_ada
    sh1, sc1, g1, sh2, sc2, g2 = [m[:, None, :] for m in jnp.split(mod, 6, axis=-1)]

    h = rms_norm(x, norm1_g) * (1 + sc1) + sh1
    proj = h @ w_in
    qa, ka, va, qb, kb, vb, gl = jnp.split(proj, IN_SPLITS, axis=-1)

    qa = rope(rms_norm(qa.reshape(b, s, DIL_HEADS, HEAD_DIM), qn_a), positions)
    ka = rope(rms_norm(ka.reshape(b, s, DIL_HEADS, HEAD_DIM), kn_a), positions)
    va = va.reshape(b, s, DIL_HEADS, HEAD_DIM)
    outs, lses = [], []
    for gi, (win, dil) in enumerate(DIL_GROUPS):
        sl = slice(gi * DIL_HEADS_PER_GROUP, (gi + 1) * DIL_HEADS_PER_GROUP)
        o, l = dilated_window_attention(qa[:, :, sl], ka[:, :, sl], va[:, :, sl], win, dil)
        outs.append(o)
        lses.append(l)
    wg = jax.nn.softmax(jnp.stack(lses), axis=0)
    oa = jnp.sum(wg[..., None] * jnp.stack(outs).astype(jnp.float32), axis=0).astype(x.dtype)
    branch_a = oa.reshape(b, s, DIL_OUT) @ w_proj_a

    qb = rms_norm(qb.reshape(b, s, DIFF_HEADS, 2, HEAD_DIM), qn_b)
    kb = rms_norm(kb.reshape(b, s, DIFF_HEADS, 2, HEAD_DIM), kn_b)
    q1, q2 = rope(qb[:, :, :, 0], positions), rope(qb[:, :, :, 1], positions)
    k1, k2 = rope(kb[:, :, :, 0], positions), rope(kb[:, :, :, 1], positions)
    f32 = jnp.float32
    lam = (jnp.exp(jnp.sum(lam_q1.astype(f32) * lam_k1.astype(f32)))
           - jnp.exp(jnp.sum(lam_q2.astype(f32) * lam_k2.astype(f32))) + lam_init)
    ob = differential_attention(q1, q2, k1, k2, vb.reshape(b, s, DIFF_HEADS, 2 * HEAD_DIM), lam)
    ob = rms_norm(ob, subln_g) * (1.0 - lam_init)
    branch_b = ob.reshape(b, s, DIFF_V_WIDTH) @ w_proj_b

    gates = jax.nn.sigmoid((gl + b_gate).astype(f32)).astype(x.dtype).reshape(b, s, N_BRANCHES, d)
    mixed = gates[:, :, 0] * branch_a + gates[:, :, 1] * branch_b
    x = x + g1 * (mixed @ w_out)

    h2 = rms_norm(x, norm2_g) * (1 + sc2) + sh2
    x = x + g2 * peer_ffn(h2, w_query, sub_keys, expert_u, expert_v)
    return x

def second_inputs(seed: int = 0) -> dict:
    key = jax.random.key(seed)
    ks = jax.random.split(key, 32)
    f32 = jnp.float32

    def nrm(k, shape, scale):
        return jax.random.normal(k, shape, f32) * scale

    def gain(k, shape):
        return 1.0 + 0.02 * jax.random.normal(k, shape, f32)

    L = DEPTH
    D = D_MODEL
    return {
        "x": jax.random.normal(ks[0], (BATCH, SEQ, D), f32),
        "c": jax.random.normal(ks[1], (BATCH, D), f32),
        "positions": jnp.broadcast_to(jnp.arange(SEQ, dtype=jnp.int32), (BATCH, SEQ)),
        "w_ada": nrm(ks[2], (L, D, 6 * D), 0.5 * D ** -0.5),
        "b_ada": nrm(ks[3], (L, 6 * D), 0.02),
        "norm1_g": gain(ks[4], (L, D)),
        "w_in": nrm(ks[5], (L, D, IN_WIDTH_2), D ** -0.5),
        "b_gate": nrm(ks[6], (L, GATE_WIDTH), 0.02),
        "qn_a": gain(ks[7], (L, HEAD_DIM)),
        "kn_a": gain(ks[8], (L, HEAD_DIM)),
        "w_proj_a": nrm(ks[9], (L, DIL_OUT, D), DIL_OUT ** -0.5),
        "qn_b": gain(ks[10], (L, HEAD_DIM)),
        "kn_b": gain(ks[11], (L, HEAD_DIM)),
        "lam_q1": nrm(ks[12], (L, HEAD_DIM), 0.1),
        "lam_k1": nrm(ks[13], (L, HEAD_DIM), 0.1),
        "lam_q2": nrm(ks[14], (L, HEAD_DIM), 0.1),
        "lam_k2": nrm(ks[15], (L, HEAD_DIM), 0.1),
        "subln_g": gain(ks[16], (L, 2 * HEAD_DIM)),
        "w_proj_b": nrm(ks[17], (L, DIFF_V_WIDTH, D), DIFF_V_WIDTH ** -0.5),
        "w_out": nrm(ks[18], (L, D, D), D ** -0.5),
        "norm2_g": gain(ks[19], (L, D)),
        "w_query": nrm(ks[20], (L, D, PEER_HEADS * PEER_QUERY_DIM), D ** -0.5),
        "sub_keys": nrm(ks[21], (L, PEER_HEADS, 2, PEER_N_KEYS, PEER_HALF), PEER_HALF ** -0.5),
        "expert_u": nrm(ks[22], (L, PEER_N_EXPERTS, D), D ** -0.5),
        "expert_v": nrm(ks[23], (L, PEER_N_EXPERTS, D), PEER_HEADS ** -0.5),
    }

def second_block(x, c, positions, w_ada, b_ada, norm1_g, w_in, b_gate, qn_a, kn_a, w_proj_a,
              qn_b, kn_b, lam_q1, lam_k1, lam_q2, lam_k2, subln_g, w_proj_b, w_out,
              norm2_g, w_query, sub_keys, expert_u, expert_v):
    for l in range(DEPTH):
        lam_init = 0.8 - 0.6 * math.exp(-0.3 * l)
        x = hybrid_layer(x, c, positions, lam_init, w_ada[l], b_ada[l], norm1_g[l], w_in[l],
                         b_gate[l], qn_a[l], kn_a[l], w_proj_a[l], qn_b[l], kn_b[l],
                         lam_q1[l], lam_k1[l], lam_q2[l], lam_k2[l], subln_g[l], w_proj_b[l],
                         w_out[l], norm2_g[l], w_query[l], sub_keys[l], expert_u[l], expert_v[l])
    return x


def setup_inputs(seed=0):
    out = dict(first_inputs(seed))
    for name, value in second_inputs(seed + 1).items():
        if name != "x":
            out[name + "_2"] = value
    return out


def reference(
    x, mem, norm_mix_g, w_in, att_q_g, att_k_g, rel_bias, ssm_lam_re, ssm_lam_im, ssm_log_step,
    ssm_b_re, ssm_b_im, ssm_c_re, ssm_c_im, ssm_d, ssm_w_glu, ssm_b_glu, att_out_g, ssm_out_g,
    w_out, norm_mem_g, norm_memkv_g, w_mem_q, w_mem_k, w_mem_v, mem_q_g, mem_k_g, w_mem_o,
    norm_peer_g, w_peer_q, peer_keys, peer_u, peer_v, c_2, positions_2, w_ada_2, b_ada_2,
    norm1_g_2, w_in_2, b_gate_2, qn_a_2, kn_a_2, w_proj_a_2, qn_b_2, kn_b_2, lam_q1_2, lam_k1_2,
    lam_q2_2, lam_k2_2, subln_g_2, w_proj_b_2, w_out_2, norm2_g_2, w_query_2, sub_keys_2,
    expert_u_2, expert_v_2,
):
    x = first_block(
        x, mem, norm_mix_g, w_in, att_q_g, att_k_g, rel_bias, ssm_lam_re, ssm_lam_im,
        ssm_log_step, ssm_b_re, ssm_b_im, ssm_c_re, ssm_c_im, ssm_d, ssm_w_glu, ssm_b_glu,
        att_out_g, ssm_out_g, w_out, norm_mem_g, norm_memkv_g, w_mem_q, w_mem_k, w_mem_v,
        mem_q_g, mem_k_g, w_mem_o, norm_peer_g, w_peer_q, peer_keys, peer_u, peer_v,
    )
    return second_block(
        x, c_2, positions_2, w_ada_2, b_ada_2, norm1_g_2, w_in_2, b_gate_2, qn_a_2, kn_a_2,
        w_proj_a_2, qn_b_2, kn_b_2, lam_q1_2, lam_k1_2, lam_q2_2, lam_k2_2, subln_g_2,
        w_proj_b_2, w_out_2, norm2_g_2, w_query_2, sub_keys_2, expert_u_2, expert_v_2,
    )


_drawn_inputs = setup_inputs


def setup_inputs(seed=0):
    import zlib

    import numpy as np

    out = dict(_drawn_inputs(seed))
    spreads = {}
    factors = {'att_q_g': 3.415,
     'att_k_g': 3.067,
     'ssm_lam_re': 64.0,
     'ssm_b_glu': 8.0,
     'att_out_g': 3.282,
     'ssm_out_g': 3.183,
     'norm_mem_g': 8.0,
     'norm_memkv_g': 8.0,
     'mem_q_g': 8.0,
     'mem_k_g': 8.0,
     'norm_peer_g': 2.889,
     'b_ada_2': 4.97,
     'norm1_g_2': 8.0,
     'b_gate_2': 64.0,
     'qn_a_2': 8.0,
     'kn_a_2': 8.0,
     'qn_b_2': 8.0,
     'kn_b_2': 8.0,
     'lam_q1_2': 8.0,
     'lam_k1_2': 8.0,
     'lam_q2_2': 8.0,
     'lam_k2_2': 8.0,
     'subln_g_2': 64.0,
     'norm2_g_2': 32.633}
    for name, (base, spread) in spreads.items():
        noise = np.random.default_rng([zlib.crc32(name.encode()), seed]).standard_normal(out[name].shape)
        drawn = base * np.exp(spread * noise) if base else spread * noise
        out[name] = jnp.asarray(drawn.astype(out[name].dtype))
    for name, factor in factors.items():
        out[name] = (out[name] * factor).astype(out[name].dtype)
    return out
```

```python
from contextlib import ExitStack

import numpy as np
import concourse.bass as bass
from concourse import mybir

F32 = mybir.dt.float32
F32R = mybir.dt.float32r
U32 = mybir.dt.uint32
I32 = mybir.dt.int32
ALU = mybir.AluOpType
ACT = mybir.ActivationFunctionType
AX = mybir.AxisListType

P = 128
SEQ, D = 512, 1024
TT = SEQ // P
DK = D // P
BANK = 512
EPS = 1e-6
MASKED = -1e30

CHUNK = 64
HEADS, HEAD = 8, 64
ATT_W = HEADS * HEAD
SSM_W = D - ATT_W
STATES, GROUP = 64, 16
SSM_GROUPS = SSM_W // GROUP
STILES = SSM_GROUPS * STATES // P
MEM_LEN, MEM_HEADS = 256, 4
MEM_HEAD = D // MEM_HEADS
REL_MAX = 128

KEYS, TOPK, PHEADS = 128, 16, 8
HALVES = 2 * PHEADS
PAIRS = PHEADS * TOPK
EGROUP = 4

DIL_W, DIFF_W = 768, 1024
DIL = ((128, 1), (512, 4), (2048, 16))
DIL_HEADS = 4
DIFF_HEADS = 8
LAM_INIT = 0.2

TWO_PI = 2.0 * float(np.pi)
TWO_PI_A = float(np.float32(6.28125))
TWO_PI_B = float(np.float32(np.floor((TWO_PI - TWO_PI_A) * 2.0**23) / 2.0**23))
TWO_PI_C = float(np.float32(TWO_PI - TWO_PI_A - TWO_PI_B))
ROUND = 12582912.0


def phase_tools(nc, ctx, tag):
    def sb(name, shape, dt=F32):
        return ctx.enter_context(nc.sbuf_tensor(f"{tag}_{name}", shape, dt))

    def ps(name, shape, dt=F32):
        return ctx.enter_context(nc.psum_tensor(f"{tag}_{name}", shape, dt))

    taken = []

    def clear():
        nc.clear_and_free_semaphores(taken)
        nc.all_engine_barrier()

    def sem(name):
        if not taken:
            ctx.callback(clear)
        taken.append(nc.alloc_semaphore(f"{tag}_{name}"))
        return taken[-1]

    return sb, ps, sem


class Chain:
    def __init__(self, eng, sem):
        self.eng, self.sem, self.n = eng, sem, 0

    def add(self, instruction):
        instruction.then_inc(self.sem, 1)
        self.n += 1

    def wait(self):
        self.eng.wait_ge(self.sem, self.n)


def refined_rsqrt(V, chain, meansq, guess, tmp, out):
    chain.add(V.tensor_tensor(tmp, meansq, guess, ALU.mult))
    chain.wait()
    chain.add(V.tensor_tensor(tmp, tmp, guess, ALU.mult))
    chain.wait()
    chain.add(V.tensor_scalar(tmp, tmp, -0.5, 1.5, ALU.mult, ALU.add))
    chain.wait()
    chain.add(V.tensor_tensor(out, tmp, guess, ALU.mult))
    chain.wait()


ON_ACT, ON_DVE = 0, 1


def product(nc, tag, srcT, kt, tokens, chunks, SLABS=4):
    width = max(src.shape[2] for src, _, _ in chunks)
    NCH = len(chunks)

    def evacuated(upto, which):
        return sum(e == which for _, _, units in chunks[:upto + 1] for e, _ in units)

    with ExitStack() as ctx:
        sb, ps, sem = phase_tools(nc, ctx, tag)
        x_hi, x_lo = sb("x_hi", [P, kt, tokens], F32R), sb("x_lo", [P, kt, tokens], F32R)
        w = sb("w", [P, 2, kt, width])
        w_hi, w_lo = sb("w_hi", [P, SLABS, width], F32R), sb("w_lo", [P, SLABS, width], F32R)
        out = ps("out", [P, 8, BANK])
        loaded = [sem("loaded0"), sem("loaded1")]
        x_hi_ready, x_ready, w_hi_ready, w_ready, multiplied = (
            sem(n) for n in ("x_hi_ready", "x_ready", "w_hi_ready", "w_ready", "multiplied"))
        copied = [sem("copied_by_act"), sem("copied_by_dve")]
        step = [sem("step_act"), sem("step_dve")]
        block = ctx.enter_context(nc.Block())

        @block.sync
        def _(sp):
            for c, (src, _, _) in enumerate(chunks):
                if c >= 2:
                    sp.wait_ge(w_ready, kt * (c - 1))
                sp.dma_start(w[:, c % 2, :, 0:src.shape[2]], src).then_inc(loaded[c % 2], 16)

        @block.tensor
        def _(pe):
            for c, (src, on_tokens, units) in enumerate(chunks):
                cols = src.shape[2]
                for which in (ON_ACT, ON_DVE):
                    if c >= 2 and evacuated(c - 2, which):
                        pe.wait_ge(copied[which], evacuated(c - 2, which))
                for k in range(kt):
                    s = (c * kt + k) % SLABS
                    if c == 0:
                        pe.wait_ge(x_ready, k + 1)
                    pe.wait_ge(w_ready, c * kt + k + 1)
                    for u in range(len(units)):
                        tile = slice(u * P, (u + 1) * P)
                        for n, (xs, ws) in enumerate(((x_hi, w_hi), (x_lo, w_hi), (x_hi, w_lo))):
                            if on_tokens:
                                dst, lhsT, rhs = out[:, c % 2 * 4 + u, 0:cols], xs[:, k, tile], ws[:, s, 0:cols]
                            else:
                                dst, lhsT, rhs = out[:, c % 2 * 4 + u, 0:tokens], ws[:, s, tile], xs[:, k, :]
                            last = nc.tensor.matmul(dst, lhsT, rhs, start=(k == 0 and n == 0),
                                                    stop=(k == kt - 1 and n == 2), skip_group_check=True)
                    last.then_inc(multiplied, 1)

        def evacuations(eng, which, c, steps):
            src, on_tokens, units = chunks[c]
            cols = src.shape[2] if on_tokens else tokens
            if any(e == which for e, _ in units):
                eng.wait_ge(multiplied, kt * (c + 1))
            for u, (engine, evacuate) in enumerate(units):
                if engine != which:
                    continue
                parts = evacuate(out[:, c % 2 * 4 + u, 0:cols])
                for make in parts[:-1]:
                    make().then_inc(step[which], 1)
                    steps += 1
                    eng.wait_ge(step[which], steps)
                parts[-1]().then_inc(copied[which], 1)
            return steps

        @block.scalar
        def _(act):
            steps = 0
            for c, (src, _, _) in enumerate(chunks):
                cols = src.shape[2]
                act.wait_ge(loaded[c % 2], 16 * (c // 2 + 1))
                for k in range(kt):
                    s = c * kt + k
                    if c == 0:
                        nc.scalar.copy(x_hi[:, k, :], srcT[:, k, 0:tokens]).then_inc(x_hi_ready, 1)
                    if s >= SLABS:
                        act.wait_ge(multiplied, s - SLABS + 1)
                    nc.scalar.copy(w_hi[:, s % SLABS, 0:cols], w[:, c % 2, k, 0:cols]).then_inc(w_hi_ready, 1)
                if c >= 1:
                    steps = evacuations(act, ON_ACT, c - 1, steps)
            evacuations(act, ON_ACT, NCH - 1, steps)

        @block.vector
        def _(dve):
            steps = 0
            for c, (src, _, _) in enumerate(chunks):
                cols = src.shape[2]
                for k in range(kt):
                    s = c * kt + k
                    if c == 0:
                        dve.wait_ge(x_hi_ready, k + 1)
                        nc.vector.tensor_tensor(x_lo[:, k, :], srcT[:, k, 0:tokens], x_hi[:, k, :],
                                                ALU.subtract).then_inc(x_ready, 1)
                    dve.wait_ge(w_hi_ready, s + 1)
                    nc.vector.tensor_tensor(w_lo[:, s % SLABS, 0:cols], w[:, c % 2, k, 0:cols],
                                            w_hi[:, s % SLABS, 0:cols], ALU.subtract).then_inc(w_ready, 1)
                if c >= 1:
                    steps = evacuations(dve, ON_DVE, c - 1, steps)
            evacuations(dve, ON_DVE, NCH - 1, steps)


def alternate(u):
    return ON_ACT if u % 2 == 0 else ON_DVE


def copy_to(nc, u, dst):
    if alternate(u) == ON_ACT:
        return ON_ACT, lambda psum: [lambda: nc.scalar.copy(dst, psum)]
    return ON_DVE, lambda psum: [lambda: nc.vector.tensor_copy(dst, psum)]


def columns_to(nc, dst, first, cols, tiles):
    return [copy_to(nc, t, dst[:, t, first:first + cols]) for t in range(tiles)]


def heads_norm_transpose(nc, tag, C, src, tiles, heads, hd, dst, gain):
    width = heads * hd
    kt, n = width // P, tiles * P
    with ExitStack() as ctx:
        sb, ps, sem = phase_tools(nc, ctx, tag)
        sq = sb("sq", [P, 2, width])
        sumsq = sb("sumsq", [P, tiles, heads])
        meansq = sb("meansq", [P, tiles, heads])
        rms = sb("rms", [P, tiles, heads])
        guess, tmp, rstd = (sb(n, [P, tiles, heads]) for n in ("guess", "tmp", "rstd"))
        tp = ps("tp", [P, 4, BANK])
        squared, summed, mean_ready, rms_ready, rstd_ready = (
            sem("squared"), sem("summed"), sem("mean_ready"), sem("rms_ready"), sem("rstd_ready"))
        normed, turned, copied = sem("normed"), sem("turned"), [sem("copied_by_act"), sem("copied_by_dve")]
        block = ctx.enter_context(nc.Block())

        @block.scalar
        def _(act):
            for t in range(tiles):
                if t >= 2:
                    act.wait_ge(summed, t - 1)
                nc.scalar.activation(sq[:, t % 2, :], src[:, t, :], ACT.Square).then_inc(squared, 1)
            act.wait_ge(mean_ready, 1)
            nc.scalar.activation(rms[:], meansq[:], ACT.Sqrt).then_inc(rms_ready, 1)
            for k in range(0, kt, 2):
                act.wait_ge(turned, k + 1)
                nc.scalar.activation(dst[:, k, :], tp[:, k % 4, 0:n], ACT.Identity,
                                     scale=gain(k)).then_inc(copied[0], 1)

        @block.vector
        def _(dve):
            for t in range(tiles):
                dve.wait_ge(squared, t + 1)
                nc.vector.tensor_reduce(sumsq[:, t, :], sq[:, t % 2, :].rearrange("p (h d) -> p h d", h=heads),
                                        AX.X, ALU.add).then_inc(summed, 1)
            dve.wait_ge(summed, tiles)
            nc.vector.tensor_scalar(meansq[:], sumsq[:], 1.0 / hd, EPS, ALU.mult, ALU.add).then_inc(mean_ready, 1)
            dve.wait_ge(rms_ready, 1)
            ch = Chain(dve, rstd_ready)
            ch.add(nc.vector.reciprocal(guess[:], rms[:]))
            ch.wait()
            refined_rsqrt(nc.vector, ch, meansq[:], guess[:], tmp[:], rstd[:])
            for t in range(tiles):
                x = src[:, t, :].rearrange("p (h d) -> p h d", h=heads)
                nc.vector.tensor_tensor(x, x, rstd[:, t, :].unsqueeze(2).broadcast_to([P, heads, hd]),
                                        ALU.mult).then_inc(normed, 1)
            for k in range(1, kt, 2):
                dve.wait_ge(turned, k + 1)
                nc.vector.tensor_scalar(dst[:, k, :], tp[:, k % 4, 0:n], gain(k), None,
                                        ALU.mult).then_inc(copied[1], 1)

        @block.tensor
        def _(pe):
            pe.wait_ge(normed, tiles)
            for k in range(kt):
                if k >= 4:
                    pe.wait_ge(copied[k % 2], (k - 4) // 2 + 1)
                for t in range(tiles):
                    last = nc.tensor.transpose(tp[:, k % 4, t * P:(t + 1) * P], src[:, t, k * P:(k + 1) * P],
                                               C["ident"][:])
                last.then_inc(turned, 1)


def feature_norm(nc, tag, C, src, kt, dst, gain, per_tile, factor=1.0):
    groups = kt if per_tile else 1
    width = P if per_tile else kt * P
    with ExitStack() as ctx:
        sb, ps, sem = phase_tools(nc, ctx, tag)
        sq = sb("sq", [P, kt, SEQ])
        meansq = sb("meansq", [P, 2, SEQ])
        rms = sb("rms", [P, 2, SEQ])
        guess, tmp, rstd = (sb(n, [P, 2, SEQ]) for n in ("guess", "tmp", "rstd"))
        tot = ps("tot", [P, 2, BANK])
        squared, totalled, mean_ready, rms_ready, rstd_ready, done = (
            sem("squared"), sem("totalled"), sem("mean_ready"), sem("rms_ready"), sem("rstd_ready"), sem("done"))
        block = ctx.enter_context(nc.Block())

        @block.scalar
        def _(act):
            for k in range(kt):
                nc.scalar.activation(sq[:, k, :], src[:, k, :], ACT.Square).then_inc(squared, 1)
            for g in range(groups):
                act.wait_ge(mean_ready, g + 1)
                if g >= 2:
                    act.wait_ge(rstd_ready, 5 * (g - 1))
                nc.scalar.activation(rms[:, g % 2, :], meansq[:, g % 2, :], ACT.Sqrt).then_inc(rms_ready, 1)

        @block.tensor
        def _(pe):
            for g in range(groups):
                mine = [g] if per_tile else range(kt)
                if g >= 2:
                    pe.wait_ge(mean_ready, g - 1)
                for k in mine:
                    pe.wait_ge(squared, k + 1)
                    last = nc.tensor.matmul(tot[:, g % 2, :], C["ones"][:], sq[:, k, :], start=(k == mine[0]),
                                            stop=(k == mine[-1]))
                last.then_inc(totalled, 1)

        @block.vector
        def _(dve):
            ch = Chain(dve, rstd_ready)
            for g in range(groups):
                dve.wait_ge(totalled, g + 1)
                if g >= 2:
                    dve.wait_ge(rms_ready, g - 1)
                nc.vector.tensor_scalar(meansq[:, g % 2, :], tot[:, g % 2, :], 1.0 / width, EPS, ALU.mult,
                                        ALU.add).then_inc(mean_ready, 1)
                dve.wait_ge(rms_ready, g + 1)
                q = g % 2
                ch.add(nc.vector.reciprocal(guess[:, q, :], rms[:, q, :]))
                ch.wait()
                refined_rsqrt(nc.vector, ch, meansq[:, q, :], guess[:, q, :], tmp[:, q, :], rstd[:, q, :])
                for k in ([g] if per_tile else range(kt)):
                    nc.vector.scalar_tensor_tensor(dst[:, k, :], src[:, k, :], gain(k), rstd[:, g % 2, :],
                                                   ALU.mult, ALU.mult).then_inc(done, 1)
            dve.wait_ge(done, kt)


def attention(nc, tag, C, items, outs, wide, scale, parts=1, lam=None, score_ring=2, turn_ring=2,
              out_ring=2, bias_loads=(), bias_prepare=None):
    R = 2
    with ExitStack() as ctx:
        sb, ps, sem = phase_tools(nc, ctx, tag)
        biased = any(it["bias"] is not None for it in items)
        s_sb = sb("s", [P, R, wide]) if biased else None
        e = sb("e", [P, R, parts, wide])
        p = sb("p", [P, R, wide])
        first = sb("first", [P, R, wide]) if parts == 2 else None
        pT = sb("pT", [P, R, wide])
        mx = sb("mx", [P, R, parts])
        neg = sb("neg", [P, R, parts])
        total = sb("total", [P, R, parts])
        rtotal = sb("rtotal", [P, R, parts])
        factor = sb("factor", [P, R])
        sbanks = parts * -(-wide // BANK)
        score = ps("score", [P, score_ring, sbanks * BANK])
        tp = ps("tp", [P, turn_ring, BANK])
        out = ps("out", [P, out_ring, BANK])
        scored, biased_ready, max_ready, neg_ready, exp_ready = (
            sem("scored"), sem("biased_ready"), sem("max_ready"), sem("neg_ready"), sem("exp_ready"))
        recip_ready, step, p_ready, turned, moved, summed, out_copied = (
            sem("recip_ready"), sem("step"), sem("p_ready"), sem("turned"), sem("moved"), sem("summed"),
            sem("out_copied"))
        bias_in = sem("bias_in")
        bias_set = sem("bias_set")
        block = ctx.enter_context(nc.Block())
        N = len(items)
        turns = [(i, a, min(4, it["width"] // P - a)) for i, it in enumerate(items)
                 for a in range(0, it["width"] // P, 4)]
        turns_before = [sum(1 for x in turns if x[0] < i) for i in range(N + 1)]
        ends = {}
        for n, (_, _, i) in enumerate(outs):
            ends.setdefault(i, []).append(n)

        def part_of(tile, it, s):
            return tile[:, s * wide:s * wide + it["width"]] if parts == 2 else tile[:, 0:it["width"]]

        @block.sync
        def _(sp):
            for n, (dst, src, after) in enumerate(bias_loads):
                if after is not None:
                    sp.wait_ge(biased_ready, after + 1)
                sp.dma_start(dst, src).then_inc(bias_in, 16)
                sp.wait_ge(bias_in, 16 * (n + 1))

        @block.gpsimd
        def _(pool):
            for n in range(len(bias_loads)):
                pool.wait_ge(bias_in, 16 * (n + 1))
                if bias_prepare:
                    bias_prepare(n).then_inc(bias_set, 1)
                else:
                    pool.sem_inc(bias_set, 1)

        def scores(pe, i):
            it = items[i]
            if i >= score_ring:
                pe.wait_ge(biased_ready if biased else exp_ready, (i - score_ring + 1) * (1 if biased else parts))
            for c0, n, pairs in it["scores"]:
                for m, (lhsT, rhs) in enumerate(pairs):
                    last = nc.tensor.matmul(score[:, i % score_ring, c0:c0 + n], lhsT, rhs, start=(m == 0),
                                            stop=(m == len(pairs) - 1), skip_group_check=True)
            last.then_inc(scored, 1)

        def turn_and_sum(pe, i):
            it = items[i]
            pe.wait_ge(p_ready, i + 1)
            for n in range(turns_before[i], turns_before[i + 1]):
                _, a, tiles = turns[n]
                if n >= turn_ring:
                    pe.wait_ge(moved, n - turn_ring + 1)
                for m in range(tiles):
                    last = nc.tensor.transpose(tp[:, n % turn_ring, m * P:(m + 1) * P],
                                               p[:, i % R, (a + m) * P:(a + m + 1) * P], C["ident"][:])
                last.then_inc(turned, 1)
            pe.wait_ge(moved, turns_before[i + 1])
            for o, rows, cols, values in it["values"]:
                if o >= out_ring:
                    pe.wait_ge(out_copied, o - out_ring + 1)
                for m, (kt, v) in enumerate(values):
                    last = nc.tensor.matmul(out[rows, o % out_ring, cols], v,
                                            pT[:, i % R, kt * P:(kt + 1) * P], start=(m == 0),
                                            stop=(m == len(values) - 1), skip_group_check=True)
            last.then_inc(summed, 1)

        @block.tensor
        def _(pe):
            for i in range(min(score_ring, N)):
                scores(pe, i)
            for i in range(N):
                if score_ring == 1 and i + 1 < N:
                    scores(pe, i + 1)
                turn_and_sum(pe, i)
                if score_ring > 1 and i + score_ring < N:
                    scores(pe, i + score_ring)

        def exps(act, i):
            it = items[i]
            act.wait_ge(neg_ready, i + 1)
            if i >= R:
                act.wait_ge(p_ready, i - R + 1)
            for s in range(parts):
                src = s_sb[:, i % R, 0:it["width"]] if biased else part_of(score[:, i % score_ring], it, s)
                nc.scalar.activation(e[:, i % R, s, 0:it["width"]], src, ACT.Exp, bias=neg[:, i % R, s:s + 1],
                                     scale=1.0 if biased else scale,
                                     accum_out=total[:, i % R, s:s + 1]).then_inc(exp_ready, 1)

        def moves(act, i):
            if i >= R:
                act.wait_ge(summed, i - R + 1)
            for n in range(turns_before[i], turns_before[i + 1]):
                _, a, tiles = turns[n]
                act.wait_ge(turned, n + 1)
                nc.scalar.copy(pT[:, i % R, a * P:(a + tiles) * P],
                               tp[:, n % turn_ring, 0:tiles * P]).then_inc(moved, 1)

        @block.scalar
        def _(act):
            exps(act, 0)
            for i in range(N):
                if i + 1 < N:
                    exps(act, i + 1)
                moves(act, i)

        def maxima(dve, i):
            it = items[i]
            dve.wait_ge(scored, i + 1)
            if biased:
                if i >= R:
                    dve.wait_ge(exp_ready, i - R + 1)
                if bias_loads:
                    dve.wait_ge(bias_set, it["bias_load"] + 1)
                nc.vector.scalar_tensor_tensor(s_sb[:, i % R, 0:it["width"]], score[:, i % score_ring, 0:it["width"]],
                                               scale, it["bias"], ALU.mult, ALU.add).then_inc(biased_ready, 1)
                dve.wait_ge(biased_ready, i + 1)
            elif i >= R:
                dve.wait_ge(exp_ready, parts * (i - R + 1))
            for s in range(parts):
                src = s_sb[:, i % R, 0:it["width"]] if biased else part_of(score[:, i % score_ring], it, s)
                nc.vector.tensor_reduce(mx[:, i % R, s:s + 1], src, AX.X, ALU.max).then_inc(max_ready, 1)
            dve.wait_ge(max_ready, parts * (i + 1))
            nc.vector.tensor_scalar(neg[:, i % R, :], mx[:, i % R, :], -1.0 if biased else -scale, None,
                                    ALU.mult).then_inc(neg_ready, 1)

        outs_done = [0]

        def weights(dve, i, steps):
            it = items[i]
            w = it["width"]
            dve.wait_ge(exp_ready, parts * (i + 1))
            nc.vector.reciprocal(rtotal[:, i % R, :], total[:, i % R, :]).then_inc(recip_ready, 1)
            dve.wait_ge(recip_ready, i + 1)
            if i >= R:
                dve.wait_ge(turned, turns_before[i - R + 1])
            if parts == 1:
                nc.vector.tensor_scalar(p[:, i % R, 0:w], e[:, i % R, 0, 0:w], rtotal[:, i % R, 0:1], None,
                                        ALU.mult).then_inc(p_ready, 1)
                return
            nc.vector.tensor_scalar(first[:, i % R, 0:w], e[:, i % R, 0, 0:w], rtotal[:, i % R, 0:1], None,
                                    ALU.mult).then_inc(step, 1)
            nc.vector.tensor_tensor(factor[:, i % R:i % R + 1], rtotal[:, i % R, 1:2], lam, ALU.mult).then_inc(step, 1)
            dve.wait_ge(step, 2 * (i + 1))
            nc.vector.scalar_tensor_tensor(p[:, i % R, 0:w], e[:, i % R, 1, 0:w], factor[:, i % R:i % R + 1],
                                           first[:, i % R, 0:w], ALU.mult, ALU.add).then_inc(p_ready, 1)

        def finish(dve, i):
            for n in ends.get(i, []):
                rows, dst, _ = outs[n]
                dve.wait_ge(summed, i + 1)
                nc.vector.tensor_copy(dst, out[rows, n % out_ring, :]).then_inc(out_copied, 1)

        @block.vector
        def _(dve):
            maxima(dve, 0)
            for i in range(N):
                if i + 1 < N:
                    maxima(dve, i + 1)
                weights(dve, i, None)
                if i >= 1:
                    finish(dve, i - 1)
            finish(dve, N - 1)


def norm_transpose(nc, tag, C, src, tiles, width, dst, scale, bias=None):
    kt = width // P
    with ExitStack() as ctx:
        sb, ps, sem = phase_tools(nc, ctx, tag)
        xn = sb("xn", [P, tiles, width])
        junk = sb("junk", [P, width])
        sumsq = sb("sumsq", [P, tiles])
        meansq = sb("meansq", [P, tiles])
        rms = sb("rms", [P, tiles])
        guess, tmp, rstd = sb("guess", [P, tiles]), sb("tmp", [P, tiles]), sb("rstd", [P, tiles])
        tp = ps("tp", [P, 4, tiles * P if tiles * P == BANK else BANK])
        squares_done, mean_ready, rms_ready, rstd_ready = sem("sq"), sem("mean"), sem("rms"), sem("rstd")
        xn_ready, turned, copied = sem("xn_ready"), sem("turned"), [sem("copied_act"), sem("copied_dve")]
        block = ctx.enter_context(nc.Block())

        @block.scalar
        def _(act):
            for t in range(tiles):
                if t >= 1:
                    act.wait_ge(squares_done, t)
                nc.scalar.activation(junk[:], src[:, t, :], ACT.Square,
                                     accum_out=sumsq[:, t:t + 1]).then_inc(squares_done, 1)
            act.wait_ge(mean_ready, 1)
            nc.scalar.activation(rms[:], meansq[:], ACT.Sqrt).then_inc(rms_ready, 1)
            for k in range(0, kt, 2):
                act.wait_ge(turned, k + 1)
                b = bias(k) if bias else 0.0
                nc.scalar.activation(dst[:, k, :], tp[:, k % 4, 0:tiles * P], ACT.Identity, bias=b,
                                     scale=scale(k)).then_inc(copied[0], 1)

        @block.vector
        def _(dve):
            dve.wait_ge(squares_done, tiles)
            nc.vector.tensor_scalar(meansq[:], sumsq[:], 1.0 / width, EPS, ALU.mult, ALU.add).then_inc(mean_ready, 1)
            dve.wait_ge(rms_ready, 1)
            ch = Chain(dve, rstd_ready)
            ch.add(nc.vector.reciprocal(guess[:], rms[:]))
            ch.wait()
            refined_rsqrt(nc.vector, ch, meansq[:], guess[:], tmp[:], rstd[:])
            for t in range(tiles):
                nc.vector.tensor_scalar(xn[:, t, :], src[:, t, :], rstd[:, t:t + 1], None,
                                        ALU.mult).then_inc(xn_ready, 1)
            for k in range(1, kt, 2):
                dve.wait_ge(turned, k + 1)
                b = bias(k) if bias else 0.0
                nc.vector.tensor_scalar(dst[:, k, :], tp[:, k % 4, 0:tiles * P], scale(k), b, ALU.mult,
                                        ALU.add).then_inc(copied[1], 1)

        @block.tensor
        def _(pe):
            pe.wait_ge(xn_ready, tiles)
            for k in range(kt):
                if k >= 4:
                    pe.wait_ge(copied[k % 2], (k - 4) // 2 + 1)
                for t in range(tiles):
                    last = nc.tensor.transpose(tp[:, k % 4, t * P:(t + 1) * P], xn[:, t, k * P:(k + 1) * P],
                                               C["ident"][:])
                last.then_inc(turned, 1)


def peer(nc, tag, C, h, hT, wq, keysT, u_tab, v_tab, gates, acc):
    with ExitStack() as outer:
        sbo, _, _ = phase_tools(nc, outer, tag)
        rows = [sbo(f"{n}T", [P, SEQ]) for n in ("first", "second", "gate")]
        with ExitStack() as mid:
            sbm, _, _ = phase_tools(nc, mid, tag + "m")
            qT = sbm("qT", [P, HALVES, SEQ])
            peer_queries(nc, tag + "q", hT, wq, qT)
            peer_choose(nc, tag + "c", C, qT, keysT, rows)
        peer_gates(nc, tag + "g", C, rows, gates)
    peer_experts(nc, tag + "e", hT, u_tab, v_tab, gates, acc)


def peer_queries(nc, tag, hT, wq, qT):
    product(nc, tag, hT, DK, SEQ,
            [(wq[c], False, [copy_to(nc, u, qT[:, 4 * c + u, :]) for u in range(4)]) for c in range(HALVES // 4)])


def peer_choose(nc, tag, C, qT, keysT, rows):
    with ExitStack() as ctx:
        sb, ps, sem = phase_tools(nc, ctx, tag)
        keys = sb("keys", [P, HALVES, KEYS])
        rest = sb("rest", [P, HALVES, KEYS])
        val = sb("val", [P, PHEADS, 2, TOPK])
        idx = sb("idx", [P, PHEADS, 2, TOPK], U32)
        idxf = sb("idxf", [P, PHEADS, 2, TOPK])
        cand = sb("cand", [P, PHEADS, TOPK, TOPK])
        crest = sb("crest", [P, PHEADS, TOPK * TOPK])
        top = sb("top", [P, PHEADS, TOPK])
        pos = sb("pos", [P, PHEADS, TOPK], U32)
        part = sb("part", [P, 2, PAIRS], U32)
        partf = sb("partf", [P, 2, PAIRS])
        hit = sb("hit", [P, PHEADS, TOPK, TOPK])
        picked = sb("picked", [P, PHEADS, TOPK, TOPK])
        chosen = sb("chosen", [P, 2, PAIRS])
        shifted = sb("shifted", [P, PHEADS, TOPK])
        weight = sb("weight", [P, PHEADS, TOPK])
        total = sb("total", [P, PHEADS])
        rtotal = sb("rtotal", [P, PHEADS])
        gate = sb("gate", [P, PHEADS, TOPK])
        score = ps("score", [P, HALVES, KEYS])
        tp = ps("tp", [P, 4, BANK])
        keys_in, scored, step, exp_done, turned, moved = (
            sem("keys_in"), sem("scored"), sem("step"), sem("exp_done"), sem("turned"), sem("moved"))
        scores_free, chosen_ready = sem("scores_free"), sem("chosen_ready")
        shifted_ready = sem("shifted_ready")
        block = ctx.enter_context(nc.Block())
        V = nc.vector

        @block.sync
        def _(sp):
            sp.dma_start(keys[:], keysT).then_inc(keys_in, 16)

        def turn(pe, t):
            pe.wait_ge(chosen_ready, t + 1)
            if t >= 1:
                pe.wait_ge(moved, 3 * t)
            for n, src in enumerate((chosen[:, 0, :], chosen[:, 1, :], gate[:].rearrange("p h k -> p (h k)"))):
                last = nc.tensor.transpose(tp[:, n, 0:P], src, C["ident"][:])
            last.then_inc(turned, 1)

        @block.tensor
        def _(pe):
            pe.wait_ge(keys_in, 16)
            for t in range(TT):
                if t >= 1:
                    pe.wait_ge(scores_free, t)
                for j in range(HALVES):
                    last = nc.tensor.matmul(score[:, j, :], qT[:, j, t * P:(t + 1) * P], keys[:, j, :],
                                            start=True, stop=True, skip_group_check=True)
                last.then_inc(scored, 1)
                if t >= 1:
                    turn(pe, t - 1)
            turn(pe, TT - 1)

        @block.scalar
        def _(act):
            for t in range(TT):
                act.wait_ge(shifted_ready, t + 1)
                nc.scalar.activation(weight[:], shifted[:], ACT.Exp).then_inc(exp_done, 1)
                act.wait_ge(turned, t + 1)
                for n in range(3):
                    nc.scalar.copy(rows[n][:, t * P:(t + 1) * P], tp[:, n, 0:P]).then_inc(moved, 1)

        @block.vector
        def _(dve):
            n = 0
            for t in range(TT):
                dve.wait_ge(scored, t + 1)
                for j in range(HALVES):
                    V.max(val[:, j // 2, j % 2, 0:8], score[:, j, :]).then_inc(step, 1)
                n += HALVES
                dve.wait_ge(step, n)
                for j in range(HALVES):
                    V.max_index(idx[:, j // 2, j % 2, 0:8], val[:, j // 2, j % 2, 0:8], score[:, j, :])
                    V.match_replace(rest[:, j, :], val[:, j // 2, j % 2, 0:8], score[:, j, :],
                                    -3.0e38).then_inc(step, 1)
                n += HALVES
                dve.wait_ge(step, n)
                V.engine_nop().then_inc(scores_free, 1)
                for j in range(HALVES):
                    V.max(val[:, j // 2, j % 2, 8:16], rest[:, j, :]).then_inc(step, 1)
                n += HALVES
                dve.wait_ge(step, n)
                for j in range(HALVES):
                    last = V.max_index(idx[:, j // 2, j % 2, 8:16], val[:, j // 2, j % 2, 8:16], rest[:, j, :])
                last.then_inc(step, 1)
                V.tensor_tensor(cand[:], val[:, :, 0, :].unsqueeze(3).broadcast_to([P, PHEADS, TOPK, TOPK]),
                                val[:, :, 1, :].unsqueeze(2).broadcast_to([P, PHEADS, TOPK, TOPK]),
                                ALU.add).then_inc(step, 1)
                n += 2
                dve.wait_ge(step, n)
                V.tensor_copy(idxf[:], idx[:]).then_inc(step, 1)
                for h in range(PHEADS):
                    V.max(top[:, h, 0:8], cand[:, h].rearrange("p a b -> p (a b)")).then_inc(step, 1)
                n += PHEADS + 1
                dve.wait_ge(step, n)
                for h in range(PHEADS):
                    V.max_index(pos[:, h, 0:8], top[:, h, 0:8], cand[:, h].rearrange("p a b -> p (a b)"))
                    V.match_replace(crest[:, h], top[:, h, 0:8], cand[:, h].rearrange("p a b -> p (a b)"), -3.0e38).then_inc(step, 1)
                n += PHEADS
                dve.wait_ge(step, n)
                for h in range(PHEADS):
                    V.max(top[:, h, 8:16], crest[:, h]).then_inc(step, 1)
                n += PHEADS
                dve.wait_ge(step, n)
                for h in range(PHEADS):
                    V.max_index(pos[:, h, 8:16], top[:, h, 8:16], crest[:, h]).then_inc(step, 1)
                V.tensor_tensor(shifted[:], top[:], top[:, :, 0:1].broadcast_to([P, PHEADS, TOPK]),
                                ALU.subtract).then_inc(shifted_ready, 1)
                n += PHEADS
                dve.wait_ge(step, n)
                flat = pos[:].rearrange("p h k -> p (h k)")
                V.tensor_scalar(part[:, 0, :], flat, 4, None, ALU.logical_shift_right).then_inc(step, 1)
                V.tensor_scalar(part[:, 1, :], flat, TOPK - 1, None, ALU.bitwise_and).then_inc(step, 1)
                n += 2
                dve.wait_ge(step, n)
                V.tensor_copy(partf[:], part[:]).then_inc(step, 1)
                n += 1
                dve.wait_ge(step, n)
                if t >= 1:
                    dve.wait_ge(turned, t)
                for s in range(2):
                    V.tensor_tensor(hit[:].rearrange("p h k m -> p (h k) m"),
                                    C["iota"][:, 0:TOPK].unsqueeze(1).broadcast_to([P, PAIRS, TOPK]),
                                    partf[:, s, :].unsqueeze(2).broadcast_to([P, PAIRS, TOPK]),
                                    ALU.is_equal).then_inc(step, 1)
                    n += 1
                    dve.wait_ge(step, n)
                    V.tensor_tensor(picked[:], hit[:],
                                    idxf[:, :, s, :].unsqueeze(2).broadcast_to([P, PHEADS, TOPK, TOPK]),
                                    ALU.mult).then_inc(step, 1)
                    n += 1
                    dve.wait_ge(step, n)
                    V.tensor_reduce(chosen[:, s, :], picked[:].rearrange("p h k m -> p (h k) m"), AX.X,
                                    ALU.add).then_inc(step, 1)
                    n += 1
                    dve.wait_ge(step, n)
                dve.wait_ge(exp_done, t + 1)
                V.tensor_reduce(total[:], weight[:], AX.X, ALU.add).then_inc(step, 1)
                n += 1
                dve.wait_ge(step, n)
                V.reciprocal(rtotal[:], total[:]).then_inc(step, 1)
                n += 1
                dve.wait_ge(step, n)
                V.tensor_tensor(gate[:], weight[:], rtotal[:].unsqueeze(2).broadcast_to([P, PHEADS, TOPK]),
                                ALU.mult).then_inc(chosen_ready, 1)


def peer_gates(nc, tag, C, rows, gates):
    first, second, gate = rows
    TOK = 4
    RING = 4
    STEPS = P // (TOK * RING)
    with ExitStack() as ctx:
        sb, ps, sem = phase_tools(nc, ctx, tag)
        hot1 = sb("hot1", [P, RING, TOK, KEYS])
        hot2 = sb("hot2", [P, RING, TOK, KEYS])
        away = sb("away", [P, RING, TOK, KEYS])
        out = sb("out", [P, 2, KEYS, P])
        prod = ps("prod", [P, RING, TOK, KEYS])
        hot_ready, away_ready, hot_free, prod_free = (
            sem("hot_ready"), sem("away_ready"), sem("hot_free"), sem("prod_free"))
        stored = [sem("stored0"), sem("stored1")]
        block = ctx.enter_context(nc.Block())

        @block.vector
        def _(dve):
            for t in range(TT):
                with dve.Fori(0, STEPS) as i:
                    for r in range(RING):
                        token = t * P + i * (RING * TOK) + r * TOK
                        dve.wait_ge(hot_free, (t * STEPS + i) * RING + r + 1)
                        for q in range(TOK):
                            nc.vector.tensor_scalar(hot1[:, r, q, :], C["iota"][:, 0:KEYS],
                                                    first[:, bass.ds(token + q, 1)],
                                                    gate[:, bass.ds(token + q, 1)], ALU.is_equal, ALU.mult)
                        dve.wait_ge(away_ready, (t * STEPS + i) * RING + r + 1)
                        nc.vector.tensor_scalar(hot2[:, r], away[:, r], 0.0, None,
                                                ALU.is_equal).then_inc(hot_ready, 1)

        @block.gpsimd
        def _(pool):
            for t in range(TT):
                with pool.Fori(0, STEPS) as i:
                    for r in range(RING):
                        token = t * P + i * (RING * TOK) + r * TOK
                        pool.wait_ge(hot_free, (t * STEPS + i) * RING + r + 1)
                        nc.gpsimd.tensor_tensor(
                            away[:, r], C["iota"][:, 0:KEYS].unsqueeze(1).broadcast_to([P, TOK, KEYS]),
                            second[:, bass.ds(token, TOK)].unsqueeze(2).broadcast_to([P, TOK, KEYS]),
                            ALU.subtract).then_inc(away_ready, 1)

        @block.tensor
        def _(pe):
            pe.sem_inc(hot_free, RING)
            for t in range(TT):
                with pe.Fori(0, STEPS) as i:
                    for r in range(RING):
                        pe.wait_ge(hot_ready, (t * STEPS + i) * RING + r + 1)
                        pe.wait_ge(prod_free, (t * STEPS + i) * RING + r + 1)
                        for q in range(TOK):
                            last = nc.tensor.matmul(prod[:, r, q, :], hot2[:, r, q, :], hot1[:, r, q, :],
                                                    start=True, stop=True, skip_group_check=True)
                        last.then_inc(hot_free, 1)

        @block.scalar
        def _(act):
            act.sem_inc(prod_free, RING)
            for t in range(TT):
                if t >= 2:
                    act.wait_ge(stored[t % 2], 16)
                with act.Fori(0, STEPS) as i:
                    for r in range(RING):
                        act.wait_ge(hot_free, (t * STEPS + i) * RING + r + 1 + RING)
                        nc.scalar.copy(out[:, t % 2, :, bass.ds(i * (RING * TOK) + r * TOK, TOK)],
                                       prod[:, r].rearrange("p q k -> p k q")).then_inc(prod_free, 1)

        @block.sync
        def _(sp):
            for t in range(TT):
                sp.wait_ge(prod_free, RING + (t + 1) * STEPS * RING)
                sp.dma_start(gates[:, :, t * P:(t + 1) * P].rearrange("k p t -> p k t"),
                             out[:, t % 2]).then_inc(stored[t % 2], 16)
            sp.wait_ge(stored[0], 32)
            sp.wait_ge(stored[1], 32)


def after(eng, sem, value):
    if not isinstance(value, int) or value > 0:
        eng.wait_ge(sem, value)


def peer_experts(nc, tag, hT, u_tab, v_tab, gates, acc):
    G, OUTS = EGROUP, TT * 2
    NG = KEYS // G
    with ExitStack() as ctx:
        sb, ps, sem = phase_tools(nc, ctx, tag)
        x_hi, x_lo = sb("x_hi", [P, DK, SEQ], F32R), sb("x_lo", [P, DK, SEQ], F32R)
        u = sb("u", [P, G, DK * P])
        u_hi, u_lo = sb("u_hi", [P, 2, DK * P], F32R), sb("u_lo", [P, 2, DK * P], F32R)
        v = sb("v", [P, G, D])
        v_hi, v_lo = sb("v_hi", [P, G, D], F32R), sb("v_lo", [P, G, D], F32R)
        g = sb("g", [P, G, SEQ])
        a = sb("a", [P, 2, SEQ])
        w = sb("w", [P, 2, SEQ])
        w_hi, w_lo = sb("w_hi", [P, 2, G, SEQ], F32R), sb("w_lo", [P, 2, G, SEQ], F32R)
        pre = ps("pre", [P, 2, BANK])
        out = ps("out", [P, 4, BANK])
        u_in = [sem(f"u_in{j}") for j in range(G)]
        v_in = [sem(f"v_in{j}") for j in range(G)]
        g_in = [sem(f"g_in{j}") for j in range(G)]
        x_hi_ready, x_ready, u_hi_ready, u_ready, v_hi_ready, v_ready = (
            sem(n) for n in ("x_hi_ready", "x_ready", "u_hi_ready", "u_ready", "v_hi_ready", "v_ready"))
        pre_ready, gelu_done, w_made, w_hi_ready, w_ready, out_ready, summed = (
            sem(n) for n in ("pre_ready", "gelu_done", "w_made", "w_hi_ready", "w_ready", "out_ready", "summed"))
        block = ctx.enter_context(nc.Block())
        V = nc.vector

        def for_groups(eng, body):
            body(0, 0, first=True, last=False)
            with eng.Fori(0, (NG - 2) // 2) as i:
                body(2 * i + 1, 1, first=False, last=False)
                body(2 * i + 2, 0, first=False, last=False)
            body(NG - 1, 1, first=False, last=True)

        @block.sync
        def _(sp):
            def fixed(x):
                return x if isinstance(x, int) else sp.snap(x)

            def loads(gr, _, first, last):
                tiles = [fixed(gr * G + j) for j in range(G)]
                used = [fixed((gr - 1) * G + j + 1) for j in range(G)]
                for j in range(G):
                    after(sp, u_ready, used[j])
                    sp.dma_start(u[:, j], u_tab[bass.ds(tiles[j], 1)].rearrange("o p k e -> (o p) (k e)")
                                 ).then_inc(u_in[j], 16)
                for j in range(G):
                    after(sp, w_made, used[j])
                    sp.dma_start(g[:, j], gates[bass.ds(tiles[j], 1)].rearrange("o p t -> (o p) t")
                                 ).then_inc(g_in[j], 16)
                    after(sp, v_ready, used[j])
                    sp.dma_start(v[:, j], v_tab[bass.ds(tiles[j], 1)].rearrange("o p d -> (o p) d")
                                 ).then_inc(v_in[j], 16)
            for_groups(sp, loads)

        @block.tensor
        def _(pe):
            def activations(gr, j):
                n = gr * G + j
                pe.wait_ge(u_ready, n + 1)
                after(pe, gelu_done, n - 1)
                q, passes = j % 2, 3 * DK
                m = 0
                for k in range(DK):
                    for lhs, rhs in ((u_hi, x_hi), (u_hi, x_lo), (u_lo, x_hi)):
                        last = nc.tensor.matmul(pre[:, q, :], lhs[:, q, k * P:(k + 1) * P], rhs[:, k, :],
                                                start=(m == 0), stop=(m == passes - 1))
                        m += 1
                last.then_inc(pre_ready, 1)

            def values(gr, par):
                pe.wait_ge(w_ready, gr * G + G)
                pe.wait_ge(v_ready, gr * G + G)
                for o in range(OUTS):
                    t, cols = o // 2, slice(o % 2 * BANK, (o % 2 + 1) * BANK)
                    pe.wait_ge(summed, gr * OUTS + o + 1)
                    m = 0
                    for j in range(G):
                        for lhs, rhs in ((w_hi, v_hi), (w_hi, v_lo), (w_lo, v_hi)):
                            last = nc.tensor.matmul(out[:, o % 4, :], lhs[:, par, j, t * P:(t + 1) * P],
                                                    rhs[:, j, cols], start=(m == 0), stop=(m == 3 * G - 1))
                            m += 1
                    last.then_inc(out_ready, 1)

            def body(gr, par, first, last):
                activations(gr, 0)
                if not first:
                    values(gr - 1, 1 - par)
                for j in range(1, G):
                    activations(gr, j)
                if last:
                    values(gr, par)
            pe.wait_ge(x_ready, DK)
            for_groups(pe, body)

        @block.scalar
        def _(act):
            for k in range(DK):
                nc.scalar.copy(x_hi[:, k, :], hT[:, k, :]).then_inc(x_hi_ready, 1)

            def split_u(gr, j):
                act.wait_ge(u_in[j], gr * 16 + 16)
                after(act, pre_ready, gr * G + j - 1)
                nc.scalar.copy(u_hi[:, j % 2, :], u[:, j, :]).then_inc(u_hi_ready, 1)

            def split_v(gr, j):
                act.wait_ge(v_in[j], gr * 16 + 16)
                after(act, out_ready, gr * OUTS)
                nc.scalar.copy(v_hi[:, j, :], v[:, j, :]).then_inc(v_hi_ready, 1)

            def body(gr, par, first, last):
                for j in range(G):
                    n = gr * G + j
                    act.wait_ge(pre_ready, n + 1)
                    after(act, w_made, n - 1)
                    nc.scalar.activation(a[:, j % 2, :], pre[:, j % 2, :], ACT.Gelu).then_inc(gelu_done, 1)
                    if j + 2 < G:
                        split_u(gr, j + 2)
                    elif not last:
                        split_u(gr + 1, j + 2 - G)
                    if j == 1:
                        split_v(gr, 0)
                    if j >= 1:
                        split_v(gr, j)
            split_u(0, 0)
            split_u(0, 1)
            for_groups(act, body)

        @block.vector
        def _(dve):
            dve.sem_inc(summed, 4)
            for k in range(DK):
                dve.wait_ge(x_hi_ready, k + 1)
                V.tensor_tensor(x_lo[:, k, :], hT[:, k, :], x_hi[:, k, :], ALU.subtract).then_inc(x_ready, 1)

            def split_u(gr, j):
                dve.wait_ge(u_hi_ready, gr * G + j + 1)
                V.tensor_tensor(u_lo[:, j % 2, :], u[:, j, :], u_hi[:, j % 2, :], ALU.subtract).then_inc(u_ready, 1)

            def split_v(gr, j):
                dve.wait_ge(v_hi_ready, gr * G + j + 1)
                V.tensor_tensor(v_lo[:, j, :], v[:, j, :], v_hi[:, j, :], ALU.subtract).then_inc(v_ready, 1)

            def add_outputs(gr):
                for o in range(OUTS):
                    dve.wait_ge(out_ready, gr * OUTS + o + 1)
                    part = acc[:, o // 2, o % 2 * BANK:(o % 2 + 1) * BANK]
                    V.tensor_tensor(part, part, out[:, o % 4, :], ALU.add).then_inc(summed, 1)

            def body(gr, par, first, last):
                for j in range(G):
                    n, q = gr * G + j, j % 2
                    dve.wait_ge(gelu_done, n + 1)
                    dve.wait_ge(g_in[j], gr * 16 + 16)
                    after(dve, w_ready, n - 1)
                    V.tensor_tensor(w[:, q, :], a[:, q, :], g[:, j, :], ALU.mult).then_inc(w_made, 1)
                    dve.wait_ge(w_made, n + 1)
                    V.tensor_copy(w_hi[:, par, j, :], w[:, q, :]).then_inc(w_hi_ready, 1)
                    dve.wait_ge(w_hi_ready, n + 1)
                    V.tensor_tensor(w_lo[:, par, j, :], w[:, q, :], w_hi[:, par, j, :],
                                    ALU.subtract).then_inc(w_ready, 1)
                    if j + 2 < G:
                        split_u(gr, j + 2)
                    elif not last:
                        split_u(gr + 1, j + 2 - G)
                    if j == 0 and not first:
                        add_outputs(gr - 1)
                    if j == 1:
                        split_v(gr, 0)
                    if j >= 1:
                        split_v(gr, j)
                if last:
                    add_outputs(gr)
            split_u(0, 0)
            split_u(0, 1)
            for_groups(dve, body)


def sincos_reduced(V, chain, ang, turns, red):
    chain.add(V.tensor_scalar(turns, ang, 1.0 / TWO_PI, ROUND, ALU.mult, ALU.add))
    chain.wait()
    chain.add(V.tensor_scalar(turns, turns, -ROUND, None, ALU.add))
    chain.wait()
    chain.add(V.scalar_tensor_tensor(red, turns, -TWO_PI_A, ang, ALU.mult, ALU.add))
    chain.wait()
    chain.add(V.scalar_tensor_tensor(red, turns, -TWO_PI_B, red, ALU.mult, ALU.add))
    chain.wait()
    chain.add(V.scalar_tensor_tensor(red, turns, -TWO_PI_C, red, ALU.mult, ALU.add))
    chain.wait()
    chain.add(V.tensor_scalar(red, red, float(np.float32(3.1415925)), float(np.float32(-3.1415925)), ALU.min,
                              ALU.max))
    chain.wait()


def ssm(nc, tag, C, uT, bc, lam, dcol, wglu, bglu, ssm_out):
    with ExitStack() as outer:
        sbo, _, _ = phase_tools(nc, outer, tag)
        y = sbo("y", [P, 4, SEQ])
        with ExitStack() as ctx:
            sb, ps, sem = phase_tools(nc, ctx, tag)
            cosT = sb("cosT", [P, STILES, SEQ])
            sinT = sb("sinT", [P, STILES, SEQ])
            mag = sb("mag", [P, STILES])
            BT = sb("BT", [P, 4, 2, P])
            CB = sb("CB", [P, 2, STILES, 32])
            ssm_tables(nc, tag + "t", C, bc, lam, cosT, sinT, mag, BT, CB)
            ssm_scan(nc, tag + "s", uT, dcol, cosT, sinT, mag, BT, CB, y)
        ssm_glu(nc, tag + "g", y, wglu, bglu, ssm_out)


def ssm_tables(nc, tag, C, bc, lam, cosT, sinT, mag, BT, CB):
    with ExitStack() as ctx:
        sb, ps, sem = phase_tools(nc, ctx, tag)
        raw = sb("raw", [P, 4, STILES, GROUP])
        small = sb("small", [P, 24, STILES])
        bb = sb("bb", [P, 2, STILES, 32])
        prod = sb("prod", [P, 4, STILES, GROUP])
        tmp = sb("tmp", [P, 4, STILES, SEQ // 8])
        tp = ps("tp", [P, 2, BANK])
        bc_in, v, a, zeroed, turned, ready = sem("bc_in"), sem("v"), sem("a"), sem("zeroed"), sem("turned"), sem("ready")
        block = ctx.enter_context(nc.Block())
        (step, lrs, ang, turns, red, half, s_half, sn, cs, sq, ar, ai, zr, t1, t2, t3, t4, den, rden, fr, fi,
         pc, psn, t5) = [small[:, n, :] for n in range(24)]
        lr, li, logstep = (lam[:, n, :] for n in range(3))

        @block.sync
        def _(sp):
            sp.dma_start(raw[:], bc.rearrange("w p t c -> p w t c")).then_inc(bc_in, 16)

        @block.gpsimd
        def _(pool):
            pool.memset(bb[:], 0.0).then_inc(zeroed, 1)
            pool.memset(CB[:], 0.0).then_inc(zeroed, 1)

        @block.scalar
        def _(act):
            nc.scalar.activation(step, logstep, ACT.Exp).then_inc(a, 1)
            act.wait_ge(ready, 1)
            nc.scalar.activation(mag[:], lrs, ACT.Exp).then_inc(a, 1)
            nc.scalar.activation(sn, red, ACT.Sin).then_inc(a, 1)
            nc.scalar.activation(s_half, half, ACT.Sin).then_inc(a, 1)

        @block.tensor
        def _(pe):
            pe.wait_ge(ready, 2)
            for ri in range(2):
                for kk in range(4):
                    last = nc.tensor.transpose(tp[:, ri, kk * P:(kk + 1) * P],
                                               bb[:, ri, 4 * kk:4 * kk + 4, :].rearrange("p j c -> p (j c)"),
                                               C["ident"][:])
                last.then_inc(turned, 1)

        @block.vector
        def _(dve):
            V = nc.vector
            ch = Chain(dve, v)
            dve.wait_ge(a, 1)
            ch.add(V.tensor_tensor(lrs, lr, step, ALU.mult))
            ch.add(V.tensor_tensor(ang, li, step, ALU.mult))
            ch.wait()
            sincos_reduced(V, ch, ang, turns, red)
            ch.add(V.tensor_scalar(half, red, 0.5, None, ALU.mult))
            ch.wait()
            V.engine_nop().then_inc(ready, 1)
            dve.wait_ge(a, 4)
            ch.add(V.tensor_tensor(sq, s_half, s_half, ALU.mult))
            ch.wait()
            ch.add(V.tensor_scalar(cs, sq, -2.0, 1.0, ALU.mult, ALU.add))
            ch.wait()
            ch.add(V.tensor_tensor(ar, mag[:], cs, ALU.mult))
            ch.add(V.tensor_tensor(ai, mag[:], sn, ALU.mult))
            ch.add(V.tensor_tensor(t1, lr, lr, ALU.mult))
            ch.add(V.tensor_tensor(t2, li, li, ALU.mult))
            ch.wait()
            ch.add(V.tensor_scalar(zr, ar, -1.0, None, ALU.add))
            ch.add(V.tensor_tensor(den, t1, t2, ALU.add))
            ch.wait()
            ch.add(V.reciprocal(rden, den))
            ch.add(V.tensor_tensor(t1, zr, lr, ALU.mult))
            ch.add(V.tensor_tensor(t2, ai, li, ALU.mult))
            ch.add(V.tensor_tensor(t3, ai, lr, ALU.mult))
            ch.add(V.tensor_tensor(t4, zr, li, ALU.mult))
            ch.wait()
            ch.add(V.tensor_tensor(t1, t1, t2, ALU.add))
            ch.add(V.tensor_tensor(t3, t3, t4, ALU.subtract))
            ch.wait()
            ch.add(V.tensor_tensor(fr, t1, rden, ALU.mult))
            ch.add(V.tensor_tensor(fi, t3, rden, ALU.mult))
            ch.wait()
            dve.wait_ge(bc_in, 16)
            dve.wait_ge(zeroed, 2)
            wide = lambda x: x.unsqueeze(2).broadcast_to([P, STILES, GROUP])
            for n, (f, b) in enumerate(((fr, 0), (fi, 1), (fr, 1), (fi, 0))):
                ch.add(V.tensor_tensor(prod[:, n], wide(f), raw[:, b], ALU.mult))
            ch.wait()
            for half_ in range(2):
                rows, cols = slice(64 * half_, 64 * half_ + 64), slice(16 * half_, 16 * half_ + 16)
                ch.add(V.tensor_tensor(bb[rows, 0, :, cols], prod[rows, 0], prod[rows, 1], ALU.subtract))
                ch.add(V.tensor_tensor(bb[rows, 1, :, cols], prod[rows, 2], prod[rows, 3], ALU.add))
                ch.add(V.tensor_copy(CB[rows, 0, :, cols], raw[rows, 2]))
                ch.add(V.tensor_scalar(CB[rows, 1, :, cols], raw[rows, 3], -1.0, None, ALU.mult))
            ch.wait()
            V.engine_nop().then_inc(ready, 1)
            ch.add(V.memset(cosT[:, :, 0:1], 1.0))
            ch.add(V.memset(sinT[:, :, 0:1], 0.0))
            ch.add(V.tensor_copy(pc, cs))
            ch.add(V.tensor_copy(psn, sn))
            ch.wait()
            n = 1
            while n < SEQ:
                for c0 in range(0, n, SEQ // 8):
                    m = min(n, SEQ // 8)
                    a_c, a_s = cosT[:, :, c0:c0 + m], sinT[:, :, c0:c0 + m]
                    bcast = lambda x: x.unsqueeze(2).broadcast_to([P, STILES, m])
                    for q, (x, f) in enumerate(((a_c, pc), (a_s, psn), (a_c, psn), (a_s, pc))):
                        ch.add(V.tensor_tensor(tmp[:, q, :, 0:m], x, bcast(f), ALU.mult))
                    ch.wait()
                    ch.add(V.tensor_tensor(cosT[:, :, n + c0:n + c0 + m], tmp[:, 0, :, 0:m], tmp[:, 1, :, 0:m],
                                           ALU.subtract))
                    ch.add(V.tensor_tensor(sinT[:, :, n + c0:n + c0 + m], tmp[:, 2, :, 0:m], tmp[:, 3, :, 0:m],
                                           ALU.add))
                    ch.wait()
                ch.add(V.tensor_tensor(t1, pc, pc, ALU.mult))
                ch.add(V.tensor_tensor(t2, psn, psn, ALU.mult))
                ch.add(V.tensor_tensor(t3, pc, psn, ALU.mult))
                ch.wait()
                ch.add(V.tensor_tensor(pc, t1, t2, ALU.subtract))
                ch.add(V.tensor_scalar(psn, t3, 2.0, None, ALU.mult))
                ch.wait()
                n *= 2
            dve.wait_ge(turned, 2)
            for ri in range(2):
                ch.add(V.tensor_copy(BT[:, :, ri, :], tp[:, ri, :].rearrange("p (k s) -> p k s", k=4)))


def ssm_scan(nc, tag, uT, dcol, cosT, sinT, mag, BT, CB, y):
    with ExitStack() as ctx:
        sb, ps, sem = phase_tools(nc, ctx, tag)
        R = 2
        m = sb("m", [P, R, 4, SEQ])
        b = sb("b", [P, R, 2, SEQ])
        z = sb("z", [P, R, 2, SEQ])
        q = sb("q", [P, R, 4, SEQ])
        x = sb("x", [P, R, 2, SEQ])
        pre = sb("pre", [P, 4, SEQ])
        bu = ps("bu", [P, R, 2, BANK])
        yp = ps("yp", [P, 4, BANK])
        fed, turned_in, v, z_ready, back, x_ready, y_ready, pre_ready = (
            sem("fed"), sem("turned_in"), sem("v"), sem("z_ready"), sem("back"), sem("x_ready"), sem("y_ready"),
            sem("pre_ready"))
        block = ctx.enter_context(nc.Block())
        V, G = nc.vector, nc.gpsimd

        @block.tensor
        def _(pe):
            def feed(n):
                kk, j = n // 4, n % 4
                rows = slice(32 * j, 32 * j + 32)
                if n >= R:
                    pe.wait_ge(turned_in, n - R + 1)
                for ri in range(2):
                    last = nc.tensor.matmul(bu[:, n % R, ri, :], BT[rows, kk, ri, :], uT[rows, kk, :], start=True,
                                            stop=True, tile_position=(32 * j, 0))
                last.then_inc(fed, 1)

            feed(0)
            for n in range(STILES):
                if n + 1 < STILES:
                    feed(n + 1)
                kk, j = n // 4, n % 4
                rows = slice(32 * j, 32 * j + 32)
                pe.wait_ge(x_ready, n + 1)
                for ri in range(2):
                    last = nc.tensor.matmul(yp[rows, kk, :], CB[:, ri, n, :], x[:, n % R, ri, :], start=(ri == 0),
                                            stop=(ri == 1), skip_group_check=True)
                last.then_inc(y_ready, 1)

        def skip(dve, kk):
            dve.wait_ge(y_ready, 4 * (kk + 1))
            V.scalar_tensor_tensor(pre[:, kk, :], uT[:, kk, :], dcol(kk), yp[:, kk, :], ALU.mult,
                                   ALU.add).then_inc(pre_ready, 1)

        @block.vector
        def _(dve):
            ch = Chain(dve, v)
            for n in range(STILES):
                c, s = cosT[:, n, :], sinT[:, n, :]
                dve.wait_ge(fed, n + 1)
                for i, (part, f) in enumerate(((0, c), (1, s), (1, c), (0, s))):
                    ch.add(V.tensor_tensor(m[:, n % R, i, :], bu[:, n % R, part, :], f, ALU.mult))
                ch.wait()
                ch.add(V.tensor_tensor(b[:, n % R, 0, :], m[:, n % R, 0, :], m[:, n % R, 1, :], ALU.add))
                V.tensor_tensor(b[:, n % R, 1, :], m[:, n % R, 2, :], m[:, n % R, 3, :],
                                ALU.subtract).then_inc(turned_in, 1)
                ch.wait()
                dve.wait_ge(turned_in, n + 1)
                if n >= R:
                    dve.wait_ge(back, 4 * (n - R + 1))
                r = mag[:, n:n + 1].broadcast_to([P, SEQ])
                for ri in range(2):
                    V.tensor_tensor_scan(z[:, n % R, ri, :], r, b[:, n % R, ri, :], 0.0, ALU.mult,
                                         ALU.add).then_inc(z_ready, 1)
                if n % 4 == 3 and n >= 7:
                    skip(dve, n // 4 - 1)
            skip(dve, 3)

        @block.gpsimd
        def _(pool):
            for n in range(STILES):
                c, s = cosT[:, n, :], sinT[:, n, :]
                pool.wait_ge(z_ready, 2 * (n + 1))
                for i, (part, f) in enumerate(((0, c), (1, s), (1, c), (0, s))):
                    G.tensor_tensor(q[:, n % R, i, :], z[:, n % R, part, :], f, ALU.mult).then_inc(back, 1)
                pool.wait_ge(back, 4 * (n + 1))
                if n >= R:
                    pool.wait_ge(y_ready, n - R + 1)
                G.tensor_tensor(x[:, n % R, 0, :], q[:, n % R, 0, :], q[:, n % R, 1, :], ALU.subtract)
                G.tensor_tensor(x[:, n % R, 1, :], q[:, n % R, 2, :], q[:, n % R, 3, :],
                                ALU.add).then_inc(x_ready, 1)

        @block.scalar
        def _(act):
            for kk in range(4):
                act.wait_ge(pre_ready, kk + 1)
                nc.scalar.activation(y[:, kk, :], pre[:, kk, :], ACT.Gelu)


def ssm_glu(nc, tag, y, wglu, bglu, ssm_out):
    with ExitStack() as ctx:
        sb, ps, sem = phase_tools(nc, ctx, tag)
        w = sb("w", [P, 4, 4, P])
        sig = sb("sig", [P, 4, SEQ])
        z = ps("z", [P, 4, BANK])
        w_in, multiplied, sig_ready = sem("w_in"), sem("multiplied"), sem("sig_ready")
        block = ctx.enter_context(nc.Block())

        @block.sync
        def _(sp):
            sp.dma_start(w[:], wglu.rearrange("j p k n -> p j k n")).then_inc(w_in, 16)

        @block.tensor
        def _(pe):
            pe.wait_ge(w_in, 16)
            for j in range(4):
                for k in range(4):
                    last = nc.tensor.matmul(z[:, j, :], w[:, j, k, :], y[:, k, :], start=(k == 0), stop=(k == 3))
                last.then_inc(multiplied, 1)

        @block.scalar
        def _(act):
            for j in range(4):
                act.wait_ge(multiplied, j + 1)
                nc.scalar.activation(sig[:, j, :], z[:, j, :], ACT.Sigmoid, bias=bglu(j)).then_inc(sig_ready, 1)

        @block.vector
        def _(dve):
            for j in range(4):
                dve.wait_ge(sig_ready, j + 1)
                nc.vector.tensor_tensor(ssm_out[:, j, :], y[:, j, :], sig[:, j, :], ALU.mult)


COLS, ROWS = {}, {}
_n = 0
for _name, _width in (("norm_mix_g", 8), ("att_q_g", 1), ("att_k_g", 1), ("att_out_g", 4), ("ssm_out_g", 4),
                      ("norm_mem_g", 8), ("norm_memkv_g", 8), ("mem_q_g", 2), ("mem_k_g", 2),
                      ("norm_peer_g", 8), ("ssm_d", 4), ("ssm_b_glu", 4), ("lam", 48), ("norm1_g", 8),
                      ("norm2_g", 8), ("b_gate", 16), ("b_ada", 48), ("subln_g", 1), ("c", 8)):
    COLS[_name] = (_n, _width)
    _n += _width
NCOLS = _n
_n = 0
for _name, _width in (("gains", 2 * DIL_W + 2 * DIFF_W), ("inv_freq", HEAD // 2), ("lambdas", 4 * HEAD)):
    ROWS[_name] = (_n, _width)
    _n += _width
NROWS = _n
QK2 = 2 * DIL_W + 2 * DIFF_W
QK2_TILES = QK2 // P
MODS = 4


def constants(nc, ctx, cols_dram):
    ident = ctx.enter_context(nc.sbuf_tensor("ident", [P, P], F32))
    ones = ctx.enter_context(nc.sbuf_tensor("ones", [P, P], F32))
    iota = ctx.enter_context(nc.sbuf_tensor("iota", [P, P], F32))
    cols = ctx.enter_context(nc.sbuf_tensor("cols", [P, NCOLS], F32))
    with ExitStack() as c:
        _, _, sem = phase_tools(nc, c, "const")
        zeroed, cols_in = sem("zeroed"), sem("cols_in")
        block = c.enter_context(nc.Block())

        @block.gpsimd
        def _(pool):
            pool.memset(ident[:], 0.0).then_inc(zeroed, 1)
            pool.memset(ones[:], 1.0)
            pool.iota(iota[:], pattern=[[1, P]], base=0, channel_multiplier=0,
                      allow_small_or_imprecise_dtypes=True)
            pool.wait_ge(zeroed, 1)
            pool.affine_select(out=ident[:], in_=ident[:], compare_op=ALU.not_equal, fill=1.0, base=0,
                               pattern=[[-1, P]], channel_multiplier=1)

        @block.sync
        def _(sp):
            sp.dma_start(cols[:], cols_dram).then_inc(cols_in, 16)
            sp.wait_ge(cols_in, 16)
    return {"ident": ident, "ones": ones, "iota": iota, "cols": cols}


def column(C, name, n=None):
    a, width = COLS[name]
    return lambda k: C["cols"][:, a + k % width:a + k % width + 1]


def load(nc, tag, pairs):
    with ExitStack() as c:
        _, _, sem = phase_tools(nc, c, tag)
        arrived = [sem(f"in{n}") for n in range(len(pairs))]
        block = c.enter_context(nc.Block())

        @block.sync
        def _(sp):
            for n, (dst, src) in enumerate(pairs):
                sp.dma_start(dst, src).then_inc(arrived[n], 16)
            for n in range(len(pairs)):
                sp.wait_ge(arrived[n], 16)


def block1(nc, C, h, hT, A):
    with ExitStack() as mid:
        sb, _, _ = phase_tools(nc, mid, "b1")
        mixT = sb("mixT", [P, 8, SEQ])
        uT = sb("uT", [P, 4, SEQ])
        with ExitStack() as att:
            sba, _, _ = phase_tools(nc, att, "b1a")
            qk = sba("qk", [P, TT, 2 * ATT_W])
            v = sba("v", [P, TT, ATT_W])
            norm_transpose(nc, "n0", C, h, TT, D, hT, column(C, "norm_mix_g"))
            chunks = [(A["w_in"][c], True, columns_to(nc, qk, c * BANK, BANK, TT)) for c in range(2)]
            chunks.append((A["w_in"][2], True, columns_to(nc, v, 0, BANK, TT)))
            chunks.append((A["w_in"][3], False, [copy_to(nc, j, uT[:, j, :]) for j in range(4)]))
            product(nc, "w1", hT, DK, SEQ, chunks)
            qkT = sba("qkT", [P, 8, SEQ])
            heads_norm_transpose(nc, "hn1", C, qk, TT, 2 * HEADS, HEAD, qkT,
                                 lambda k: column(C, "att_q_g" if k < 4 else "att_k_g")(0))
            chunk_attention(nc, C, qkT, v, A["bias"], mixT)
        feature_norm(nc, "fn1", C, mixT, 4, mixT, column(C, "att_out_g"), False)
        a = COLS["lam"][0]
        lam = C["cols"][:, a:a + 48].rearrange("p (w t) -> p w t", w=3)
        ssm(nc, "ssm", C, uT, A["ssm_bc"], lam, column(C, "ssm_d"), A["w_glu"], column(C, "ssm_b_glu"),
            mixT[:, 4:8])
        feature_norm(nc, "fn2", C, mixT[:, 4:8], 4, mixT[:, 4:8], column(C, "ssm_out_g"), False)
        add_product(nc, "wo1", mixT, A["w_out"], h)
    norm_transpose(nc, "n1", C, h, TT, D, hT, column(C, "norm_mem_g"))
    memory_attention(nc, C, h, hT, A)
    norm_transpose(nc, "n2", C, h, TT, D, hT, column(C, "norm_peer_g"))
    peer(nc, "p1", C, h, hT, A["w_peer_q"], A["peer_keys"], A["peer_u"], A["peer_v"], A["gates"], h)


def add_product(nc, tag, srcT, w, h):
    def add(dst):
        return ON_DVE, lambda psum: [lambda: nc.vector.tensor_tensor(dst, dst, psum, ALU.add)]
    product(nc, tag, srcT, DK, SEQ,
            [(w[half], True, [add(h[:, t, half * BANK:(half + 1) * BANK]) for t in range(TT)]) for half in range(2)])


def chunk_attention(nc, C, qkT, v, bias_dram, outT):
    with ExitStack() as ctx:
        sb, _, _ = phase_tools(nc, ctx, "ca")
        bias = sb("bias", [P, 2, SEQ])
        items, outs = [], []
        for hd in range(HEADS):
            rows = slice(64 * (hd % 2), 64 * (hd % 2) + 64)
            for qt in range(TT):
                n = (qt + 1) * P
                q = qkT[rows, hd // 2, qt * P:(qt + 1) * P]
                items.append(dict(
                    scores=[(0, n, [(q, qkT[rows, 4 + hd // 2, 0:n])])], width=n,
                    bias=bias[:, hd % 2, SEQ - n:SEQ], bias_load=hd,
                    values=[(hd, rows, slice(qt * P, (qt + 1) * P),
                             [(kt, v[:, kt, hd * HEAD:(hd + 1) * HEAD]) for kt in range(qt + 1)])]))
            outs.append((rows, outT[rows, hd // 2, :], TT * hd + TT - 1))
        loads = [(bias[:, hd % 2, :], bias_dram[hd], None if hd < 2 else TT * (hd - 2) + TT - 1)
                 for hd in range(HEADS)]

        def mask(hd):
            return nc.gpsimd.memset(bias[0:CHUNK, hd % 2, SEQ - CHUNK:SEQ], MASKED)
        attention(nc, "ca", C, items, outs, SEQ, HEAD ** -0.5, bias_loads=loads, bias_prepare=mask)


def memory_attention(nc, C, h, hT, A):
    MT = MEM_LEN // P
    with ExitStack() as ctx:
        sb, _, _ = phase_tools(nc, ctx, "ma")
        oT = sb("oT", [P, DK, SEQ])
        qT = sb("qT", [P, DK, SEQ])
        kT = sb("kT", [P, DK, MEM_LEN])
        v = sb("v", [P, MT, D])
        with ExitStack() as ctx2:
            sb2, _, _ = phase_tools(nc, ctx2, "mb")
            q = sb2("q", [P, TT, D])
            k = sb2("k", [P, MT, D])
            mem = sb2("mem", [P, MT, D])
            memT = sb2("memT", [P, DK, MEM_LEN])
            load(nc, "mem", [(mem[:], A["mem"].rearrange("(t p) d -> p t d", p=P))])
            norm_transpose(nc, "nm", C, mem, MT, D, memT, column(C, "norm_memkv_g"))
            product(nc, "wmq", hT, DK, SEQ,
                    [(A["w_mem_q"][n], True, columns_to(nc, q, n * BANK, BANK, TT)) for n in range(2)])
            product(nc, "wmkv", memT, DK, MEM_LEN,
                    [(A[name][n], True, columns_to(nc, dst, n * BANK, BANK, MT))
                     for name, dst in (("w_mem_k", k), ("w_mem_v", v)) for n in range(2)])
            heads_norm_transpose(nc, "hnq", C, q, TT, MEM_HEADS, MEM_HEAD, qT, column(C, "mem_q_g"))
            heads_norm_transpose(nc, "hnk", C, k, MT, MEM_HEADS, MEM_HEAD, kT, column(C, "mem_k_g"))
        items, outs = [], []
        for hd in range(MEM_HEADS):
            for qt in range(TT):
                cols = slice(qt * P, (qt + 1) * P)
                items.append(dict(
                    scores=[(0, MEM_LEN, [(qT[:, 2 * hd + f, cols], kT[:, 2 * hd + f, :]) for f in range(2)])],
                    width=MEM_LEN, bias=None,
                    values=[(2 * hd + f, slice(0, P), cols,
                             [(kt, v[:, kt, (2 * hd + f) * P:(2 * hd + f + 1) * P]) for kt in range(MT)])
                            for f in range(2)]))
            for f in range(2):
                outs.append((slice(0, P), oT[:, 2 * hd + f, :], TT * hd + TT - 1))
        attention(nc, "mat", C, items, outs, MEM_LEN, MEM_HEAD ** -0.5, out_ring=4)
        add_product(nc, "wmo", oT, A["w_mem_o"], h)


def modulation(nc, C, A, mods, g1, g2):
    with ExitStack() as ctx:
        sb, ps, sem = phase_tools(nc, ctx, "ad")
        SL = 3
        cs = sb("cs", [P, DK])
        csb = sb("csb", [P, DK, P])
        w = sb("w", [P, SL, DK, BANK])
        brow = sb("brow", [P, 2, D])
        colp = ps("colp", [P, BANK])
        rowp = ps("rowp", [P, 4, BANK])
        loaded = [sem(f"loaded{s}") for s in range(SL)]
        silu_done, spread, multiplied, rows_in = sem("silu"), sem("spread"), sem("multiplied"), sem("rows_in")
        a = COLS["c"][0]
        ab = COLS["b_ada"][0]
        per_feature = {0: 0, 1: 1, 3: 2, 4: 3}
        block = ctx.enter_context(nc.Block())

        @block.sync
        def _(sp):
            sp.dma_start(brow[:], A["ada_rows"].partition_broadcast(P)).then_inc(rows_in, 16)
            for c in range(12):
                if c >= SL:
                    sp.wait_ge(multiplied, c - SL + 1)
                sp.dma_start(w[:, c % SL], A["w_ada"][c]).then_inc(loaded[c % SL], 16)

        @block.scalar
        def _(act):
            nc.scalar.activation(cs[:], C["cols"][:, a:a + DK], ACT.Silu).then_inc(silu_done, 1)

        @block.vector
        def _(dve):
            dve.wait_ge(silu_done, 1)
            nc.vector.tensor_copy(csb[:], cs[:].unsqueeze(2).broadcast_to([P, DK, P])).then_inc(spread, 1)
            dve.wait_ge(rows_in, 16)
            for n, (c, g) in enumerate(((4, g1), (5, g1), (10, g2), (11, g2))):
                dve.wait_ge(multiplied, c + 1)
                half = c % 2
                nc.vector.tensor_tensor(g[:, half * BANK:(half + 1) * BANK], rowp[:, n, :],
                                        brow[:, n // 2, half * BANK:(half + 1) * BANK], ALU.add)
            dve.wait_ge(multiplied, 12)
            for m in range(4):
                src = (0, 1, 3, 4)[m]
                nc.vector.tensor_tensor(mods[:, m, :], colp[:, m * 8:(m + 1) * 8],
                                        C["cols"][:, ab + 8 * src:ab + 8 * src + 8], ALU.add)

        @block.tensor
        def _(pe):
            pe.wait_ge(spread, 1)
            rows = 0
            for c in range(12):
                pe.wait_ge(loaded[c % SL], 16 * (c // SL + 1))
                if c // 2 in per_feature:
                    for f in range(4):
                        col = per_feature[c // 2] * 8 + (c % 2) * 4 + f
                        for k in range(DK):
                            last = nc.tensor.matmul(colp[:, col:col + 1], w[:, c % SL, k, f * P:(f + 1) * P],
                                                    cs[:, k:k + 1], start=(k == 0), stop=(k == DK - 1),
                                                    skip_group_check=True)
                else:
                    for k in range(DK):
                        last = nc.tensor.matmul(rowp[:, rows, :], csb[:, k, :], w[:, c % SL, k, :],
                                                start=(k == 0), stop=(k == DK - 1))
                    rows += 1
                last.then_inc(multiplied, 1)


def rope_tables(nc, C, A, cosb, sinb, rows, lam_neg):
    with ExitStack() as ctx:
        sb, ps, sem = phase_tools(nc, ctx, "rt")
        posi = sb("posi", [P, TT], I32)
        posf = sb("posf", [P, TT])
        F = HEAD // 2
        ang, turns, red, half, s_half, sq = (sb(n, [P, TT, F]) for n in ("ang", "turns", "red", "half", "s_half", "sq"))
        prod = sb("prod", [P, 2, HEAD])
        dots = sb("dots", [P, 2])
        edots = sb("edots", [P, 2])
        diff = sb("diff", [P, 1])
        v, loaded, ready, sined, exped = sem("v"), sem("loaded"), sem("ready"), sem("sined"), sem("exped")
        block = ctx.enter_context(nc.Block())
        f0 = ROWS["inv_freq"][0]
        l0 = ROWS["lambdas"][0]

        @block.sync
        def _(sp):
            with nc.allow_non_contiguous_dma("512 positions, once"):
                sp.dma_start(posi[:], A["positions"].rearrange("(t p) -> p t", p=P)).then_inc(loaded, 16)

        @block.scalar
        def _(act):
            act.wait_ge(ready, 1)
            nc.scalar.activation(sinb[:], red[:], ACT.Sin).then_inc(sined, 1)
            nc.scalar.activation(s_half[:], half[:], ACT.Sin).then_inc(sined, 1)
            nc.scalar.activation(edots[:], dots[:], ACT.Exp).then_inc(exped, 1)

        @block.vector
        def _(dve):
            V = nc.vector
            ch = Chain(dve, v)
            dve.wait_ge(loaded, 16)
            ch.add(V.tensor_copy(posf[:], posi[:]))
            lams = rows[:, l0:l0 + 4 * HEAD].rearrange("p (a b d) -> p a b d", a=2, b=2)
            ch.add(V.tensor_tensor(prod[:], lams[:, :, 0, :], lams[:, :, 1, :], ALU.mult))
            ch.wait()
            ch.add(V.tensor_reduce(dots[:], prod[:], AX.X, ALU.add))
            ch.add(V.tensor_tensor(ang[:], posf[:].unsqueeze(2).broadcast_to([P, TT, F]),
                                   rows[:, f0:f0 + F].unsqueeze(1).broadcast_to([P, TT, F]), ALU.mult))
            ch.wait()
            sincos_reduced(V, ch, ang[:], turns[:], red[:])
            ch.add(V.tensor_scalar(half[:], red[:], 0.5, None, ALU.mult))
            ch.wait()
            V.engine_nop().then_inc(ready, 1)
            dve.wait_ge(sined, 2)
            ch.add(V.tensor_tensor(sq[:], s_half[:], s_half[:], ALU.mult))
            ch.wait()
            V.tensor_scalar(cosb[:], sq[:], -2.0, 1.0, ALU.mult, ALU.add)
            dve.wait_ge(exped, 1)
            ch.add(V.tensor_tensor(diff[:], edots[:, 1:2], edots[:, 0:1], ALU.subtract))
            ch.wait()
            V.tensor_scalar(lam_neg[:], diff[:], -LAM_INIT, None, ALU.add)


def queries_keys(nc, C, hT, w_qk, rows, cosb, sinb, qkT):
    NC_ = QK2 // BANK
    HC = BANK // HEAD
    F = HEAD // 2
    with ExitStack() as ctx:
        sb, ps, sem = phase_tools(nc, ctx, "qk")
        w = sb("w", [P, 2, DK, BANK])
        raw = sb("raw", [P, 2, TT, BANK])
        sq = sb("sq", [P, 2, BANK])
        sumsq = sb("sumsq", [P, TT, HC])
        meansq = sb("meansq", [P, TT, HC])
        rms = sb("rms", [P, TT, HC])
        guess, tmp, rstd = (sb(n, [P, TT, HC]) for n in ("guess", "tmp", "rstd"))
        normed = sb("normed", [P, 2, BANK])
        gained = sb("gained", [P, 2, BANK])
        prod = sb("prod", [P, 2, 4, HC, F])
        rot = sb("rot", [P, TT, BANK])
        out = ps("out", [P, 4, BANK])
        tp = ps("tp", [P, 4, BANK])
        loaded = [sem("loaded0"), sem("loaded1")]
        (multiplied, raw_ready, squared, summed, mean_ready, rms_ready, v, rotated, turned, moved) = (
            sem(n) for n in ("multiplied", "raw_ready", "squared", "summed", "mean_ready", "rms_ready", "v",
                             "rotated", "turned", "moved"))
        block = ctx.enter_context(nc.Block())
        V = nc.vector

        @block.sync
        def _(sp):
            for c in range(NC_):
                if c >= 2:
                    sp.wait_ge(multiplied, TT * (c - 1))
                sp.dma_start(w[:, c % 2], w_qk[c]).then_inc(loaded[c % 2], 16)

        def turn(pe, c):
            pe.wait_ge(rotated, TT * (c + 1))
            for f in range(4):
                if c >= 1:
                    pe.wait_ge(moved, 4 * (c - 1) + f + 1)
                for t in range(TT):
                    last = nc.tensor.transpose(tp[:, f, t * P:(t + 1) * P], rot[:, t, f * P:(f + 1) * P],
                                               C["ident"][:])
                last.then_inc(turned, 1)

        def move(act, c):
            for f in range(4):
                act.wait_ge(turned, 4 * c + f + 1)
                nc.scalar.copy(qkT[:, 4 * c + f, :], tp[:, f, :]).then_inc(moved, 1)

        @block.tensor
        def _(pe):
            for c in range(NC_):
                pe.wait_ge(loaded[c % 2], 16 * (c // 2 + 1))
                for t in range(TT):
                    if c >= 1:
                        pe.wait_ge(raw_ready, TT * (c - 1) + t + 1)
                    for k in range(DK):
                        last = nc.tensor.matmul(out[:, t, :], hT[:, k, t * P:(t + 1) * P], w[:, c % 2, k, :],
                                                start=(k == 0), stop=(k == DK - 1))
                    last.then_inc(multiplied, 1)
                if c >= 1:
                    turn(pe, c - 1)
            turn(pe, NC_ - 1)

        @block.scalar
        def _(act):
            for c in range(NC_):
                for t in range(TT):
                    act.wait_ge(multiplied, TT * c + t + 1)
                    if c >= 2:
                        act.wait_ge(rotated, TT * (c - 2) + t + 1)
                    nc.scalar.copy(raw[:, c % 2, t, :], out[:, t, :]).then_inc(raw_ready, 1)
                    act.wait_ge(raw_ready, TT * c + t + 1)
                    if TT * c + t >= 2:
                        act.wait_ge(summed, TT * c + t - 1)
                    nc.scalar.activation(sq[:, t % 2, :], raw[:, c % 2, t, :], ACT.Square).then_inc(squared, 1)
                act.wait_ge(mean_ready, c + 1)
                nc.scalar.activation(rms[:], meansq[:], ACT.Sqrt).then_inc(rms_ready, 1)
                if c >= 1:
                    move(act, c - 1)
            move(act, NC_ - 1)

        @block.vector
        def _(dve):
            ch = Chain(dve, v)
            for c in range(NC_):
                for t in range(TT):
                    dve.wait_ge(squared, TT * c + t + 1)
                    V.tensor_reduce(sumsq[:, t, :], sq[:, t % 2, :].rearrange("p (h d) -> p h d", h=HC), AX.X,
                                    ALU.add).then_inc(summed, 1)
                dve.wait_ge(summed, TT * (c + 1))
                V.tensor_scalar(meansq[:], sumsq[:], 1.0 / HEAD, EPS, ALU.mult, ALU.add).then_inc(mean_ready, 1)
                dve.wait_ge(rms_ready, c + 1)
                ch.add(V.reciprocal(guess[:], rms[:]))
                ch.wait()
                refined_rsqrt(V, ch, meansq[:], guess[:], tmp[:], rstd[:])
                if c >= 1:
                    dve.wait_ge(turned, 4 * c)
                g = rows[:, c * BANK:(c + 1) * BANK]
                for t in range(TT):
                    i = t % 2
                    heads = lambda x: x.rearrange("p (h d) -> p h d", h=HC)
                    ch.add(V.tensor_tensor(heads(normed[:, i, :]), heads(raw[:, c % 2, t, :]),
                                           rstd[:, t, :].unsqueeze(2).broadcast_to([P, HC, HEAD]), ALU.mult))
                    ch.wait()
                    ch.add(V.tensor_tensor(gained[:, i, :], normed[:, i, :], g, ALU.mult))
                    ch.wait()
                    x1, x2 = heads(gained[:, i, :])[:, :, 0:F], heads(gained[:, i, :])[:, :, F:HEAD]
                    cb = cosb[:, t, :].unsqueeze(1).broadcast_to([P, HC, F])
                    sn = sinb[:, t, :].unsqueeze(1).broadcast_to([P, HC, F])
                    for n, (x, f) in enumerate(((x1, cb), (x2, sn), (x2, cb), (x1, sn))):
                        ch.add(V.tensor_tensor(prod[:, i, n], x, f, ALU.mult))
                    ch.wait()
                    o = heads(rot[:, t, :])
                    V.tensor_tensor(o[:, :, 0:F], prod[:, i, 0], prod[:, i, 1], ALU.subtract)
                    V.tensor_tensor(o[:, :, F:HEAD], prod[:, i, 2], prod[:, i, 3], ALU.add).then_inc(rotated, 1)


def block2(nc, C, h, hT, mods, g1, g2, A):
    scale1, scale2 = (C["scales"][:, i, :] for i in range(2))
    norm_transpose(nc, "n3", C, h, TT, D, hT, lambda k: scale1[:, k:k + 1], lambda k: mods[:, 0, k:k + 1])
    with ExitStack() as mid:
        sb, _, _ = phase_tools(nc, mid, "b2")
        qkT = sb("qkT", [P, QK2_TILES, SEQ])
        cosb = sb("cosb", [P, TT, HEAD // 2])
        sinb = sb("sinb", [P, TT, HEAD // 2])
        lam_neg = sb("lam_neg", [P, 1])
        with ExitStack() as ctx:
            sbr, _, _ = phase_tools(nc, ctx, "b2r")
            rows = sbr("rows", [P, NROWS])
            load(nc, "rows", [(rows[:], A["rows"].partition_broadcast(P))])
            rope_tables(nc, C, A, cosb, sinb, rows, lam_neg)
            queries_keys(nc, C, hT, A["w_qk_2"], rows, cosb, sinb, qkT)
        oaT = sb("oaT", [P, 2, SEQ])
        obT = sb("obT", [P, DIFF_HEADS, SEQ])
        with ExitStack() as ctx:
            sbv, _, _ = phase_tools(nc, ctx, "b2v")
            va = sbv("va", [P, TT, DIL_W])
            value_product(nc, "va", hT, A["w_va_2"], DIL_W // 2, va)
            dilated_attention(nc, C, qkT, va, A["masks"], oaT)
        with ExitStack() as ctx:
            sbv, _, _ = phase_tools(nc, ctx, "b2w")
            vb = sbv("vb", [P, TT, DIFF_W])
            value_product(nc, "vb", hT, A["w_vb_2"], BANK, vb)
            differential_attention(nc, C, qkT, vb, lam_neg, obT)
        feature_norm(nc, "fn3", C, obT, DIFF_HEADS, obT, lambda k: C["subln"][:, 0:1], True)
        mixT = sb("mixT", [P, DK, SEQ])
        gated_branches(nc, C, hT, oaT, obT, A, mixT, qkT[:, 0:DK])
        gated_add(nc, mixT, A["w_out_2"], g1, h)
    norm_transpose(nc, "n4", C, h, TT, D, hT, lambda k: scale2[:, k:k + 1], lambda k: mods[:, 2, k:k + 1])
    with ExitStack() as ctx:
        _, _, sem = phase_tools(nc, ctx, "hs")
        hs = sem("h_saved")
        block = ctx.enter_context(nc.Block())

        @block.sync
        def _(sp):
            sp.dma_start(A["h_scratch"].rearrange("(t p) d -> p t d", p=P), h[:]).then_inc(hs, 16)
            sp.wait_ge(hs, 16)

        @block.vector
        def _(dve):
            dve.wait_ge(hs, 16)
            nc.vector.memset(h[:], 0.0)
    peer(nc, "p2", C, h, hT, A["w_query_2"], A["sub_keys_2"], A["expert_u_2"], A["expert_v_2"], A["gates"], h)
    finish(nc, h, g2, A)


def value_product(nc, tag, hT, w, width, dst):
    product(nc, tag, hT, DK, SEQ, [(w[n], True, columns_to(nc, dst, n * width, width, TT)) for n in range(2)], SLABS=2)


def dilated_attention(nc, C, qkT, va, masks_dram, oaT):
    with ExitStack() as ctx:
        sb, _, _ = phase_tools(nc, ctx, "da")
        wide = 2 * SEQ + 3 * P
        masks = sb("masks", [P, TT, wide])
        load(nc, "masks", [(masks[:], masks_dram)])
        items, outs = [], []
        for hd in range(DIL_HEADS):
            rows = slice(64 * (hd % 2), 64 * (hd % 2) + 64)

            def at(first, g):
                return (first + (g * DIL_HEADS + hd) * HEAD) // P
            for qt in range(TT):
                near = range(max(0, qt - 1), min(TT, qt + 2))
                scores, values = [], []
                for n, (g, tiles) in enumerate(((1, range(TT)), (2, range(TT)), (0, near))):
                    q = qkT[rows, at(0, g), qt * P:(qt + 1) * P]
                    k = qkT[rows, at(DIL_W, g), tiles[0] * P:(tiles[-1] + 1) * P]
                    scores.append((n * SEQ, len(tiles) * P, [(q, k)]))
                    f = (g * DIL_HEADS + hd) * HEAD
                    values += [(n * TT + m, va[:, kt, f:f + HEAD]) for m, kt in enumerate(tiles)]
                width = 2 * SEQ + len(near) * P
                items.append(dict(scores=scores, width=width, bias=masks[:, qt, 0:width],
                                  values=[(hd, rows, slice(qt * P, (qt + 1) * P), values)]))
            outs.append((rows, oaT[rows, hd // 2, :], TT * hd + TT - 1))
        attention(nc, "dat", C, items, outs, wide, HEAD ** -0.5, score_ring=1, turn_ring=3)


def differential_attention(nc, C, qkT, vb, lam_neg, obT):
    first_q, first_k = 2 * DIL_W // P, (2 * DIL_W + DIFF_W) // P
    items, outs = [], []
    for hd in range(DIFF_HEADS):
        for qt in range(TT):
            cols = slice(qt * P, (qt + 1) * P)
            scores = []
            for s in range(2):
                rows = slice(64 * s, 64 * s + 64)
                scores.append((s * SEQ, SEQ, [(qkT[rows, first_q + hd, cols], qkT[rows, first_k + hd, :])]))
            items.append(dict(scores=scores, width=SEQ, bias=None,
                              values=[(hd, slice(0, P), cols,
                                       [(kt, vb[:, kt, hd * P:(hd + 1) * P]) for kt in range(TT)])]))
        outs.append((slice(0, P), obT[:, hd, :], TT * hd + TT - 1))
    attention(nc, "dif", C, items, outs, SEQ, HEAD ** -0.5, parts=2, lam=lam_neg[:, 0:1])


def gated_branches(nc, C, hT, oaT, obT, A, mixT, sig):
    def gate(dst, n):
        return ON_ACT, lambda psum: [
            lambda: nc.scalar.activation(dst, psum, ACT.Sigmoid, bias=column(C, "b_gate")(n))]

    def weigh(dst):
        return ON_DVE, lambda psum: [lambda: nc.vector.tensor_tensor(dst, dst, psum, ALU.mult)]

    def weigh_and_add(f):
        return ON_DVE, lambda psum: [
            lambda: nc.vector.tensor_tensor(sig[:, f, :], sig[:, f, :], psum, ALU.mult),
            lambda: nc.vector.tensor_tensor(mixT[:, f, :], mixT[:, f, :], sig[:, f, :], ALU.add)]
    product(nc, "gl", hT, DK, SEQ,
            [(A["w_gate_2"][c], False, [gate((mixT if c < 2 else sig)[:, (4 * c + u) % DK, :], 4 * c + u)
                                        for u in range(4)]) for c in range(4)], SLABS=2)
    product(nc, "pa", oaT, 2, SEQ,
            [(A["w_proj_a_2"][c], False, [weigh(mixT[:, 4 * c + u, :]) for u in range(4)]) for c in range(2)], SLABS=2)
    product(nc, "pb", obT, DK, SEQ,
            [(A["w_proj_b_2"][c], False, [weigh_and_add(4 * c + u) for u in range(4)]) for c in range(2)], SLABS=2)


def gated_add(nc, mixT, w, g1, h):
    def add(t, half):
        cols = slice(half * BANK, (half + 1) * BANK)
        return ON_DVE, lambda psum: [
            lambda: nc.vector.tensor_tensor(psum, psum, g1[:, cols], ALU.mult),
            lambda: nc.vector.tensor_tensor(h[:, t, cols], h[:, t, cols], psum, ALU.add)]
    product(nc, "wo2", mixT, DK, SEQ, [(w[half], True, [add(t, half) for t in range(TT)]) for half in range(2)],
            SLABS=2)


def finish(nc, acc, g2, A):
    with ExitStack() as ctx:
        sb, _, sem = phase_tools(nc, ctx, "fi")
        hb = sb("hb", [P, TT, D])
        part = sb("part", [P, TT, D])
        res = sb("res", [P, TT, D])
        h_in, scaled, added = sem("h_in"), sem("scaled"), sem("added")
        stored = [sem(f"stored{t}") for t in range(TT)]
        block = ctx.enter_context(nc.Block())

        @block.sync
        def _(sp):
            sp.dma_start(hb[:], A["h_scratch"].rearrange("(t p) d -> p t d", p=P)).then_inc(h_in, 16)
            for t in range(TT):
                sp.wait_ge(added, t + 1)
                sp.dma_start(A["out"][t * P:(t + 1) * P, :], res[:, t, :]).then_inc(stored[t], 16)
            for t in range(TT):
                sp.wait_ge(stored[t], 16)

        @block.vector
        def _(dve):
            for t in range(TT):
                nc.vector.tensor_tensor(part[:, t, :], acc[:, t, :], g2[:], ALU.mult).then_inc(scaled, 1)
            dve.wait_ge(h_in, 16)
            for t in range(TT):
                dve.wait_ge(scaled, t + 1)
                nc.vector.tensor_tensor(res[:, t, :], part[:, t, :], hb[:, t, :], ALU.add).then_inc(added, 1)


def scales(nc, C, mods):
    with ExitStack() as ctx:
        block = ctx.enter_context(nc.Block())

        @block.vector
        def _(dve):
            V = nc.vector
            for i, name in enumerate(("norm1_g", "norm2_g")):
                a = COLS[name][0]
                V.scalar_tensor_tensor(C["scales"][:, i, :], mods[:, 2 * i + 1, :], 1.0,
                                       C["cols"][:, a:a + 8], ALU.add, ALU.mult)
            V.tensor_scalar(C["subln"][:], column(C, "subln_g")(0), 1.0 - LAM_INIT, None, ALU.mult)


def program(nc, A, stop=None):
    with ExitStack() as ctx:
        C = constants(nc, ctx, A["cols"])
        sb, _, _ = phase_tools(nc, ctx, "main")
        h = sb("h", [P, TT, D])
        hT = sb("hT", [P, DK, SEQ])
        load(nc, "x", [(h[:], A["x"].rearrange("(t p) d -> p t d", p=P))])
        block1(nc, C, h, hT, A)
        mods = sb("mods", [P, MODS, DK])
        g1 = sb("g1", [P, D])
        g2 = sb("g2", [P, D])
        C["scales"] = sb("scales", [P, 2, DK])
        C["subln"] = sb("subln", [P, 1])
        modulation(nc, C, A, mods, g1, g2)
        scales(nc, C, mods)
        block2(nc, C, h, hT, mods, g1, g2, A)


def lay_out(i):
    def one(name):
        return np.asarray(i[name])[0]

    def vec(x):
        return np.asarray(x).reshape(-1, P).T

    def tok(w, width):
        k, n = w.shape
        return np.ascontiguousarray(w.reshape(k // P, P, n // width, width).transpose(2, 1, 0, 3))

    def states(x):
        return x.reshape(STILES, P).T

    a = {"x": np.asarray(i["x"])[0], "mem": np.asarray(i["mem"])[0]}
    step = np.repeat(one("ssm_log_step")[:, None], STATES, axis=1)
    cols = {
        "att_q_g": vec(np.tile(one("att_q_g"), 2)), "att_k_g": vec(np.tile(one("att_k_g"), 2)),
        "ssm_d": vec(one("ssm_d").reshape(-1)),
        "lam": np.concatenate([states(one("ssm_lam_re")), states(one("ssm_lam_im")), states(step)], axis=1),
        "norm1_g": vec(one("norm1_g_2")), "norm2_g": vec(one("norm2_g_2")), "b_gate": vec(one("b_gate_2")),
        "b_ada": vec(one("b_ada_2")), "subln_g": vec(one("subln_g_2")), "c": vec(i["c_2"]),
    }
    for name in COLS:
        if name not in cols:
            cols[name] = vec(one(name))
    a["cols"] = np.ascontiguousarray(np.concatenate([cols[n] for n in COLS], axis=1))
    w_in = one("w_in")
    a["w_in"] = tok(w_in, BANK)
    dist = np.arange(P)[:, None] + (SEQ - P) - np.arange(SEQ)[None, :]
    bucket = np.clip(dist, -(CHUNK - 1), REL_MAX) + CHUNK - 1
    a["bias"] = np.ascontiguousarray(one("rel_bias")[:, bucket])
    bc = [one(n).reshape(STILES, P, GROUP).transpose(1, 0, 2) for n in ("ssm_b_re", "ssm_b_im")]
    bc += [one(n).transpose(0, 2, 1).reshape(STILES, P, GROUP).transpose(1, 0, 2) for n in ("ssm_c_re", "ssm_c_im")]
    a["ssm_bc"] = np.ascontiguousarray(np.stack(bc))
    a["w_glu"] = tok(one("ssm_w_glu"), P)
    a["w_out"] = tok(one("w_out"), BANK)
    for n in ("w_mem_q", "w_mem_k", "w_mem_v", "w_mem_o"):
        a[n] = tok(one(n), BANK)

    def experts(u):
        return np.ascontiguousarray(u.reshape(KEYS, P, DK, P).transpose(0, 3, 2, 1))

    def keys(k):
        return np.ascontiguousarray(k.reshape(HALVES, KEYS, P).transpose(2, 0, 1))
    a["w_peer_q"], a["peer_keys"] = tok(one("w_peer_q"), BANK), keys(one("peer_keys"))
    a["peer_u"], a["peer_v"] = experts(one("peer_u")), one("peer_v").reshape(KEYS, P, D)
    a["w_query_2"], a["sub_keys_2"] = tok(one("w_query_2"), BANK), keys(one("sub_keys_2"))
    a["expert_u_2"], a["expert_v_2"] = experts(one("expert_u_2")), one("expert_v_2").reshape(KEYS, P, D)

    w2 = one("w_in_2")
    s = np.cumsum([0, DIL_W, DIL_W, DIL_W, DIFF_W, DIFF_W, DIFF_W, 2 * D])
    a["w_qk_2"] = tok(np.concatenate([w2[:, s[0]:s[2]], w2[:, s[3]:s[5]]], axis=1), BANK)
    a["w_va_2"] = tok(w2[:, s[2]:s[3]], DIL_W // 2)
    a["w_vb_2"] = tok(w2[:, s[5]:s[6]], BANK)
    a["w_gate_2"] = tok(w2[:, s[6]:s[7]], BANK)
    a["w_proj_a_2"], a["w_proj_b_2"] = tok(one("w_proj_a_2"), BANK), tok(one("w_proj_b_2"), BANK)
    a["w_out_2"], a["w_ada"] = tok(one("w_out_2"), BANK), tok(one("w_ada_2"), BANK)
    b_ada = one("b_ada_2").reshape(6, D)
    a["ada_rows"] = np.ascontiguousarray(np.stack([b_ada[2], b_ada[5]]))
    a["positions"] = np.asarray(i["positions_2"])[0]
    half = np.arange(0, HEAD, 2, dtype=np.float32) / np.float32(HEAD)
    inv_freq = (np.float32(1.0) / (np.float32(10000.0) ** half)).astype(np.float32)
    gains = [np.tile(one(n), w // HEAD) for n, w in (("qn_a_2", DIL_W), ("kn_a_2", DIL_W), ("qn_b_2", DIFF_W),
                                                     ("kn_b_2", DIFF_W))]
    lams = [one(n) for n in ("lam_q1_2", "lam_k1_2", "lam_q2_2", "lam_k2_2")]
    a["rows"] = np.concatenate(gains + [inv_freq] + lams)
    q = np.arange(SEQ)[:, None]
    k = np.arange(SEQ)[None, :]
    masks = np.full((SEQ, 2 * SEQ + 3 * P), MASKED, np.float32)
    allowed = [((q - k) % r == 0) & (np.abs(q - k) <= w // 2) for w, r in DIL]
    masks[:, 0:SEQ] = np.where(allowed[1], 0.0, MASKED)
    masks[:, SEQ:2 * SEQ] = np.where(allowed[2], 0.0, MASKED)
    for t in range(TT):
        a0, a1 = max(0, t - 1) * P, min(TT, t + 2) * P
        rows = slice(t * P, (t + 1) * P)
        masks[rows, 2 * SEQ:2 * SEQ + a1 - a0] = np.where(allowed[0][rows, a0:a1], 0.0, MASKED)
    a["masks"] = np.ascontiguousarray(masks.reshape(TT, P, -1).transpose(1, 0, 2))
    return a


def build(nc, arrays):
    A = {n: nc.dram_tensor(f"in_{n}", x.shape, mybir.dt.from_np(x.dtype), kind="ExternalInput").ap()
         for n, x in arrays.items()}
    A["gates"] = nc.dram_tensor("gates", (KEYS, P, SEQ), F32).ap()
    A["h_scratch"] = nc.dram_tensor("h_scratch", (SEQ, D), F32).ap()
    A["out"] = nc.dram_tensor("out_0", (SEQ, D), F32, kind="ExternalOutput").ap()
    program(nc, A)


def kernel(**inputs):
    import concourse.bacc as bacc
    from concourse.bass_utils import run_bass_kernel_spmd
    arrays = lay_out(inputs)
    nc = bacc.Bacc("TRN2", target_bir_lowering=False, num_devices=1)
    build(nc, arrays)
    r = run_bass_kernel_spmd(nc, [{f"in_{n}": x for n, x in arrays.items()}], core_ids=[0])
    return r.results[0]["out_0"].reshape(1, SEQ, D)
```

```python
from contextlib import ExitStack

import numpy as np
import concourse.bass as bass
from concourse import mybir

F32 = mybir.dt.float32
F32R = mybir.dt.float32r
U32 = mybir.dt.uint32
I32 = mybir.dt.int32
ALU = mybir.AluOpType
ACT = mybir.ActivationFunctionType
AX = mybir.AxisListType

P = 128
SEQ, D = 512, 1024
TT = SEQ // P
DK = D // P
BANK = 512
EPS = 1e-6
MASKED = -1e30

CHUNK = 64
HEADS, HEAD = 8, 64
ATT_W = HEADS * HEAD
SSM_W = D - ATT_W
STATES, GROUP = 64, 16
SSM_GROUPS = SSM_W // GROUP
STILES = SSM_GROUPS * STATES // P
MEM_LEN, MEM_HEADS = 256, 4
MEM_HEAD = D // MEM_HEADS
REL_MAX = 128

KEYS, TOPK, PHEADS = 128, 16, 8
HALVES = 2 * PHEADS
PAIRS = PHEADS * TOPK
PIECE = 32
EGROUP = 4

DIL_W, DIFF_W = 768, 1024
DIL = ((128, 1), (512, 4), (2048, 16))
DIL_HEADS = 4
DIL_KEYS = 2 * SEQ + 3 * P
DIFF_HEADS = 8
LAM_INIT = 0.2

TWO_PI = 2.0 * float(np.pi)
TWO_PI_A = float(np.float32(6.28125))
TWO_PI_B = float(np.float32(np.floor((TWO_PI - TWO_PI_A) * 2.0**23) / 2.0**23))
TWO_PI_C = float(np.float32(TWO_PI - TWO_PI_A - TWO_PI_B))
ROUND = 12582912.0


def phase_tools(nc, ctx, tag):
    def sb(name, shape, dt=F32):
        return ctx.enter_context(nc.sbuf_tensor(f"{tag}_{name}", shape, dt))

    def ps(name, shape, dt=F32):
        return ctx.enter_context(nc.psum_tensor(f"{tag}_{name}", shape, dt))

    taken = []

    def clear():
        nc.clear_and_free_semaphores(taken)
        nc.all_engine_barrier()

    def sem(name):
        if not taken:
            ctx.callback(clear)
        taken.append(nc.alloc_semaphore(f"{tag}_{name}"))
        return taken[-1]

    return sb, ps, sem


class Chain:
    def __init__(self, eng, sem):
        self.eng, self.sem, self.n = eng, sem, 0

    def add(self, instruction):
        instruction.then_inc(self.sem, 1)
        self.n += 1

    def wait(self):
        self.eng.wait_ge(self.sem, self.n)


def refined_rsqrt(V, chain, meansq, guess, tmp, out):
    chain.add(V.tensor_tensor(tmp, meansq, guess, ALU.mult))
    chain.wait()
    chain.add(V.tensor_tensor(tmp, tmp, guess, ALU.mult))
    chain.wait()
    chain.add(V.tensor_scalar(tmp, tmp, -0.5, 1.5, ALU.mult, ALU.add))
    chain.wait()
    chain.add(V.tensor_tensor(out, tmp, guess, ALU.mult))
    chain.wait()


ON_ACT, ON_DVE = 0, 1


def product(nc, tag, srcT, kt, tokens, chunks, SLABS=4, transfers=()):
    width = max(src.shape[2] for src, _, _ in chunks)
    LOADS = 8
    NCH = len(chunks)

    def evacuated(upto, which):
        return sum(e == which for _, _, units in chunks[:upto + 1] for e, _ in units)

    with ExitStack() as ctx:
        sb, ps, sem = phase_tools(nc, ctx, tag)
        x_hi, x_lo = sb("x_hi", [P, kt, tokens], F32R), sb("x_lo", [P, kt, tokens], F32R)
        w = sb("w", [P, LOADS, width])
        w_hi, w_lo = sb("w_hi", [P, SLABS, width], F32R), sb("w_lo", [P, SLABS, width], F32R)
        out = ps("out", [P, 8, BANK])
        loaded = [sem(f"loaded{n}") for n in range(LOADS)]
        transferred = sem("transferred")
        x_hi_ready, x_ready, w_hi_ready, w_ready, multiplied = (
            sem(n) for n in ("x_hi_ready", "x_ready", "w_hi_ready", "w_ready", "multiplied"))
        copied = [sem("copied_by_act"), sem("copied_by_dve")]
        step = [sem("step_act"), sem("step_dve")]
        block = ctx.enter_context(nc.Block())

        @block.sync
        def _(sp):
            for c, (src, _, _) in enumerate(chunks):
                for k in range(kt):
                    s = c * kt + k
                    if s >= LOADS:
                        sp.wait_ge(w_ready, s - LOADS + 1)
                    sp.dma_start(w[:, s % LOADS, 0:src.shape[2]], src[:, k, :]).then_inc(loaded[s % LOADS], 16)
            for n, (to, source) in enumerate(transfers):
                sp.dma_start(to, source).then_inc(transferred, 16)
                sp.wait_ge(transferred, 16 * (n + 1))

        @block.tensor
        def _(pe):
            for c, (src, on_tokens, units) in enumerate(chunks):
                cols = src.shape[2]
                for which in (ON_ACT, ON_DVE):
                    if c >= 2 and evacuated(c - 2, which):
                        pe.wait_ge(copied[which], evacuated(c - 2, which))
                for k in range(kt):
                    s = (c * kt + k) % SLABS
                    if c == 0:
                        pe.wait_ge(x_ready, k + 1)
                    pe.wait_ge(w_ready, c * kt + k + 1)
                    for u in range(len(units)):
                        tile = slice(u * P, (u + 1) * P)
                        for n, (xs, ws) in enumerate(((x_hi, w_hi), (x_lo, w_hi), (x_hi, w_lo))):
                            if on_tokens:
                                dst, lhsT, rhs = out[:, c % 2 * 4 + u, 0:cols], xs[:, k, tile], ws[:, s, 0:cols]
                            else:
                                dst, lhsT, rhs = out[:, c % 2 * 4 + u, 0:tokens], ws[:, s, tile], xs[:, k, :]
                            last = nc.tensor.matmul(dst, lhsT, rhs, start=(k == 0 and n == 0),
                                                    stop=(k == kt - 1 and n == 2), skip_group_check=True)
                    last.then_inc(multiplied, 1)

        def evacuations(eng, which, c, steps):
            src, on_tokens, units = chunks[c]
            cols = src.shape[2] if on_tokens else tokens
            if any(e == which for e, _ in units):
                eng.wait_ge(multiplied, kt * (c + 1))
            for u, (engine, evacuate) in enumerate(units):
                if engine != which:
                    continue
                parts = evacuate(out[:, c % 2 * 4 + u, 0:cols])
                for make in parts[:-1]:
                    make().then_inc(step[which], 1)
                    steps += 1
                    eng.wait_ge(step[which], steps)
                parts[-1]().then_inc(copied[which], 1)
            return steps

        @block.scalar
        def _(act):
            steps = 0
            for c, (src, _, _) in enumerate(chunks):
                cols = src.shape[2]
                for k in range(kt):
                    s = c * kt + k
                    if c == 0:
                        nc.scalar.copy(x_hi[:, k, :], srcT[:, k, 0:tokens]).then_inc(x_hi_ready, 1)
                    if s >= SLABS:
                        act.wait_ge(multiplied, s - SLABS + 1)
                    act.wait_ge(loaded[s % LOADS], 16 * (s // LOADS + 1))
                    nc.scalar.copy(w_hi[:, s % SLABS, 0:cols], w[:, s % LOADS, 0:cols]).then_inc(w_hi_ready, 1)
                if c >= 1:
                    steps = evacuations(act, ON_ACT, c - 1, steps)
            evacuations(act, ON_ACT, NCH - 1, steps)

        @block.vector
        def _(dve):
            steps = 0
            for c, (src, _, _) in enumerate(chunks):
                cols = src.shape[2]
                for k in range(kt):
                    s = c * kt + k
                    if c == 0:
                        dve.wait_ge(x_hi_ready, k + 1)
                        nc.vector.tensor_tensor(x_lo[:, k, :], srcT[:, k, 0:tokens], x_hi[:, k, :],
                                                ALU.subtract).then_inc(x_ready, 1)
                    dve.wait_ge(w_hi_ready, s + 1)
                    nc.vector.tensor_tensor(w_lo[:, s % SLABS, 0:cols], w[:, s % LOADS, 0:cols],
                                            w_hi[:, s % SLABS, 0:cols], ALU.subtract).then_inc(w_ready, 1)
                if c >= 1:
                    steps = evacuations(dve, ON_DVE, c - 1, steps)
            evacuations(dve, ON_DVE, NCH - 1, steps)


def alternate(u):
    return ON_ACT if u % 2 == 0 else ON_DVE


def copy_to(nc, u, dst):
    if alternate(u) == ON_ACT:
        return ON_ACT, lambda psum: [lambda: nc.scalar.copy(dst, psum)]
    return ON_DVE, lambda psum: [lambda: nc.vector.tensor_copy(dst, psum)]


def columns_to(nc, dst, first, cols, tiles):
    return [copy_to(nc, t, dst[:, t, first:first + cols]) for t in range(tiles)]


def heads_norm_transpose(nc, tag, C, src, tiles, heads, hd, dst, gain):
    width = heads * hd
    kt, n = width // P, tiles * P
    with ExitStack() as ctx:
        sb, ps, sem = phase_tools(nc, ctx, tag)
        sq = sb("sq", [P, 2, width])
        sumsq = sb("sumsq", [P, tiles, heads])
        meansq = sb("meansq", [P, tiles, heads])
        rms = sb("rms", [P, tiles, heads])
        guess, tmp, rstd = (sb(n, [P, tiles, heads]) for n in ("guess", "tmp", "rstd"))
        tp = ps("tp", [P, 4, BANK])
        squared, summed, mean_ready, rms_ready, rstd_ready = (
            sem("squared"), sem("summed"), sem("mean_ready"), sem("rms_ready"), sem("rstd_ready"))
        normed, turned, copied = sem("normed"), sem("turned"), [sem("copied_by_act"), sem("copied_by_dve")]
        block = ctx.enter_context(nc.Block())

        @block.scalar
        def _(act):
            for t in range(tiles):
                if t >= 2:
                    act.wait_ge(summed, t - 1)
                nc.scalar.activation(sq[:, t % 2, :], src[:, t, :], ACT.Square).then_inc(squared, 1)
            act.wait_ge(mean_ready, 1)
            nc.scalar.activation(rms[:], meansq[:], ACT.Sqrt).then_inc(rms_ready, 1)
            for k in range(0, kt, 2):
                act.wait_ge(turned, k + 1)
                nc.scalar.activation(dst[:, k, :], tp[:, k % 4, 0:n], ACT.Identity,
                                     scale=gain(k)).then_inc(copied[0], 1)

        @block.vector
        def _(dve):
            for t in range(tiles):
                dve.wait_ge(squared, t + 1)
                nc.vector.tensor_reduce(sumsq[:, t, :], sq[:, t % 2, :].rearrange("p (h d) -> p h d", h=heads),
                                        AX.X, ALU.add).then_inc(summed, 1)
            dve.wait_ge(summed, tiles)
            nc.vector.tensor_scalar(meansq[:], sumsq[:], 1.0 / hd, EPS, ALU.mult, ALU.add).then_inc(mean_ready, 1)
            dve.wait_ge(rms_ready, 1)
            ch = Chain(dve, rstd_ready)
            ch.add(nc.vector.reciprocal(guess[:], rms[:]))
            ch.wait()
            refined_rsqrt(nc.vector, ch, meansq[:], guess[:], tmp[:], rstd[:])
            for t in range(tiles):
                x = src[:, t, :].rearrange("p (h d) -> p h d", h=heads)
                nc.vector.tensor_tensor(x, x, rstd[:, t, :].unsqueeze(2).broadcast_to([P, heads, hd]),
                                        ALU.mult).then_inc(normed, 1)
            for k in range(1, kt, 2):
                dve.wait_ge(turned, k + 1)
                nc.vector.tensor_scalar(dst[:, k, :], tp[:, k % 4, 0:n], gain(k), None,
                                        ALU.mult).then_inc(copied[1], 1)

        @block.tensor
        def _(pe):
            pe.wait_ge(normed, tiles)
            for k in range(kt):
                if k >= 4:
                    pe.wait_ge(copied[k % 2], (k - 4) // 2 + 1)
                for t in range(tiles):
                    last = nc.tensor.transpose(tp[:, k % 4, t * P:(t + 1) * P], src[:, t, k * P:(k + 1) * P],
                                               C["ident"][:])
                last.then_inc(turned, 1)


def feature_norm(nc, tag, C, src, kt, dst, gain):
    with ExitStack() as ctx:
        sb, ps, sem = phase_tools(nc, ctx, tag)
        sq = sb("sq", [P, kt, SEQ])
        meansq, rms, guess, tmp, rstd = (sb(n, [P, SEQ]) for n in ("meansq", "rms", "guess", "tmp", "rstd"))
        tot = ps("tot", [P, BANK])
        squared, totalled, mean_ready, rms_ready, step = (
            sem(n) for n in ("squared", "totalled", "mean_ready", "rms_ready", "step"))
        block = ctx.enter_context(nc.Block())
        V = nc.vector

        @block.scalar
        def _(act):
            for k in range(kt):
                nc.scalar.activation(sq[:, k, :], src[:, k, :], ACT.Square).then_inc(squared, 1)
            act.wait_ge(mean_ready, 1)
            nc.scalar.activation(rms[:], meansq[:], ACT.Sqrt).then_inc(rms_ready, 1)

        @block.tensor
        def _(pe):
            for k in range(kt):
                pe.wait_ge(squared, k + 1)
                last = nc.tensor.matmul(tot[:], C["ones"][:], sq[:, k, :], start=(k == 0), stop=(k == kt - 1))
            last.then_inc(totalled, 1)

        @block.vector
        def _(dve):
            ch = Chain(dve, step)
            dve.wait_ge(totalled, 1)
            V.tensor_scalar(meansq[:], tot[:], 1.0 / (kt * P), EPS, ALU.mult, ALU.add).then_inc(mean_ready, 1)
            dve.wait_ge(rms_ready, 1)
            ch.add(V.reciprocal(guess[:], rms[:]))
            ch.wait()
            refined_rsqrt(V, ch, meansq[:], guess[:], tmp[:], rstd[:])
            for k in range(kt):
                V.scalar_tensor_tensor(dst[:, k, :], src[:, k, :], gain(k), rstd[:], ALU.mult, ALU.mult)


def tile_norm(nc, tag, C, src, kt, dst, gain):
    with ExitStack() as ctx:
        sb, ps, sem = phase_tools(nc, ctx, tag)
        sq = sb("sq", [P, kt, SEQ])
        collect = sb("collect", [P, kt, kt])
        spread = sb("spread", [kt, kt, P])
        meansq, rms, guess, tmp, rstd = (sb(n, [kt, SEQ]) for n in ("meansq", "rms", "guess", "tmp", "rstd"))
        tot = ps("tot", [P, BANK])
        wide = ps("wide", [P, 4, BANK])
        squared, zeroed, collect_ready, totalled, mean_ready, rms_ready, step, roots_ready, spread_out, done = (
            sem(n) for n in ("squared", "zeroed", "collect_ready", "totalled", "mean_ready", "rms_ready", "step",
                             "roots_ready", "spread_out", "done"))
        block = ctx.enter_context(nc.Block())
        V = nc.vector

        @block.scalar
        def _(act):
            for k in range(kt):
                nc.scalar.activation(sq[:, k, :], src[:, k, :], ACT.Square).then_inc(squared, 1)
            act.wait_ge(mean_ready, 1)
            nc.scalar.activation(rms[:], meansq[:], ACT.Sqrt).then_inc(rms_ready, 1)

        @block.tensor
        def _(pe):
            pe.wait_ge(collect_ready, kt)
            for k in range(kt):
                pe.wait_ge(squared, k + 1)
                last = nc.tensor.matmul(tot[0:kt, :], collect[:, k, :], sq[:, k, :], start=(k == 0),
                                        stop=(k == kt - 1))
            last.then_inc(totalled, 1)
            pe.wait_ge(roots_ready, 1)
            for k in range(kt):
                if k >= 4:
                    pe.wait_ge(done, k - 3)
                nc.tensor.matmul(wide[:, k % 4, :], spread[:, k, :], rstd[:], start=True,
                                 stop=True).then_inc(spread_out, 1)

        @block.vector
        def _(dve):
            V.memset(collect[:], 0.0).then_inc(zeroed, 1)
            dve.wait_ge(zeroed, 1)
            for k in range(kt):
                V.memset(collect[:, k, k:k + 1], 1.0).then_inc(collect_ready, 1)
            ch = Chain(dve, step)
            ch.add(V.tensor_copy(spread[:], C["ident"][0:kt, 0:kt].unsqueeze(2).broadcast_to([kt, kt, P])))
            dve.wait_ge(totalled, 1)
            V.tensor_scalar(meansq[:], tot[0:kt, :], 1.0 / P, EPS, ALU.mult, ALU.add).then_inc(mean_ready, 1)
            dve.wait_ge(rms_ready, 1)
            ch.add(V.reciprocal(guess[:], rms[:]))
            ch.wait()
            refined_rsqrt(V, ch, meansq[:], guess[:], tmp[:], rstd[:])
            V.engine_nop().then_inc(roots_ready, 1)
            for k in range(kt):
                dve.wait_ge(spread_out, k + 1)
                V.scalar_tensor_tensor(dst[:, k, :], src[:, k, :], gain(k), wide[:, k % 4, :],
                                       ALU.mult, ALU.mult).then_inc(done, 1)


def attention(nc, tag, C, items, outs, wide, scale, parts=1, lam=None, score_ring=2, turn_ring=2,
              out_ring=2, bias_loads=(), bias_prepare=None):
    R = 2
    with ExitStack() as ctx:
        sb, ps, sem = phase_tools(nc, ctx, tag)
        biased = any(it["bias"] is not None for it in items)
        s_sb = sb("s", [P, R, wide]) if biased else None
        e = sb("e", [P, R, parts, wide])
        p = sb("p", [P, R, wide])
        first = sb("first", [P, R, wide]) if parts == 2 else None
        pT = sb("pT", [P, R, wide])
        mx = sb("mx", [P, R, parts])
        neg = sb("neg", [P, R, parts])
        total = sb("total", [P, R, parts])
        rtotal = sb("rtotal", [P, R, parts])
        factor = sb("factor", [P, R])
        sbanks = parts * -(-wide // BANK)
        score = ps("score", [P, score_ring, sbanks * BANK])
        tp = ps("tp", [P, turn_ring, BANK])
        out = ps("out", [P, out_ring, BANK])
        scored, biased_ready, max_ready, neg_ready, exp_ready = (
            sem("scored"), sem("biased_ready"), sem("max_ready"), sem("neg_ready"), sem("exp_ready"))
        recip_ready, step, p_ready, turned, moved, summed, out_copied = (
            sem("recip_ready"), sem("step"), sem("p_ready"), sem("turned"), sem("moved"), sem("summed"),
            sem("out_copied"))
        bias_in = sem("bias_in")
        bias_set = sem("bias_set")
        block = ctx.enter_context(nc.Block())
        N = len(items)
        turns = [(i, a, min(4, it["width"] // P - a)) for i, it in enumerate(items)
                 for a in range(0, it["width"] // P, 4)]
        turns_before = [sum(1 for x in turns if x[0] < i) for i in range(N + 1)]
        ends = {}
        for n, (_, _, i) in enumerate(outs):
            ends.setdefault(i, []).append(n)

        def part_of(tile, it, s):
            return tile[:, s * wide:s * wide + it["width"]] if parts == 2 else tile[:, 0:it["width"]]

        @block.sync
        def _(sp):
            for n, (dst, src, after) in enumerate(bias_loads):
                if after is not None:
                    sp.wait_ge(biased_ready, after + 1)
                sp.dma_start(dst, src).then_inc(bias_in, 16)
                sp.wait_ge(bias_in, 16 * (n + 1))

        @block.gpsimd
        def _(pool):
            for n in range(len(bias_loads)):
                pool.wait_ge(bias_in, 16 * (n + 1))
                if bias_prepare:
                    bias_prepare(n).then_inc(bias_set, 1)
                else:
                    pool.sem_inc(bias_set, 1)

        def scores(pe, i):
            it = items[i]
            if i >= score_ring:
                pe.wait_ge(biased_ready if biased else exp_ready, (i - score_ring + 1) * (1 if biased else parts))
            for c0, n, pairs in it["scores"]:
                for m, (lhsT, rhs) in enumerate(pairs):
                    last = nc.tensor.matmul(score[:, i % score_ring, c0:c0 + n], lhsT, rhs, start=(m == 0),
                                            stop=(m == len(pairs) - 1), skip_group_check=True)
            last.then_inc(scored, 1)

        def turn(pe, i):
            pe.wait_ge(p_ready, i + 1)
            for n in range(turns_before[i], turns_before[i + 1]):
                _, a, tiles = turns[n]
                if n >= turn_ring:
                    pe.wait_ge(moved, n - turn_ring + 1)
                for m in range(tiles):
                    last = nc.tensor.transpose(tp[:, n % turn_ring, m * P:(m + 1) * P],
                                               p[:, i % R, (a + m) * P:(a + m + 1) * P], C["ident"][:])
                last.then_inc(turned, 1)

        def weigh_values(pe, i):
            pe.wait_ge(moved, turns_before[i + 1])
            for o, rows, cols, values in items[i]["values"]:
                if o >= out_ring:
                    pe.wait_ge(out_copied, o - out_ring + 1)
                for m, (kt, v) in enumerate(values):
                    last = nc.tensor.matmul(out[rows, o % out_ring, cols], v,
                                            pT[:, i % R, kt * P:(kt + 1) * P], start=(m == 0),
                                            stop=(m == len(values) - 1), skip_group_check=True)
            last.then_inc(summed, 1)

        @block.tensor
        def _(pe):
            for i in range(min(score_ring, N)):
                scores(pe, i)
            for i in range(N):
                if i + score_ring < N:
                    scores(pe, i + score_ring)
                turn(pe, i)
                if i >= 1:
                    weigh_values(pe, i - 1)
            weigh_values(pe, N - 1)

        def exps(act, i):
            it = items[i]
            act.wait_ge(neg_ready, i + 1)
            if i >= R:
                act.wait_ge(p_ready, i - R + 1)
            for s in range(parts):
                src = s_sb[:, i % R, 0:it["width"]] if biased else part_of(score[:, i % score_ring], it, s)
                nc.scalar.activation(e[:, i % R, s, 0:it["width"]], src, ACT.Exp, bias=neg[:, i % R, s:s + 1],
                                     scale=1.0 if biased else scale,
                                     accum_out=total[:, i % R, s:s + 1]).then_inc(exp_ready, 1)

        def moves(act, i):
            if i >= R:
                act.wait_ge(summed, i - R + 1)
            for n in range(turns_before[i], turns_before[i + 1]):
                _, a, tiles = turns[n]
                act.wait_ge(turned, n + 1)
                nc.scalar.copy(pT[:, i % R, a * P:(a + tiles) * P],
                               tp[:, n % turn_ring, 0:tiles * P]).then_inc(moved, 1)

        @block.scalar
        def _(act):
            exps(act, 0)
            for i in range(N):
                if i + 1 < N:
                    exps(act, i + 1)
                moves(act, i)

        def maxima(dve, i):
            it = items[i]
            dve.wait_ge(scored, i + 1)
            if biased:
                if i >= R:
                    dve.wait_ge(exp_ready, i - R + 1)
                if bias_loads:
                    dve.wait_ge(bias_set, it["bias_load"] + 1)
                nc.vector.scalar_tensor_tensor(s_sb[:, i % R, 0:it["width"]], score[:, i % score_ring, 0:it["width"]],
                                               scale, it["bias"], ALU.mult, ALU.add).then_inc(biased_ready, 1)
                dve.wait_ge(biased_ready, i + 1)
            elif i >= R:
                dve.wait_ge(exp_ready, parts * (i - R + 1))
            for s in range(parts):
                src = s_sb[:, i % R, 0:it["width"]] if biased else part_of(score[:, i % score_ring], it, s)
                nc.vector.tensor_reduce(mx[:, i % R, s:s + 1], src, AX.X, ALU.max).then_inc(max_ready, 1)
            dve.wait_ge(max_ready, parts * (i + 1))
            nc.vector.tensor_scalar(neg[:, i % R, :], mx[:, i % R, :], -1.0 if biased else -scale, None,
                                    ALU.mult).then_inc(neg_ready, 1)

        def weights(dve, i):
            it = items[i]
            w = it["width"]
            dve.wait_ge(exp_ready, parts * (i + 1))
            nc.vector.reciprocal(rtotal[:, i % R, :], total[:, i % R, :]).then_inc(recip_ready, 1)
            dve.wait_ge(recip_ready, i + 1)
            if i >= R:
                dve.wait_ge(turned, turns_before[i - R + 1])
            if parts == 1:
                nc.vector.tensor_scalar(p[:, i % R, 0:w], e[:, i % R, 0, 0:w], rtotal[:, i % R, 0:1], None,
                                        ALU.mult).then_inc(p_ready, 1)
                return
            nc.vector.tensor_scalar(first[:, i % R, 0:w], e[:, i % R, 0, 0:w], rtotal[:, i % R, 0:1], None,
                                    ALU.mult).then_inc(step, 1)
            nc.vector.tensor_tensor(factor[:, i % R:i % R + 1], rtotal[:, i % R, 1:2], lam, ALU.mult).then_inc(step, 1)
            dve.wait_ge(step, 2 * (i + 1))
            nc.vector.scalar_tensor_tensor(p[:, i % R, 0:w], e[:, i % R, 1, 0:w], factor[:, i % R:i % R + 1],
                                           first[:, i % R, 0:w], ALU.mult, ALU.add).then_inc(p_ready, 1)

        def finish(dve, i):
            for n in ends.get(i, []):
                rows, dst, _ = outs[n]
                dve.wait_ge(summed, i + 1)
                nc.vector.tensor_copy(dst, out[rows, n % out_ring, :]).then_inc(out_copied, 1)

        @block.vector
        def _(dve):
            maxima(dve, 0)
            for i in range(N):
                if i + 1 < N and score_ring > 1:
                    maxima(dve, i + 1)
                weights(dve, i)
                if i + 1 < N and score_ring == 1:
                    maxima(dve, i + 1)
                if i >= 2:
                    finish(dve, i - 2)
            for i in range(max(N - 2, 0), N):
                finish(dve, i)


def norm_transpose(nc, tag, C, src, tiles, width, dst, scale, bias=None, transfers=()):
    kt = width // P
    with ExitStack() as ctx:
        sb, ps, sem = phase_tools(nc, ctx, tag)
        xn = sb("xn", [P, tiles, width])
        junk = sb("junk", [P, width])
        sumsq = sb("sumsq", [P, tiles])
        meansq = sb("meansq", [P, tiles])
        rms = sb("rms", [P, tiles])
        guess, tmp, rstd = sb("guess", [P, tiles]), sb("tmp", [P, tiles]), sb("rstd", [P, tiles])
        tp = ps("tp", [P, 4, tiles * P if tiles * P == BANK else BANK])
        squares_done, mean_ready, rms_ready, rstd_ready = sem("sq"), sem("mean"), sem("rms"), sem("rstd")
        xn_ready, turned, copied = sem("xn_ready"), sem("turned"), [sem("copied_act"), sem("copied_dve")]
        transferred = sem("transferred")
        block = ctx.enter_context(nc.Block())

        @block.sync
        def _(sp):
            for n, (to, source) in enumerate(transfers):
                sp.dma_start(to, source).then_inc(transferred, 16)
                sp.wait_ge(transferred, 16 * (n + 1))

        @block.scalar
        def _(act):
            for t in range(tiles):
                if t >= 1:
                    act.wait_ge(squares_done, t)
                nc.scalar.activation(junk[:], src[:, t, :], ACT.Square,
                                     accum_out=sumsq[:, t:t + 1]).then_inc(squares_done, 1)
            act.wait_ge(mean_ready, 1)
            nc.scalar.activation(rms[:], meansq[:], ACT.Sqrt).then_inc(rms_ready, 1)
            for k in range(0, kt, 2):
                act.wait_ge(turned, k + 1)
                b = bias(k) if bias else 0.0
                nc.scalar.activation(dst[:, k, :], tp[:, k % 4, 0:tiles * P], ACT.Identity, bias=b,
                                     scale=scale(k)).then_inc(copied[0], 1)

        @block.vector
        def _(dve):
            dve.wait_ge(squares_done, tiles)
            nc.vector.tensor_scalar(meansq[:], sumsq[:], 1.0 / width, EPS, ALU.mult, ALU.add).then_inc(mean_ready, 1)
            dve.wait_ge(rms_ready, 1)
            ch = Chain(dve, rstd_ready)
            ch.add(nc.vector.reciprocal(guess[:], rms[:]))
            ch.wait()
            refined_rsqrt(nc.vector, ch, meansq[:], guess[:], tmp[:], rstd[:])
            for t in range(tiles):
                nc.vector.tensor_scalar(xn[:, t, :], src[:, t, :], rstd[:, t:t + 1], None,
                                        ALU.mult).then_inc(xn_ready, 1)
            for k in range(1, kt, 2):
                dve.wait_ge(turned, k + 1)
                b = bias(k) if bias else 0.0
                nc.vector.tensor_scalar(dst[:, k, :], tp[:, k % 4, 0:tiles * P], scale(k), b, ALU.mult,
                                        ALU.add).then_inc(copied[1], 1)

        @block.tensor
        def _(pe):
            pe.wait_ge(xn_ready, tiles)
            for k in range(kt):
                if k >= 4:
                    pe.wait_ge(copied[k % 2], (k - 4) // 2 + 1)
                for t in range(tiles):
                    last = nc.tensor.transpose(tp[:, k % 4, t * P:(t + 1) * P], xn[:, t, k * P:(k + 1) * P],
                                               C["ident"][:])
                last.then_inc(turned, 1)


def peer(nc, tag, C, h, hT, wq, keysT, u_tab, v_tab, gates, acc, modulation=None):
    with ExitStack() as outer:
        sbo, _, _ = phase_tools(nc, outer, tag)
        rows = [sbo(f"{n}T", [P, SEQ]) for n in ("first", "second", "gate")]
        with ExitStack() as mid:
            sbm, _, _ = phase_tools(nc, mid, tag + "m")
            qT = sbm("qT", [P, HALVES, SEQ])
            peer_queries(nc, tag + "q", hT, wq, qT)
            peer_choose(nc, tag + "c", C, qT, keysT, rows, modulation)
        peer_gates(nc, tag + "g", C, rows, gates)
    peer_experts(nc, tag + "e", hT, u_tab, v_tab, gates, acc)


def peer_queries(nc, tag, hT, wq, qT):
    product(nc, tag, hT, DK, SEQ,
            [(wq[c], False, [copy_to(nc, u, qT[:, 4 * c + u, :]) for u in range(4)]) for c in range(HALVES // 4)])


def peer_choose(nc, tag, C, qT, keysT, rows, modulation):
    with ExitStack() as ctx:
        sb, ps, sem = phase_tools(nc, ctx, tag)
        keys = sb("keys", [P, HALVES, KEYS])
        rest = sb("rest", [P, HALVES, KEYS])
        val = sb("val", [P, PHEADS, 2, TOPK])
        idx = sb("idx", [P, PHEADS, 2, TOPK], U32)
        idxf = sb("idxf", [P, PHEADS, 2, TOPK])
        cand = sb("cand", [P, PHEADS, TOPK, TOPK])
        crest = sb("crest", [P, PHEADS, TOPK * TOPK])
        top = sb("top", [P, PHEADS, TOPK])
        pos = sb("pos", [P, PHEADS, TOPK], U32)
        part = sb("part", [P, 2, PAIRS], U32)
        partf = sb("partf", [P, 2, PAIRS])
        picked = sb("picked", [P, 2, PHEADS, TOPK, TOPK])
        chosen = sb("chosen", [P, 2, PAIRS])
        shifted = sb("shifted", [P, PHEADS, TOPK])
        weight = sb("weight", [P, PHEADS, TOPK])
        total = sb("total", [P, PHEADS])
        rtotal = sb("rtotal", [P, PHEADS])
        gate = sb("gate", [P, PHEADS, TOPK])
        score = ps("score", [P, HALVES, KEYS])
        tp = ps("tp", [P, 3, P])
        if modulation:
            modulation.place(ctx)
        keys_in, scored, step, exp_done, turned, moved = (
            sem("keys_in"), sem("scored"), sem("step"), sem("exp_done"), sem("turned"), sem("moved"))
        scores_free, chosen_ready = sem("scores_free"), sem("chosen_ready")
        shifted_ready, hit_ready, rows_picked = sem("shifted_ready"), sem("hit_ready"), sem("rows_picked")
        block = ctx.enter_context(nc.Block())
        V = nc.vector

        @block.sync
        def _(sp):
            sp.dma_start(keys[:], keysT).then_inc(keys_in, 16)
            if modulation:
                modulation.load(sp)

        def turn(pe, t):
            pe.wait_ge(chosen_ready, t + 1)
            if t >= 1:
                pe.wait_ge(moved, 3 * t)
            for n, src in enumerate((chosen[:, 0, :], chosen[:, 1, :], gate[:].rearrange("p h k -> p (h k)"))):
                last = nc.tensor.transpose(tp[:, n, 0:P], src, C["ident"][:])
            last.then_inc(turned, 1)

        @block.tensor
        def _(pe):
            pe.wait_ge(keys_in, 16)
            for t in range(TT):
                if t >= 1:
                    pe.wait_ge(scores_free, t)
                for j in range(HALVES):
                    last = nc.tensor.matmul(score[:, j, :], qT[:, j, t * P:(t + 1) * P], keys[:, j, :],
                                            start=True, stop=True, skip_group_check=True)
                last.then_inc(scored, 1)
                if t >= 1:
                    turn(pe, t - 1)
                if modulation:
                    for c in range(t * modulation.CHUNKS // TT, (t + 1) * modulation.CHUNKS // TT):
                        modulation.multiply(pe, c)
            turn(pe, TT - 1)

        @block.scalar
        def _(act):
            if modulation:
                modulation.silu(act)
            for t in range(TT):
                act.wait_ge(shifted_ready, t + 1)
                nc.scalar.activation(weight[:], shifted[:], ACT.Exp).then_inc(exp_done, 1)
                act.wait_ge(turned, t + 1)
                for n in range(3):
                    nc.scalar.copy(rows[n][:, t * P:(t + 1) * P], tp[:, n, 0:P]).then_inc(moved, 1)

        def pick(eng, s):
            return eng.tensor_tensor(picked[:, s], picked[:, s],
                                     idxf[:, :, s, :].unsqueeze(2).broadcast_to([P, PHEADS, TOPK, TOPK]), ALU.mult)

        @block.gpsimd
        def _(pool):
            for t in range(TT):
                pool.wait_ge(hit_ready, 2 * t + 1)
                pick(nc.gpsimd, 0).then_inc(rows_picked, 1)

        @block.vector
        def _(dve):
            n = 0
            if modulation:
                modulation.widen(dve)
            for t in range(TT):
                dve.wait_ge(scored, t + 1)
                for j in range(HALVES):
                    V.max(val[:, j // 2, j % 2, 0:8], score[:, j, :]).then_inc(step, 1)
                n += HALVES
                dve.wait_ge(step, n)
                for j in range(HALVES):
                    V.max_index(idx[:, j // 2, j % 2, 0:8], val[:, j // 2, j % 2, 0:8], score[:, j, :])
                    V.match_replace(rest[:, j, :], val[:, j // 2, j % 2, 0:8], score[:, j, :],
                                    -3.0e38).then_inc(step, 1)
                n += HALVES
                dve.wait_ge(step, n)
                V.engine_nop().then_inc(scores_free, 1)
                for j in range(HALVES):
                    V.max(val[:, j // 2, j % 2, 8:16], rest[:, j, :]).then_inc(step, 1)
                n += HALVES
                dve.wait_ge(step, n)
                for j in range(HALVES):
                    last = V.max_index(idx[:, j // 2, j % 2, 8:16], val[:, j // 2, j % 2, 8:16], rest[:, j, :])
                last.then_inc(step, 1)
                V.tensor_tensor(cand[:], val[:, :, 0, :].unsqueeze(3).broadcast_to([P, PHEADS, TOPK, TOPK]),
                                val[:, :, 1, :].unsqueeze(2).broadcast_to([P, PHEADS, TOPK, TOPK]),
                                ALU.add).then_inc(step, 1)
                n += 2
                dve.wait_ge(step, n)
                V.tensor_copy(idxf[:], idx[:]).then_inc(step, 1)
                for h in range(PHEADS):
                    V.max(top[:, h, 0:8], cand[:, h].rearrange("p a b -> p (a b)")).then_inc(step, 1)
                n += PHEADS + 1
                dve.wait_ge(step, n)
                for h in range(PHEADS):
                    V.max_index(pos[:, h, 0:8], top[:, h, 0:8], cand[:, h].rearrange("p a b -> p (a b)"))
                    V.match_replace(crest[:, h], top[:, h, 0:8], cand[:, h].rearrange("p a b -> p (a b)"), -3.0e38).then_inc(step, 1)
                n += PHEADS
                dve.wait_ge(step, n)
                for h in range(PHEADS):
                    V.max(top[:, h, 8:16], crest[:, h]).then_inc(step, 1)
                n += PHEADS
                dve.wait_ge(step, n)
                for h in range(PHEADS):
                    V.max_index(pos[:, h, 8:16], top[:, h, 8:16], crest[:, h]).then_inc(step, 1)
                V.tensor_tensor(shifted[:], top[:], top[:, :, 0:1].broadcast_to([P, PHEADS, TOPK]),
                                ALU.subtract).then_inc(shifted_ready, 1)
                n += PHEADS
                dve.wait_ge(step, n)
                flat = pos[:].rearrange("p h k -> p (h k)")
                V.tensor_scalar(part[:, 0, :], flat, 4, None, ALU.logical_shift_right).then_inc(step, 1)
                V.tensor_scalar(part[:, 1, :], flat, TOPK - 1, None, ALU.bitwise_and).then_inc(step, 1)
                n += 2
                dve.wait_ge(step, n)
                V.tensor_copy(partf[:], part[:]).then_inc(step, 1)
                n += 1
                dve.wait_ge(step, n)
                if t >= 1:
                    dve.wait_ge(turned, t)
                for s in range(2):
                    V.tensor_tensor(picked[:, s].rearrange("p h k m -> p (h k) m"),
                                    C["iota"][:, 0:TOPK].unsqueeze(1).broadcast_to([P, PAIRS, TOPK]),
                                    partf[:, s, :].unsqueeze(2).broadcast_to([P, PAIRS, TOPK]),
                                    ALU.is_equal).then_inc(hit_ready, 1)
                dve.wait_ge(hit_ready, 2 * (t + 1))
                pick(V, 1).then_inc(step, 1)
                n += 1
                dve.wait_ge(step, n)
                for s in (1, 0):
                    if s == 0:
                        dve.wait_ge(rows_picked, t + 1)
                    V.tensor_reduce(chosen[:, s, :], picked[:, s].rearrange("p h k m -> p (h k) m"), AX.X,
                                    ALU.add).then_inc(step, 1)
                n += 2
                dve.wait_ge(step, n)
                dve.wait_ge(exp_done, t + 1)
                V.tensor_reduce(total[:], weight[:], AX.X, ALU.add).then_inc(step, 1)
                n += 1
                dve.wait_ge(step, n)
                V.reciprocal(rtotal[:], total[:]).then_inc(step, 1)
                n += 1
                dve.wait_ge(step, n)
                V.tensor_tensor(gate[:], weight[:], rtotal[:].unsqueeze(2).broadcast_to([P, PHEADS, TOPK]),
                                ALU.mult).then_inc(chosen_ready, 1)
                if modulation and t == 2:
                    modulation.take_gate(dve, 0)
            if modulation:
                modulation.take_gate(dve, 1)
                modulation.take_columns(dve)


def peer_gates(nc, tag, C, rows, gates):
    first, second, gate = rows
    TOK = 4
    RING = 4
    SQUARED = (1, 3)
    PIECES = SEQ // PIECE
    STEPS = PIECE // (TOK * RING)
    with ExitStack() as ctx:
        sb, ps, sem = phase_tools(nc, ctx, tag)
        hot1 = sb("hot1", [P, RING, TOK, KEYS])
        hot2 = sb("hot2", [P, RING, TOK, KEYS])
        away = sb("away", [P, RING, TOK, KEYS])
        out = sb("out", [P, 2, KEYS, PIECE])
        prod = ps("prod", [P, RING, TOK, KEYS])
        hot_ready, away_ready, hot_free, prod_free = (
            sem("hot_ready"), sem("away_ready"), sem("hot_free"), sem("prod_free"))
        dist2_ready, squared_hot_ready = sem("dist2_ready"), sem("squared_hot_ready")
        stored = [sem("stored0"), sem("stored1")]
        block = ctx.enter_context(nc.Block())

        @block.vector
        def _(dve):
            for t in range(PIECES):
                with dve.Fori(0, STEPS) as i:
                    for r in range(RING):
                        token = t * PIECE + i * (RING * TOK) + r * TOK
                        dve.wait_ge(hot_free, (t * STEPS + i) * RING + r + 1)
                        for q in range(TOK):
                            last = nc.vector.tensor_scalar(hot1[:, r, q, :], C["iota"][:, 0:KEYS],
                                                           first[:, bass.ds(token + q, 1)],
                                                           gate[:, bass.ds(token + q, 1)], ALU.is_equal, ALU.mult)
                        if r in SQUARED:
                            last.then_inc(hot_ready, 1)
                            continue
                        dve.wait_ge(away_ready, (t * STEPS + i) * RING + r + 1)
                        nc.vector.tensor_scalar(hot2[:, r], away[:, r], 0.0, None,
                                                ALU.is_equal).then_inc(hot_ready, 1)

        @block.gpsimd
        def _(pool):
            for t in range(PIECES):
                with pool.Fori(0, STEPS) as i:
                    for r in range(RING):
                        token = t * PIECE + i * (RING * TOK) + r * TOK
                        pool.wait_ge(hot_free, (t * STEPS + i) * RING + r + 1)
                        nc.gpsimd.tensor_tensor(
                            away[:, r], C["iota"][:, 0:KEYS].unsqueeze(1).broadcast_to([P, TOK, KEYS]),
                            second[:, bass.ds(token, TOK)].unsqueeze(2).broadcast_to([P, TOK, KEYS]),
                            ALU.subtract).then_inc(away_ready, 1)

        @block.tensor
        def _(pe):
            pe.sem_inc(hot_free, RING)
            for t in range(PIECES):
                with pe.Fori(0, STEPS) as i:
                    for r in range(RING):
                        pe.wait_ge(hot_ready, (t * STEPS + i) * RING + r + 1)
                        if r in SQUARED:
                            pe.wait_ge(squared_hot_ready, (t * STEPS + i) * len(SQUARED) + SQUARED.index(r) + 1)
                        pe.wait_ge(prod_free, (t * STEPS + i) * RING + r + 1)
                        for q in range(TOK):
                            last = nc.tensor.matmul(prod[:, r, q, :], hot2[:, r, q, :], hot1[:, r, q, :],
                                                    start=True, stop=True, skip_group_check=True)
                        last.then_inc(hot_free, 1)

        def square_hot(act, step, n):
            r, done = SQUARED[n], step * len(SQUARED) + n
            act.wait_ge(away_ready, step * RING + r + 1)
            nc.scalar.activation(away[:, r], away[:, r], ACT.Square).then_inc(dist2_ready, 1)
            act.wait_ge(dist2_ready, done + 1)
            nc.scalar.activation(hot2[:, r], away[:, r], ACT.Relu, bias=C["ones"][:, 0:1],
                                 scale=-1.0).then_inc(squared_hot_ready, 1)

        @block.scalar
        def _(act):
            act.sem_inc(prod_free, RING)
            for t in range(PIECES):
                if t >= 2:
                    act.wait_ge(stored[t % 2], 16 * (t // 2))
                with act.Fori(0, STEPS) as i:
                    for r in range(RING):
                        if r < len(SQUARED):
                            square_hot(act, t * STEPS + i, r)
                        act.wait_ge(hot_free, (t * STEPS + i) * RING + r + 1 + RING)
                        nc.scalar.copy(out[:, t % 2, :, bass.ds(i * (RING * TOK) + r * TOK, TOK)],
                                       prod[:, r].rearrange("p q k -> p k q")).then_inc(prod_free, 1)

        @block.sync
        def _(sp):
            for t in range(PIECES):
                sp.wait_ge(prod_free, RING + (t + 1) * STEPS * RING)
                sp.dma_start(gates[:, :, t].rearrange("n p g t -> p n g t"),
                             out[:, t % 2].rearrange("p (n g) t -> p n g t", g=EGROUP)).then_inc(stored[t % 2], 16)
            sp.wait_ge(stored[0], 16 * PIECES // 2)
            sp.wait_ge(stored[1], 16 * PIECES // 2)


def after(eng, sem, value):
    if not isinstance(value, int) or value > 0:
        eng.wait_ge(sem, value)


def peer_experts(nc, tag, hT, u_tab, v_tab, gates, acc):
    G, OUTS = EGROUP, TT * 2
    NG = KEYS // G
    with ExitStack() as ctx:
        sb, ps, sem = phase_tools(nc, ctx, tag)
        x_hi, x_lo = sb("x_hi", [P, DK, SEQ], F32R), sb("x_lo", [P, DK, SEQ], F32R)
        u = sb("u", [P, G, DK * P])
        u_hi, u_lo = sb("u_hi", [P, 2, DK * P], F32R), sb("u_lo", [P, 2, DK * P], F32R)
        v = sb("v", [P, G, D])
        v_hi, v_lo = sb("v_hi", [P, G, D], F32R), sb("v_lo", [P, G, D], F32R)
        g = sb("g", [P, SEQ // PIECE, G, PIECE])
        a = sb("a", [P, 2, SEQ])
        w = sb("w", [P, 2, SEQ])
        w_hi, w_lo = sb("w_hi", [P, 2, G, SEQ], F32R), sb("w_lo", [P, 2, G, SEQ], F32R)
        pre = ps("pre", [P, 2, BANK])
        out = ps("out", [P, 4, BANK])
        u_in = [sem(f"u_in{j}") for j in range(G)]
        v_in = [sem(f"v_in{j}") for j in range(G)]
        g_in = sem("g_in")
        x_hi_ready, x_ready, u_hi_ready, u_ready, v_hi_ready, v_ready = (
            sem(n) for n in ("x_hi_ready", "x_ready", "u_hi_ready", "u_ready", "v_hi_ready", "v_ready"))
        pre_ready, gelu_done, w_made, w_hi_ready, w_ready, out_ready, summed = (
            sem(n) for n in ("pre_ready", "gelu_done", "w_made", "w_hi_ready", "w_ready", "out_ready", "summed"))
        block = ctx.enter_context(nc.Block())
        V = nc.vector

        def pieces(x):
            return x.rearrange("p (m t) -> p m t", t=PIECE)

        def for_groups(eng, body):
            body(0, 0, first=True, last=False)
            with eng.Fori(0, (NG - 2) // 2) as i:
                body(2 * i + 1, 1, first=False, last=False)
                body(2 * i + 2, 0, first=False, last=False)
            body(NG - 1, 1, first=False, last=True)

        @block.sync
        def _(sp):
            def fixed(x):
                return x if isinstance(x, int) else sp.snap(x)

            def loads(gr, _, first, last):
                tiles = [fixed(gr * G + j) for j in range(G)]
                used = [fixed((gr - 1) * G + j + 1) for j in range(G)]
                for j in range(G):
                    after(sp, u_ready, used[j])
                    sp.dma_start(u[:, j], u_tab[bass.ds(tiles[j], 1)].rearrange("o p k e -> (o p) (k e)")
                                 ).then_inc(u_in[j], 16)
                group = fixed(gr)
                after(sp, w_made, used[G - 1])
                sp.dma_start(g[:], gates[bass.ds(group, 1)].rearrange("o p m g t -> (o p) m g t")).then_inc(g_in, 16)
                for j in range(G):
                    after(sp, v_ready, used[j])
                    sp.dma_start(v[:, j], v_tab[bass.ds(tiles[j], 1)].rearrange("o p d -> (o p) d")
                                 ).then_inc(v_in[j], 16)
            for_groups(sp, loads)

        @block.tensor
        def _(pe):
            def activations(gr, j):
                n = gr * G + j
                pe.wait_ge(u_ready, n + 1)
                after(pe, gelu_done, n - 1)
                q, passes = j % 2, 3 * DK
                m = 0
                for k in range(DK):
                    for lhs, rhs in ((u_hi, x_hi), (u_hi, x_lo), (u_lo, x_hi)):
                        last = nc.tensor.matmul(pre[:, q, :], lhs[:, q, k * P:(k + 1) * P], rhs[:, k, :],
                                                start=(m == 0), stop=(m == passes - 1))
                        m += 1
                last.then_inc(pre_ready, 1)

            def values(gr, par):
                pe.wait_ge(w_ready, gr * G + G)
                pe.wait_ge(v_ready, gr * G + G)
                for o in range(OUTS):
                    t, cols = o // 2, slice(o % 2 * BANK, (o % 2 + 1) * BANK)
                    pe.wait_ge(summed, gr * OUTS + o + 1)
                    m = 0
                    for j in range(G):
                        for lhs, rhs in ((w_hi, v_hi), (w_hi, v_lo), (w_lo, v_hi)):
                            last = nc.tensor.matmul(out[:, o % 4, :], lhs[:, par, j, t * P:(t + 1) * P],
                                                    rhs[:, j, cols], start=(m == 0), stop=(m == 3 * G - 1))
                            m += 1
                    last.then_inc(out_ready, 1)

            def body(gr, par, first, last):
                activations(gr, 0)
                if not first:
                    values(gr - 1, 1 - par)
                for j in range(1, G):
                    activations(gr, j)
                if last:
                    values(gr, par)
            pe.wait_ge(x_ready, DK)
            for_groups(pe, body)

        @block.scalar
        def _(act):
            for k in range(DK):
                nc.scalar.copy(x_hi[:, k, :], hT[:, k, :]).then_inc(x_hi_ready, 1)

            def split_u(gr, j):
                act.wait_ge(u_in[j], gr * 16 + 16)
                after(act, pre_ready, gr * G + j - 1)
                nc.scalar.copy(u_hi[:, j % 2, :], u[:, j, :]).then_inc(u_hi_ready, 1)

            def split_v(gr, j):
                act.wait_ge(v_in[j], gr * 16 + 16)
                after(act, out_ready, gr * OUTS)
                nc.scalar.copy(v_hi[:, j, :], v[:, j, :]).then_inc(v_hi_ready, 1)

            def body(gr, par, first, last):
                for j in range(G):
                    n = gr * G + j
                    act.wait_ge(pre_ready, n + 1)
                    after(act, w_made, n - 1)
                    nc.scalar.activation(a[:, j % 2, :], pre[:, j % 2, :], ACT.Gelu).then_inc(gelu_done, 1)
                    if j + 2 < G:
                        split_u(gr, j + 2)
                    elif not last:
                        split_u(gr + 1, j + 2 - G)
                    if j == 1:
                        split_v(gr, 0)
                    if j >= 1:
                        split_v(gr, j)
            split_u(0, 0)
            split_u(0, 1)
            for_groups(act, body)

        @block.vector
        def _(dve):
            dve.sem_inc(summed, 4)
            for k in range(DK):
                dve.wait_ge(x_hi_ready, k + 1)
                V.tensor_tensor(x_lo[:, k, :], hT[:, k, :], x_hi[:, k, :], ALU.subtract).then_inc(x_ready, 1)

            def split_u(gr, j):
                dve.wait_ge(u_hi_ready, gr * G + j + 1)
                V.tensor_tensor(u_lo[:, j % 2, :], u[:, j, :], u_hi[:, j % 2, :], ALU.subtract).then_inc(u_ready, 1)

            def split_v(gr, j):
                dve.wait_ge(v_hi_ready, gr * G + j + 1)
                V.tensor_tensor(v_lo[:, j, :], v[:, j, :], v_hi[:, j, :], ALU.subtract).then_inc(v_ready, 1)

            def add_outputs(gr):
                for o in range(OUTS):
                    dve.wait_ge(out_ready, gr * OUTS + o + 1)
                    part = acc[:, o // 2, o % 2 * BANK:(o % 2 + 1) * BANK]
                    V.tensor_tensor(part, part, out[:, o % 4, :], ALU.add).then_inc(summed, 1)

            def body(gr, par, first, last):
                for j in range(G):
                    n, q = gr * G + j, j % 2
                    dve.wait_ge(gelu_done, n + 1)
                    dve.wait_ge(g_in, gr * 16 + 16)
                    after(dve, w_ready, n - 1)
                    V.tensor_tensor(pieces(w[:, q, :]), pieces(a[:, q, :]), g[:, :, j, :], ALU.mult).then_inc(w_made, 1)
                    dve.wait_ge(w_made, n + 1)
                    V.tensor_copy(w_hi[:, par, j, :], w[:, q, :]).then_inc(w_hi_ready, 1)
                    dve.wait_ge(w_hi_ready, n + 1)
                    V.tensor_tensor(w_lo[:, par, j, :], w[:, q, :], w_hi[:, par, j, :],
                                    ALU.subtract).then_inc(w_ready, 1)
                    if j + 2 < G:
                        split_u(gr, j + 2)
                    elif not last:
                        split_u(gr + 1, j + 2 - G)
                    if j == 0 and not first:
                        add_outputs(gr - 1)
                    if j == 1:
                        split_v(gr, 0)
                    if j >= 1:
                        split_v(gr, j)
                if last:
                    add_outputs(gr)
            split_u(0, 0)
            split_u(0, 1)
            for_groups(dve, body)


def sincos_reduced(V, chain, ang, turns, red):
    chain.add(V.tensor_scalar(turns, ang, 1.0 / TWO_PI, ROUND, ALU.mult, ALU.add))
    chain.wait()
    chain.add(V.tensor_scalar(turns, turns, -ROUND, None, ALU.add))
    chain.wait()
    chain.add(V.scalar_tensor_tensor(red, turns, -TWO_PI_A, ang, ALU.mult, ALU.add))
    chain.wait()
    chain.add(V.scalar_tensor_tensor(red, turns, -TWO_PI_B, red, ALU.mult, ALU.add))
    chain.wait()
    chain.add(V.scalar_tensor_tensor(red, turns, -TWO_PI_C, red, ALU.mult, ALU.add))
    chain.wait()
    chain.add(V.tensor_scalar(red, red, float(np.float32(3.1415925)), float(np.float32(-3.1415925)), ALU.min,
                              ALU.max))
    chain.wait()


def ssm(nc, tag, C, uT, bc, lam, dcol, wglu, bglu, pre, ssm_out):
    with ExitStack() as outer:
        sbo, _, _ = phase_tools(nc, outer, tag)
        y = sbo("y", [P, 4, SEQ])
        with ExitStack() as ctx:
            sb, ps, sem = phase_tools(nc, ctx, tag)
            cosT = sb("cosT", [P, STILES, SEQ])
            sinT = sb("sinT", [P, STILES, SEQ])
            mag = sb("mag", [P, STILES])
            BT = sb("BT", [P, 4, 2, P])
            CB = sb("CB", [P, 2, STILES, 32])
            ssm_tables(nc, tag + "t", C, bc, lam, cosT, sinT, mag, BT, CB)
            ssm_scan(nc, tag + "s", uT, dcol, cosT, sinT, mag, BT, CB, pre, y)
        ssm_glu(nc, tag + "g", y, wglu, bglu, ssm_out)


def ssm_tables(nc, tag, C, bc, lam, cosT, sinT, mag, BT, CB):
    with ExitStack() as ctx:
        sb, ps, sem = phase_tools(nc, ctx, tag)
        raw = sb("raw", [P, 4, STILES, GROUP])
        small = sb("small", [P, 24, STILES])
        bb = sb("bb", [P, 2, STILES, 32])
        prod = sb("prod", [P, 4, STILES, GROUP])
        tmp = sb("tmp", [P, 4, STILES, SEQ // 8])
        tp = ps("tp", [P, 2, BANK])
        bc_in, v, a, zeroed, turned, ready = sem("bc_in"), sem("v"), sem("a"), sem("zeroed"), sem("turned"), sem("ready")
        block = ctx.enter_context(nc.Block())
        (step, lrs, ang, turns, red, half, s_half, sn, cs, sq, ar, ai, zr, t1, t2, t3, t4, den, rden, fr, fi,
         pc, psn, t5) = [small[:, n, :] for n in range(24)]
        lr, li, logstep = (lam[:, n, :] for n in range(3))

        @block.sync
        def _(sp):
            sp.dma_start(raw[:], bc.rearrange("w p t c -> p w t c")).then_inc(bc_in, 16)

        @block.gpsimd
        def _(pool):
            pool.memset(bb[:], 0.0).then_inc(zeroed, 1)
            pool.memset(CB[:], 0.0).then_inc(zeroed, 1)

        @block.scalar
        def _(act):
            nc.scalar.activation(step, logstep, ACT.Exp).then_inc(a, 1)
            act.wait_ge(ready, 1)
            nc.scalar.activation(mag[:], lrs, ACT.Exp).then_inc(a, 1)
            nc.scalar.activation(sn, red, ACT.Sin).then_inc(a, 1)
            nc.scalar.activation(s_half, half, ACT.Sin).then_inc(a, 1)

        @block.tensor
        def _(pe):
            pe.wait_ge(ready, 2)
            for ri in range(2):
                for kk in range(4):
                    last = nc.tensor.transpose(tp[:, ri, kk * P:(kk + 1) * P],
                                               bb[:, ri, 4 * kk:4 * kk + 4, :].rearrange("p j c -> p (j c)"),
                                               C["ident"][:])
                last.then_inc(turned, 1)

        @block.vector
        def _(dve):
            V = nc.vector
            ch = Chain(dve, v)
            dve.wait_ge(a, 1)
            ch.add(V.tensor_tensor(lrs, lr, step, ALU.mult))
            ch.add(V.tensor_tensor(ang, li, step, ALU.mult))
            ch.wait()
            sincos_reduced(V, ch, ang, turns, red)
            ch.add(V.tensor_scalar(half, red, 0.5, None, ALU.mult))
            ch.wait()
            V.engine_nop().then_inc(ready, 1)
            dve.wait_ge(a, 4)
            ch.add(V.tensor_tensor(sq, s_half, s_half, ALU.mult))
            ch.wait()
            ch.add(V.tensor_scalar(cs, sq, -2.0, 1.0, ALU.mult, ALU.add))
            ch.wait()
            ch.add(V.tensor_tensor(ar, mag[:], cs, ALU.mult))
            ch.add(V.tensor_tensor(ai, mag[:], sn, ALU.mult))
            ch.add(V.tensor_tensor(t1, lr, lr, ALU.mult))
            ch.add(V.tensor_tensor(t2, li, li, ALU.mult))
            ch.wait()
            ch.add(V.tensor_scalar(zr, ar, -1.0, None, ALU.add))
            ch.add(V.tensor_tensor(den, t1, t2, ALU.add))
            ch.wait()
            ch.add(V.reciprocal(rden, den))
            ch.add(V.tensor_tensor(t1, zr, lr, ALU.mult))
            ch.add(V.tensor_tensor(t2, ai, li, ALU.mult))
            ch.add(V.tensor_tensor(t3, ai, lr, ALU.mult))
            ch.add(V.tensor_tensor(t4, zr, li, ALU.mult))
            ch.wait()
            ch.add(V.tensor_tensor(t1, t1, t2, ALU.add))
            ch.add(V.tensor_tensor(t3, t3, t4, ALU.subtract))
            ch.wait()
            ch.add(V.tensor_tensor(fr, t1, rden, ALU.mult))
            ch.add(V.tensor_tensor(fi, t3, rden, ALU.mult))
            ch.wait()
            dve.wait_ge(bc_in, 16)
            dve.wait_ge(zeroed, 2)
            wide = lambda x: x.unsqueeze(2).broadcast_to([P, STILES, GROUP])
            for n, (f, b) in enumerate(((fr, 0), (fi, 1), (fr, 1), (fi, 0))):
                ch.add(V.tensor_tensor(prod[:, n], wide(f), raw[:, b], ALU.mult))
            ch.wait()
            for half_ in range(2):
                rows, cols = slice(64 * half_, 64 * half_ + 64), slice(16 * half_, 16 * half_ + 16)
                ch.add(V.tensor_tensor(bb[rows, 0, :, cols], prod[rows, 0], prod[rows, 1], ALU.subtract))
                ch.add(V.tensor_tensor(bb[rows, 1, :, cols], prod[rows, 2], prod[rows, 3], ALU.add))
                ch.add(V.tensor_copy(CB[rows, 0, :, cols], raw[rows, 2]))
                ch.add(V.tensor_scalar(CB[rows, 1, :, cols], raw[rows, 3], -1.0, None, ALU.mult))
            ch.wait()
            V.engine_nop().then_inc(ready, 1)
            ch.add(V.memset(cosT[:, :, 0:1], 1.0))
            ch.add(V.memset(sinT[:, :, 0:1], 0.0))
            ch.add(V.tensor_copy(pc, cs))
            ch.add(V.tensor_copy(psn, sn))
            ch.wait()
            n = 1
            while n < SEQ:
                for c0 in range(0, n, SEQ // 8):
                    m = min(n, SEQ // 8)
                    a_c, a_s = cosT[:, :, c0:c0 + m], sinT[:, :, c0:c0 + m]
                    bcast = lambda x: x.unsqueeze(2).broadcast_to([P, STILES, m])
                    for q, (x, f) in enumerate(((a_c, pc), (a_s, psn), (a_c, psn), (a_s, pc))):
                        ch.add(V.tensor_tensor(tmp[:, q, :, 0:m], x, bcast(f), ALU.mult))
                    ch.wait()
                    ch.add(V.tensor_tensor(cosT[:, :, n + c0:n + c0 + m], tmp[:, 0, :, 0:m], tmp[:, 1, :, 0:m],
                                           ALU.subtract))
                    ch.add(V.tensor_tensor(sinT[:, :, n + c0:n + c0 + m], tmp[:, 2, :, 0:m], tmp[:, 3, :, 0:m],
                                           ALU.add))
                    ch.wait()
                ch.add(V.tensor_tensor(t1, pc, pc, ALU.mult))
                ch.add(V.tensor_tensor(t2, psn, psn, ALU.mult))
                ch.add(V.tensor_tensor(t3, pc, psn, ALU.mult))
                ch.wait()
                ch.add(V.tensor_tensor(pc, t1, t2, ALU.subtract))
                ch.add(V.tensor_scalar(psn, t3, 2.0, None, ALU.mult))
                ch.wait()
                n *= 2
            dve.wait_ge(turned, 2)
            for ri in range(2):
                ch.add(V.tensor_copy(BT[:, :, ri, :], tp[:, ri, :].rearrange("p (k s) -> p k s", k=4)))


def ssm_scan(nc, tag, uT, dcol, cosT, sinT, mag, BT, CB, pre, y):
    with ExitStack() as ctx:
        sb, ps, sem = phase_tools(nc, ctx, tag)
        R = 2
        m = sb("m", [P, R, 4, SEQ])
        b = sb("b", [P, R, 2, SEQ])
        z = sb("z", [P, R, 2, SEQ])
        q = sb("q", [P, R, 4, SEQ])
        x = sb("x", [P, R, 2, SEQ])
        bu = ps("bu", [P, R, 2, BANK])
        yp = ps("yp", [P, 4, BANK])
        fed, turned_in, v, z_ready, back, x_re_ready, x_im_ready, y_ready, pre_ready = (
            sem(n) for n in ("fed", "turned_in", "v", "z_ready", "back", "x_re_ready", "x_im_ready", "y_ready",
                             "pre_ready"))
        block = ctx.enter_context(nc.Block())
        V, G = nc.vector, nc.gpsimd

        @block.tensor
        def _(pe):
            def feed(n):
                kk, j = n // 4, n % 4
                rows = slice(32 * j, 32 * j + 32)
                if n >= R:
                    pe.wait_ge(turned_in, n - R + 1)
                for ri in range(2):
                    last = nc.tensor.matmul(bu[:, n % R, ri, :], BT[rows, kk, ri, :], uT[rows, kk, :], start=True,
                                            stop=True, tile_position=(32 * j, 0))
                last.then_inc(fed, 1)

            for n in range(R):
                feed(n)
            for n in range(STILES):
                if n + R < STILES:
                    feed(n + R)
                kk, j = n // 4, n % 4
                rows = slice(32 * j, 32 * j + 32)
                pe.wait_ge(x_re_ready, n + 1)
                pe.wait_ge(x_im_ready, n + 1)
                for ri in range(2):
                    last = nc.tensor.matmul(yp[rows, kk, :], CB[:, ri, n, :], x[:, n % R, ri, :], start=(ri == 0),
                                            stop=(ri == 1), skip_group_check=True)
                last.then_inc(y_ready, 1)

        def imaginary(dve, n):
            dve.wait_ge(back, 4 * (n + 1))
            if n >= R:
                dve.wait_ge(y_ready, n - R + 1)
            V.tensor_tensor(x[:, n % R, 1, :], q[:, n % R, 2, :], q[:, n % R, 3, :], ALU.add).then_inc(x_im_ready, 1)

        def skip(dve, kk):
            dve.wait_ge(y_ready, 4 * (kk + 1))
            V.scalar_tensor_tensor(pre[:, kk, :], uT[:, kk, :], dcol(kk), yp[:, kk, :], ALU.mult,
                                   ALU.add).then_inc(pre_ready, 1)

        @block.vector
        def _(dve):
            ch = Chain(dve, v)
            for n in range(STILES):
                c, s = cosT[:, n, :], sinT[:, n, :]
                dve.wait_ge(fed, n + 1)
                for i, (part, f) in enumerate(((0, c), (1, s), (1, c), (0, s))):
                    ch.add(V.tensor_tensor(m[:, n % R, i, :], bu[:, n % R, part, :], f, ALU.mult))
                ch.wait()
                ch.add(V.tensor_tensor(b[:, n % R, 0, :], m[:, n % R, 0, :], m[:, n % R, 1, :], ALU.add))
                V.tensor_tensor(b[:, n % R, 1, :], m[:, n % R, 2, :], m[:, n % R, 3, :],
                                ALU.subtract).then_inc(turned_in, 1)
                ch.wait()
                dve.wait_ge(turned_in, n + 1)
                if n >= R:
                    dve.wait_ge(back, 4 * (n - R + 1))
                r = mag[:, n:n + 1].broadcast_to([P, SEQ])
                for ri in range(2):
                    V.tensor_tensor_scan(z[:, n % R, ri, :], r, b[:, n % R, ri, :], 0.0, ALU.mult,
                                         ALU.add).then_inc(z_ready, 1)
                if n >= 1:
                    imaginary(dve, n - 1)
                if n % 4 == 3 and n >= 7:
                    skip(dve, n // 4 - 1)
            imaginary(dve, STILES - 1)
            skip(dve, 3)

        @block.gpsimd
        def _(pool):
            for n in range(STILES):
                c, s = cosT[:, n, :], sinT[:, n, :]
                pool.wait_ge(z_ready, 2 * (n + 1))
                if n >= R:
                    pool.wait_ge(x_im_ready, n - R + 1)
                for i, (part, f) in enumerate(((0, c), (1, s), (1, c), (0, s))):
                    G.tensor_tensor(q[:, n % R, i, :], z[:, n % R, part, :], f, ALU.mult).then_inc(back, 1)
                pool.wait_ge(back, 4 * (n + 1))
                if n >= R:
                    pool.wait_ge(y_ready, n - R + 1)
                G.tensor_tensor(x[:, n % R, 0, :], q[:, n % R, 0, :], q[:, n % R, 1, :],
                                ALU.subtract).then_inc(x_re_ready, 1)

        @block.scalar
        def _(act):
            for kk in range(4):
                act.wait_ge(pre_ready, kk + 1)
                nc.scalar.activation(y[:, kk, :], pre[:, kk, :], ACT.Gelu)


def ssm_glu(nc, tag, y, wglu, bglu, ssm_out):
    with ExitStack() as ctx:
        sb, ps, sem = phase_tools(nc, ctx, tag)
        w = sb("w", [P, 4, 4, P])
        sig = sb("sig", [P, 4, SEQ])
        z = ps("z", [P, 4, BANK])
        w_in, multiplied, sig_ready = sem("w_in"), sem("multiplied"), sem("sig_ready")
        block = ctx.enter_context(nc.Block())

        @block.sync
        def _(sp):
            sp.dma_start(w[:], wglu.rearrange("j p k n -> p j k n")).then_inc(w_in, 16)

        @block.tensor
        def _(pe):
            pe.wait_ge(w_in, 16)
            for j in range(4):
                for k in range(4):
                    last = nc.tensor.matmul(z[:, j, :], w[:, j, k, :], y[:, k, :], start=(k == 0), stop=(k == 3))
                last.then_inc(multiplied, 1)

        @block.scalar
        def _(act):
            for j in range(4):
                act.wait_ge(multiplied, j + 1)
                nc.scalar.activation(sig[:, j, :], z[:, j, :], ACT.Sigmoid, bias=bglu(j)).then_inc(sig_ready, 1)

        @block.vector
        def _(dve):
            for j in range(4):
                dve.wait_ge(sig_ready, j + 1)
                nc.vector.tensor_tensor(ssm_out[:, j, :], y[:, j, :], sig[:, j, :], ALU.mult)


COLS, ROWS = {}, {}
_n = 0
for _name, _width in (("norm_mix_g", 8), ("att_q_g", 1), ("att_k_g", 1), ("att_out_g", 4), ("ssm_out_g", 4),
                      ("norm_mem_g", 8), ("norm_memkv_g", 8), ("mem_q_g", 2), ("mem_k_g", 2),
                      ("norm_peer_g", 8), ("ssm_d", 4), ("ssm_b_glu", 4), ("lam", 48), ("norm1_g", 8),
                      ("norm2_g", 8), ("b_gate", 16), ("b_ada", 48), ("subln_g", 1), ("c", 8)):
    COLS[_name] = (_n, _width)
    _n += _width
NCOLS = _n
_n = 0
for _name, _width in (("gains", 2 * DIL_W + 2 * DIFF_W), ("inv_freq", HEAD // 2), ("lambdas", 4 * HEAD)):
    ROWS[_name] = (_n, _width)
    _n += _width
NROWS = _n
QK2 = 2 * DIL_W + 2 * DIFF_W
QK2_TILES = QK2 // P
MODS = 4


def constants(nc, ctx, cols_dram):
    ident = ctx.enter_context(nc.sbuf_tensor("ident", [P, P], F32))
    ones = ctx.enter_context(nc.sbuf_tensor("ones", [P, P], F32))
    iota = ctx.enter_context(nc.sbuf_tensor("iota", [P, P], F32))
    cols = ctx.enter_context(nc.sbuf_tensor("cols", [P, NCOLS], F32))
    with ExitStack() as c:
        _, _, sem = phase_tools(nc, c, "const")
        zeroed, cols_in = sem("zeroed"), sem("cols_in")
        block = c.enter_context(nc.Block())

        @block.gpsimd
        def _(pool):
            pool.memset(ident[:], 0.0).then_inc(zeroed, 1)
            pool.memset(ones[:], 1.0)
            pool.iota(iota[:], pattern=[[1, P]], base=0, channel_multiplier=0,
                      allow_small_or_imprecise_dtypes=True)
            pool.wait_ge(zeroed, 1)
            pool.affine_select(out=ident[:], in_=ident[:], compare_op=ALU.not_equal, fill=1.0, base=0,
                               pattern=[[-1, P]], channel_multiplier=1)

        @block.sync
        def _(sp):
            sp.dma_start(cols[:], cols_dram).then_inc(cols_in, 16)
            sp.wait_ge(cols_in, 16)
    return {"ident": ident, "ones": ones, "iota": iota, "cols": cols}


def column(C, name, n=None):
    a, width = COLS[name]
    return lambda k: C["cols"][:, a + k % width:a + k % width + 1]


def load(nc, tag, pairs):
    with ExitStack() as c:
        _, _, sem = phase_tools(nc, c, tag)
        arrived = [sem(f"in{n}") for n in range(len(pairs))]
        block = c.enter_context(nc.Block())

        @block.sync
        def _(sp):
            for n, (dst, src) in enumerate(pairs):
                sp.dma_start(dst, src).then_inc(arrived[n], 16)
            for n in range(len(pairs)):
                sp.wait_ge(arrived[n], 16)


def block1(nc, C, h, hT, A, modulation):
    with ExitStack() as mid:
        sb, _, _ = phase_tools(nc, mid, "b1")
        mixT = sb("mixT", [P, 8, SEQ])
        uT = sb("uT", [P, 4, SEQ])
        with ExitStack() as att:
            sba, _, _ = phase_tools(nc, att, "b1a")
            qk = sba("qk", [P, TT, 2 * ATT_W])
            v = sba("v", [P, TT, ATT_W])
            norm_transpose(nc, "n0", C, h, TT, D, hT, column(C, "norm_mix_g"))
            chunks = [(A["w_in"][c], True, columns_to(nc, qk, c * BANK, BANK, TT)) for c in range(2)]
            chunks.append((A["w_in"][2], True, columns_to(nc, v, 0, BANK, TT)))
            chunks.append((A["w_in"][3], False, [copy_to(nc, j, uT[:, j, :]) for j in range(4)]))
            product(nc, "w1", hT, DK, SEQ, chunks)
            qkT = sba("qkT", [P, 8, SEQ])
            heads_norm_transpose(nc, "hn1", C, qk, TT, 2 * HEADS, HEAD, qkT,
                                 lambda k: column(C, "att_q_g" if k < 4 else "att_k_g")(0))
            chunk_attention(nc, C, qkT, v, A["bias"], mixT)
        feature_norm(nc, "fn1", C, mixT, 4, mixT, column(C, "att_out_g"))
        a = COLS["lam"][0]
        lam = C["cols"][:, a:a + 48].rearrange("p (w t) -> p w t", w=3)
        ssm(nc, "ssm", C, uT, A["ssm_bc"], lam, column(C, "ssm_d"), A["w_glu"], column(C, "ssm_b_glu"),
            hT[:, 0:4], mixT[:, 4:8])
        feature_norm(nc, "fn2", C, mixT[:, 4:8], 4, mixT[:, 4:8], column(C, "ssm_out_g"))
        add_product(nc, "wo1", mixT, A["w_out"], h)
    norm_transpose(nc, "n1", C, h, TT, D, hT, column(C, "norm_mem_g"))
    memory_attention(nc, C, h, hT, A)
    norm_transpose(nc, "n2", C, h, TT, D, hT, column(C, "norm_peer_g"))
    peer(nc, "p1", C, h, hT, A["w_peer_q"], A["peer_keys"], A["peer_u"], A["peer_v"], A["gates"], h,
         modulation)


def add_product(nc, tag, srcT, w, h):
    def add(dst):
        return ON_DVE, lambda psum: [lambda: nc.vector.tensor_tensor(dst, dst, psum, ALU.add)]
    product(nc, tag, srcT, DK, SEQ,
            [(w[half], True, [add(h[:, t, half * BANK:(half + 1) * BANK]) for t in range(TT)]) for half in range(2)])


def chunk_attention(nc, C, qkT, v, bias_dram, outT):
    with ExitStack() as ctx:
        sb, _, _ = phase_tools(nc, ctx, "ca")
        bias = sb("bias", [P, 2, SEQ])
        items, outs = [], []
        for hd in range(HEADS):
            rows = slice(64 * (hd % 2), 64 * (hd % 2) + 64)
            for qt in range(TT):
                n = (qt + 1) * P
                q = qkT[rows, hd // 2, qt * P:(qt + 1) * P]
                items.append(dict(
                    scores=[(0, n, [(q, qkT[rows, 4 + hd // 2, 0:n])])], width=n,
                    bias=bias[:, hd % 2, SEQ - n:SEQ], bias_load=hd,
                    values=[(hd, rows, slice(qt * P, (qt + 1) * P),
                             [(kt, v[:, kt, hd * HEAD:(hd + 1) * HEAD]) for kt in range(qt + 1)])]))
            outs.append((rows, outT[rows, hd // 2, :], TT * hd + TT - 1))
        loads = [(bias[:, hd % 2, :], bias_dram[hd], None if hd < 2 else TT * (hd - 2) + TT - 1)
                 for hd in range(HEADS)]

        def mask(hd):
            return nc.gpsimd.memset(bias[0:CHUNK, hd % 2, SEQ - CHUNK:SEQ], MASKED)
        attention(nc, "ca", C, items, outs, SEQ, HEAD ** -0.5, bias_loads=loads, bias_prepare=mask)


def memory_attention(nc, C, h, hT, A):
    MT = MEM_LEN // P
    with ExitStack() as ctx:
        sb, _, _ = phase_tools(nc, ctx, "ma")
        oT = sb("oT", [P, DK, SEQ])
        qT = sb("qT", [P, DK, SEQ])
        kT = sb("kT", [P, DK, MEM_LEN])
        v = sb("v", [P, MT, D])
        with ExitStack() as ctx2:
            sb2, _, _ = phase_tools(nc, ctx2, "mb")
            q = sb2("q", [P, TT, D])
            k = sb2("k", [P, MT, D])
            mem = sb2("mem", [P, MT, D])
            memT = sb2("memT", [P, DK, MEM_LEN])
            load(nc, "mem", [(mem[:], A["mem"].rearrange("(t p) d -> p t d", p=P))])
            norm_transpose(nc, "nm", C, mem, MT, D, memT, column(C, "norm_memkv_g"))
            product(nc, "wmq", hT, DK, SEQ,
                    [(A["w_mem_q"][n], True, columns_to(nc, q, n * BANK, BANK, TT)) for n in range(2)])
            product(nc, "wmkv", memT, DK, MEM_LEN,
                    [(A[name][n], True, columns_to(nc, dst, n * BANK, BANK, MT))
                     for name, dst in (("w_mem_k", k), ("w_mem_v", v)) for n in range(2)])
            heads_norm_transpose(nc, "hnq", C, q, TT, MEM_HEADS, MEM_HEAD, qT, column(C, "mem_q_g"))
            heads_norm_transpose(nc, "hnk", C, k, MT, MEM_HEADS, MEM_HEAD, kT, column(C, "mem_k_g"))
        items, outs = [], []
        for hd in range(MEM_HEADS):
            for qt in range(TT):
                cols = slice(qt * P, (qt + 1) * P)
                items.append(dict(
                    scores=[(0, MEM_LEN, [(qT[:, 2 * hd + f, cols], kT[:, 2 * hd + f, :]) for f in range(2)])],
                    width=MEM_LEN, bias=None,
                    values=[(2 * hd + f, slice(0, P), cols,
                             [(kt, v[:, kt, (2 * hd + f) * P:(2 * hd + f + 1) * P]) for kt in range(MT)])
                            for f in range(2)]))
            for f in range(2):
                outs.append((slice(0, P), oT[:, 2 * hd + f, :], TT * hd + TT - 1))
        attention(nc, "mat", C, items, outs, MEM_LEN, MEM_HEAD ** -0.5, out_ring=4)
        add_product(nc, "wmo", oT, A["w_mem_o"], h)


class Modulation:
    CHUNKS = 12
    SLOTS = 3
    PER_FEATURE = {0: 0, 1: 1, 3: 2, 4: 3}
    GATE_CHUNKS = {4: 0, 5: 1, 10: 0, 11: 1}

    def __init__(self, nc, C, A, mods, g1, g2):
        self.nc, self.C, self.A, self.mods, self.g1, self.g2 = nc, C, A, mods, g1, g2

    def place(self, ctx):
        sb, ps, sem = phase_tools(self.nc, ctx, "ad")
        self.cs = sb("cs", [P, DK])
        self.csb = sb("csb", [P, DK, P])
        self.w = sb("w", [P, self.SLOTS, DK, BANK])
        self.brow = sb("brow", [P, 2, D])
        self.colp = ps("colp", [P, BANK])
        self.rowp = ps("rowp", [P, 2, BANK])
        self.loaded = [sem(f"loaded{s}") for s in range(self.SLOTS)]
        self.silu_done, self.spread, self.multiplied, self.rows_in, self.gate_copied = (
            sem(n) for n in ("silu", "spread", "multiplied", "rows_in", "gate_copied"))

    def load(self, sp):
        sp.dma_start(self.brow[:], self.A["ada_rows"].partition_broadcast(P)).then_inc(self.rows_in, 16)
        for c in range(self.CHUNKS):
            if c >= self.SLOTS:
                sp.wait_ge(self.multiplied, c - self.SLOTS + 1)
            sp.dma_start(self.w[:, c % self.SLOTS], self.A["w_ada"][c]).then_inc(self.loaded[c % self.SLOTS], 16)

    def silu(self, act):
        a = COLS["c"][0]
        self.nc.scalar.activation(self.cs[:], self.C["cols"][:, a:a + DK], ACT.Silu).then_inc(self.silu_done, 1)

    def widen(self, dve):
        dve.wait_ge(self.silu_done, 1)
        self.nc.vector.tensor_copy(self.csb[:], self.cs[:].unsqueeze(2).broadcast_to([P, DK, P])).then_inc(self.spread, 1)

    def multiply(self, pe, c):
        nc, slot = self.nc, c % self.SLOTS
        if c == 0:
            pe.wait_ge(self.spread, 1)
        if c >= 10:
            pe.wait_ge(self.gate_copied, c - 9)
        pe.wait_ge(self.loaded[slot], 16 * (c // self.SLOTS + 1))
        if c not in self.GATE_CHUNKS:
            for f in range(4):
                col = self.PER_FEATURE[c // 2] * 8 + (c % 2) * 4 + f
                for k in range(DK):
                    last = nc.tensor.matmul(self.colp[:, col:col + 1], self.w[:, slot, k, f * P:(f + 1) * P],
                                            self.cs[:, k:k + 1], start=(k == 0), stop=(k == DK - 1),
                                            skip_group_check=True)
        else:
            for k in range(DK):
                last = nc.tensor.matmul(self.rowp[:, self.GATE_CHUNKS[c], :], self.csb[:, k, :],
                                        self.w[:, slot, k, :], start=(k == 0), stop=(k == DK - 1))
        last.then_inc(self.multiplied, 1)

    def take_gate(self, dve, n):
        dst, chunks = ((self.g1, (4, 5)), (self.g2, (10, 11)))[n]
        dve.wait_ge(self.rows_in, 16)
        for half, c in enumerate(chunks):
            dve.wait_ge(self.multiplied, c + 1)
            cols = slice(half * BANK, (half + 1) * BANK)
            self.nc.vector.tensor_tensor(dst[:, cols], self.rowp[:, half, :], self.brow[:, n, cols],
                                         ALU.add).then_inc(self.gate_copied, 1)

    def take_columns(self, dve):
        ab = COLS["b_ada"][0]
        for src, m in self.PER_FEATURE.items():
            self.nc.vector.tensor_tensor(self.mods[:, m, :], self.colp[:, m * 8:(m + 1) * 8],
                                         self.C["cols"][:, ab + 8 * src:ab + 8 * src + 8], ALU.add)


def rope_tables(nc, C, A, cosb, sinb, rows, lam_neg):
    with ExitStack() as ctx:
        sb, ps, sem = phase_tools(nc, ctx, "rt")
        posi = sb("posi", [P, TT], I32)
        posf = sb("posf", [P, TT])
        F = HEAD // 2
        ang, turns, red, half, s_half, sq = (sb(n, [P, TT, F]) for n in ("ang", "turns", "red", "half", "s_half", "sq"))
        prod = sb("prod", [P, 2, HEAD])
        dots = sb("dots", [P, 2])
        edots = sb("edots", [P, 2])
        diff = sb("diff", [P, 1])
        v, loaded, ready, sined, exped = sem("v"), sem("loaded"), sem("ready"), sem("sined"), sem("exped")
        block = ctx.enter_context(nc.Block())
        f0 = ROWS["inv_freq"][0]
        l0 = ROWS["lambdas"][0]

        @block.sync
        def _(sp):
            with nc.allow_non_contiguous_dma("512 positions, once"):
                sp.dma_start(posi[:], A["positions"].rearrange("(t p) -> p t", p=P)).then_inc(loaded, 16)

        @block.scalar
        def _(act):
            act.wait_ge(ready, 1)
            nc.scalar.activation(sinb[:], red[:], ACT.Sin).then_inc(sined, 1)
            nc.scalar.activation(s_half[:], half[:], ACT.Sin).then_inc(sined, 1)
            nc.scalar.activation(edots[:], dots[:], ACT.Exp).then_inc(exped, 1)

        @block.vector
        def _(dve):
            V = nc.vector
            ch = Chain(dve, v)
            dve.wait_ge(loaded, 16)
            ch.add(V.tensor_copy(posf[:], posi[:]))
            lams = rows[:, l0:l0 + 4 * HEAD].rearrange("p (a b d) -> p a b d", a=2, b=2)
            ch.add(V.tensor_tensor(prod[:], lams[:, :, 0, :], lams[:, :, 1, :], ALU.mult))
            ch.wait()
            ch.add(V.tensor_reduce(dots[:], prod[:], AX.X, ALU.add))
            ch.add(V.tensor_tensor(ang[:], posf[:].unsqueeze(2).broadcast_to([P, TT, F]),
                                   rows[:, f0:f0 + F].unsqueeze(1).broadcast_to([P, TT, F]), ALU.mult))
            ch.wait()
            sincos_reduced(V, ch, ang[:], turns[:], red[:])
            ch.add(V.tensor_scalar(half[:], red[:], 0.5, None, ALU.mult))
            ch.wait()
            V.engine_nop().then_inc(ready, 1)
            dve.wait_ge(sined, 2)
            ch.add(V.tensor_tensor(sq[:], s_half[:], s_half[:], ALU.mult))
            ch.wait()
            V.tensor_scalar(cosb[:], sq[:], -2.0, 1.0, ALU.mult, ALU.add)
            dve.wait_ge(exped, 1)
            ch.add(V.tensor_tensor(diff[:], edots[:, 1:2], edots[:, 0:1], ALU.subtract))
            ch.wait()
            V.tensor_scalar(lam_neg[:], diff[:], -LAM_INIT, None, ALU.add)


def queries_keys(nc, C, hT, w_qk, rows, cosb, sinb, qkT):
    NC_ = QK2 // BANK
    HC = BANK // HEAD
    F = HEAD // 2
    SLABS = 4
    with ExitStack() as ctx:
        sb, ps, sem = phase_tools(nc, ctx, "qk")
        x_hi, x_lo = sb("x_hi", [P, DK, SEQ], F32R), sb("x_lo", [P, DK, SEQ], F32R)
        w = sb("w", [P, SLABS, BANK])
        w_hi, w_lo = sb("w_hi", [P, SLABS, BANK], F32R), sb("w_lo", [P, SLABS, BANK], F32R)
        raw = sb("raw", [P, 2, TT, BANK])
        sq = sb("sq", [P, 2, BANK])
        sumsq = sb("sumsq", [P, TT, HC])
        meansq = sb("meansq", [P, TT, HC])
        rms = sb("rms", [P, TT, HC])
        guess, tmp, rstd = (sb(n, [P, TT, HC]) for n in ("guess", "tmp", "rstd"))
        normed = sb("normed", [P, BANK])
        gained = sb("gained", [P, BANK])
        prod = sb("prod", [P, 4, HC, F])
        rot = sb("rot", [P, TT, BANK])
        out = ps("out", [P, 4, BANK])
        tp = ps("tp", [P, 4, BANK])
        loaded = [sem(f"loaded{s}") for s in range(SLABS)]
        (x_hi_ready, x_ready, w_hi_ready, w_ready, slab_done, multiplied, raw_ready, squared, summed,
         mean_ready, rms_ready, v, rotated, turned, moved) = (
            sem(n) for n in ("x_hi_ready", "x_ready", "w_hi_ready", "w_ready", "slab_done", "multiplied",
                             "raw_ready", "squared", "summed", "mean_ready", "rms_ready", "v", "rotated",
                             "turned", "moved"))
        block = ctx.enter_context(nc.Block())
        V = nc.vector

        def wait_slab_multiplied(eng, s):
            c, k = divmod(s, DK)
            if k == DK - 1:
                eng.wait_ge(multiplied, TT * (c + 1))
            else:
                eng.wait_ge(slab_done, (DK - 1) * c + k + 1)

        @block.sync
        def _(sp):
            for c in range(NC_):
                for k in range(DK):
                    s = c * DK + k
                    if s >= SLABS:
                        sp.wait_ge(w_ready, s - SLABS + 1)
                    sp.dma_start(w[:, s % SLABS, :], w_qk[c][:, k, :]).then_inc(loaded[s % SLABS], 16)

        def turn(pe, c):
            pe.wait_ge(rotated, TT * (c + 1))
            for f in range(4):
                if c >= 1:
                    pe.wait_ge(moved, 4 * (c - 1) + f + 1)
                for t in range(TT):
                    last = nc.tensor.transpose(tp[:, f, t * P:(t + 1) * P], rot[:, t, f * P:(f + 1) * P],
                                               C["ident"][:])
                last.then_inc(turned, 1)

        @block.tensor
        def _(pe):
            for c in range(NC_):
                for k in range(DK):
                    s = c * DK + k
                    if c == 0:
                        pe.wait_ge(x_ready, k + 1)
                    pe.wait_ge(w_ready, s + 1)
                    for t in range(TT):
                        if c >= 1 and k == 0:
                            pe.wait_ge(raw_ready, TT * (c - 1) + t + 1)
                        for n, (xs, ws) in enumerate(((x_hi, w_hi), (x_lo, w_hi), (x_hi, w_lo))):
                            last = nc.tensor.matmul(out[:, t, :], xs[:, k, t * P:(t + 1) * P], ws[:, s % SLABS, :],
                                                    start=(k == 0 and n == 0), stop=(k == DK - 1 and n == 2),
                                                    skip_group_check=True)
                        if k == DK - 1:
                            last.then_inc(multiplied, 1)
                    if k < DK - 1:
                        last.then_inc(slab_done, 1)
                    if c >= 2 and k == 1:
                        turn(pe, c - 2)
            turn(pe, NC_ - 2)
            turn(pe, NC_ - 1)

        def split_hi(act, c, k):
            s = c * DK + k
            if c == 0:
                nc.scalar.copy(x_hi[:, k, :], hT[:, k, :]).then_inc(x_hi_ready, 1)
            act.wait_ge(loaded[s % SLABS], 16 * (s // SLABS + 1))
            if s >= SLABS:
                wait_slab_multiplied(act, s - SLABS)
            nc.scalar.copy(w_hi[:, s % SLABS, :], w[:, s % SLABS, :]).then_inc(w_hi_ready, 1)

        def take(act, c):
            for t in range(TT):
                act.wait_ge(multiplied, TT * c + t + 1)
                if c >= 2:
                    act.wait_ge(rotated, TT * (c - 2) + t + 1)
                nc.scalar.copy(raw[:, c % 2, t, :], out[:, t, :]).then_inc(raw_ready, 1)
                act.wait_ge(raw_ready, TT * c + t + 1)
                if TT * c + t >= 2:
                    act.wait_ge(summed, TT * c + t - 1)
                nc.scalar.activation(sq[:, t % 2, :], raw[:, c % 2, t, :], ACT.Square).then_inc(squared, 1)

        def root(act, c):
            act.wait_ge(mean_ready, c + 1)
            nc.scalar.activation(rms[:], meansq[:], ACT.Sqrt).then_inc(rms_ready, 1)

        def move(act, c):
            for f in range(4):
                act.wait_ge(turned, 4 * c + f + 1)
                nc.scalar.copy(qkT[:, 4 * c + f, :], tp[:, f, :]).then_inc(moved, 1)

        @block.scalar
        def _(act):
            for c in range(NC_):
                for k in range(DK):
                    if k == 3 and c >= 1:
                        take(act, c - 1)
                    if k == 4 and c >= 1:
                        root(act, c - 1)
                    if k == 6 and c >= 2:
                        move(act, c - 2)
                    split_hi(act, c, k)
            take(act, NC_ - 1)
            root(act, NC_ - 1)
            move(act, NC_ - 2)
            move(act, NC_ - 1)

        @block.gpsimd
        def _(pool):
            for s in range(NC_ * DK):
                pool.wait_ge(w_hi_ready, s + 1)
                nc.gpsimd.tensor_tensor(w_lo[:, s % SLABS, :], w[:, s % SLABS, :], w_hi[:, s % SLABS, :],
                                        ALU.subtract).then_inc(w_ready, 1)

        def sum_squares(dve, c):
            for t in range(TT):
                dve.wait_ge(squared, TT * c + t + 1)
                V.tensor_reduce(sumsq[:, t, :], sq[:, t % 2, :].rearrange("p (h d) -> p h d", h=HC), AX.X,
                                ALU.add).then_inc(summed, 1)
            dve.wait_ge(summed, TT * (c + 1))
            V.tensor_scalar(meansq[:], sumsq[:], 1.0 / HEAD, EPS, ALU.mult, ALU.add).then_inc(mean_ready, 1)

        def scales_of_heads(dve, ch, c):
            dve.wait_ge(rms_ready, c + 1)
            ch.add(V.reciprocal(guess[:], rms[:]))
            ch.wait()
            refined_rsqrt(V, ch, meansq[:], guess[:], tmp[:], rstd[:])
            if c >= 1:
                dve.wait_ge(turned, 4 * c)

        def rotate(ch, c, t):
            g = rows[:, c * BANK:(c + 1) * BANK]
            heads = lambda x: x.rearrange("p (h d) -> p h d", h=HC)
            ch.add(V.tensor_tensor(heads(normed[:]), heads(raw[:, c % 2, t, :]),
                                   rstd[:, t, :].unsqueeze(2).broadcast_to([P, HC, HEAD]), ALU.mult))
            ch.wait()
            ch.add(V.tensor_tensor(gained[:], normed[:], g, ALU.mult))
            ch.wait()
            x1, x2 = heads(gained[:])[:, :, 0:F], heads(gained[:])[:, :, F:HEAD]
            cb = cosb[:, t, :].unsqueeze(1).broadcast_to([P, HC, F])
            sn = sinb[:, t, :].unsqueeze(1).broadcast_to([P, HC, F])
            for n, (x, f) in enumerate(((x1, cb), (x2, sn), (x2, cb), (x1, sn))):
                ch.add(V.tensor_tensor(prod[:, n], x, f, ALU.mult))
            ch.wait()
            o = heads(rot[:, t, :])
            V.tensor_tensor(o[:, :, 0:F], prod[:, 0], prod[:, 1], ALU.subtract)
            V.tensor_tensor(o[:, :, F:HEAD], prod[:, 2], prod[:, 3], ALU.add).then_inc(rotated, 1)

        @block.vector
        def _(dve):
            for k in range(DK):
                dve.wait_ge(x_hi_ready, k + 1)
                V.tensor_tensor(x_lo[:, k, :], hT[:, k, :], x_hi[:, k, :], ALU.subtract).then_inc(x_ready, 1)
            ch = Chain(dve, v)
            for c in range(NC_):
                sum_squares(dve, c)
                scales_of_heads(dve, ch, c)
                for t in range(TT):
                    rotate(ch, c, t)


def block2(nc, C, h, hT, mods, g1, g2, A):
    scale1, scale2 = (C["scales"][:, i, :] for i in range(2))
    with ExitStack() as mid:
        sb, _, _ = phase_tools(nc, mid, "b2")
        qkT = sb("qkT", [P, QK2_TILES, SEQ])
        cosb = sb("cosb", [P, TT, HEAD // 2])
        sinb = sb("sinb", [P, TT, HEAD // 2])
        lam_neg = sb("lam_neg", [P, 1])
        with ExitStack() as ctx:
            sbr, _, _ = phase_tools(nc, ctx, "b2r")
            rows = sbr("rows", [P, NROWS])
            norm_transpose(nc, "n3", C, h, TT, D, hT, lambda k: scale1[:, k:k + 1], lambda k: mods[:, 0, k:k + 1],
                           transfers=[(rows[:], A["rows"].partition_broadcast(P))])
            rope_tables(nc, C, A, cosb, sinb, rows, lam_neg)
            queries_keys(nc, C, hT, A["w_qk_2"], rows, cosb, sinb, qkT)
        oaT = sb("oaT", [P, 2, SEQ])
        obT = sb("obT", [P, DIFF_HEADS, SEQ])
        with ExitStack() as ctx:
            sbv, _, _ = phase_tools(nc, ctx, "b2v")
            va = sbv("va", [P, TT, DIL_W])
            masks = sbv("masks", [P, TT, DIL_KEYS])
            value_product(nc, "va", hT, A["w_va_2"], DIL_W // 2, va, transfers=[(masks[:], A["masks"])])
            dilated_attention(nc, C, qkT, va, masks, oaT)
        with ExitStack() as ctx:
            sbv, _, _ = phase_tools(nc, ctx, "b2w")
            vb = sbv("vb", [P, TT, DIFF_W])
            value_product(nc, "vb", hT, A["w_vb_2"], BANK, vb)
            differential_attention(nc, C, qkT, vb, lam_neg, obT)
        tile_norm(nc, "fn3", C, obT, DIFF_HEADS, obT, lambda k: C["subln"][:, 0:1])
        mixT = sb("mixT", [P, DK, SEQ])
        gated_branches(nc, C, hT, oaT, obT, A, mixT, qkT[:, 0:DK])
        gated_add(nc, mixT, A["w_out_2"], g1, h)
    norm_transpose(nc, "n4", C, h, TT, D, hT, lambda k: scale2[:, k:k + 1], lambda k: mods[:, 2, k:k + 1],
                   transfers=[(A["h_scratch"].rearrange("(t p) d -> p t d", p=P), h[:])])
    with ExitStack() as ctx:
        block = ctx.enter_context(nc.Block())

        @block.vector
        def _(dve):
            nc.vector.memset(h[:], 0.0)
    peer(nc, "p2", C, h, hT, A["w_query_2"], A["sub_keys_2"], A["expert_u_2"], A["expert_v_2"], A["gates"], h)
    finish(nc, h, g2, A)


def value_product(nc, tag, hT, w, width, dst, transfers=()):
    product(nc, tag, hT, DK, SEQ, [(w[n], True, columns_to(nc, dst, n * width, width, TT)) for n in range(2)],
            SLABS=2, transfers=transfers)


def dilated_attention(nc, C, qkT, va, masks, oaT):
    items, outs = [], []
    for hd in range(DIL_HEADS):
        rows = slice(64 * (hd % 2), 64 * (hd % 2) + 64)

        def at(first, g):
            return (first + (g * DIL_HEADS + hd) * HEAD) // P
        for qt in range(TT):
            near = range(max(0, qt - 1), min(TT, qt + 2))
            scores, values = [], []
            for n, (g, tiles) in enumerate(((1, range(TT)), (2, range(TT)), (0, near))):
                q = qkT[rows, at(0, g), qt * P:(qt + 1) * P]
                k = qkT[rows, at(DIL_W, g), tiles[0] * P:(tiles[-1] + 1) * P]
                scores.append((n * SEQ, len(tiles) * P, [(q, k)]))
                f = (g * DIL_HEADS + hd) * HEAD
                values += [(n * TT + m, va[:, kt, f:f + HEAD]) for m, kt in enumerate(tiles)]
            width = 2 * SEQ + len(near) * P
            items.append(dict(scores=scores, width=width, bias=masks[:, qt, 0:width],
                              values=[(hd, rows, slice(qt * P, (qt + 1) * P), values)]))
        outs.append((rows, oaT[rows, hd // 2, :], TT * hd + TT - 1))
    attention(nc, "dat", C, items, outs, DIL_KEYS, HEAD ** -0.5, score_ring=1, turn_ring=3)


def differential_attention(nc, C, qkT, vb, lam_neg, obT):
    first_q, first_k = 2 * DIL_W // P, (2 * DIL_W + DIFF_W) // P
    items, outs = [], []
    for hd in range(DIFF_HEADS):
        for qt in range(TT):
            cols = slice(qt * P, (qt + 1) * P)
            scores = []
            for s in range(2):
                rows = slice(64 * s, 64 * s + 64)
                scores.append((s * SEQ, SEQ, [(qkT[rows, first_q + hd, cols], qkT[rows, first_k + hd, :])]))
            items.append(dict(scores=scores, width=SEQ, bias=None,
                              values=[(hd, slice(0, P), cols,
                                       [(kt, vb[:, kt, hd * P:(hd + 1) * P]) for kt in range(TT)])]))
        outs.append((slice(0, P), obT[:, hd, :], TT * hd + TT - 1))
    attention(nc, "dif", C, items, outs, SEQ, HEAD ** -0.5, parts=2, lam=lam_neg[:, 0:1])


def gated_branches(nc, C, hT, oaT, obT, A, mixT, sig):
    def gate(dst, n):
        return ON_ACT, lambda psum: [
            lambda: nc.scalar.activation(dst, psum, ACT.Sigmoid, bias=column(C, "b_gate")(n))]

    def weigh(dst):
        return ON_DVE, lambda psum: [lambda: nc.vector.tensor_tensor(dst, dst, psum, ALU.mult)]

    def weigh_and_add(f):
        return ON_DVE, lambda psum: [
            lambda: nc.vector.tensor_tensor(sig[:, f, :], sig[:, f, :], psum, ALU.mult),
            lambda: nc.vector.tensor_tensor(mixT[:, f, :], mixT[:, f, :], sig[:, f, :], ALU.add)]
    product(nc, "gl", hT, DK, SEQ,
            [(A["w_gate_2"][c], False, [gate((mixT if c < 2 else sig)[:, (4 * c + u) % DK, :], 4 * c + u)
                                        for u in range(4)]) for c in range(4)], SLABS=2)
    product(nc, "pa", oaT, 2, SEQ,
            [(A["w_proj_a_2"][c], False, [weigh(mixT[:, 4 * c + u, :]) for u in range(4)]) for c in range(2)], SLABS=2)
    product(nc, "pb", obT, DK, SEQ,
            [(A["w_proj_b_2"][c], False, [weigh_and_add(4 * c + u) for u in range(4)]) for c in range(2)], SLABS=2)


def gated_add(nc, mixT, w, g1, h):
    def add(t, half):
        cols = slice(half * BANK, (half + 1) * BANK)
        return ON_DVE, lambda psum: [
            lambda: nc.vector.tensor_tensor(psum, psum, g1[:, cols], ALU.mult),
            lambda: nc.vector.tensor_tensor(h[:, t, cols], h[:, t, cols], psum, ALU.add)]
    product(nc, "wo2", mixT, DK, SEQ, [(w[half], True, [add(t, half) for t in range(TT)]) for half in range(2)],
            SLABS=2)


def finish(nc, acc, g2, A):
    with ExitStack() as ctx:
        sb, _, sem = phase_tools(nc, ctx, "fi")
        hb = sb("hb", [P, TT, D])
        part = sb("part", [P, TT, D])
        res = sb("res", [P, TT, D])
        scaled, added = sem("scaled"), sem("added")
        h_in = [sem(f"h_in{t}") for t in range(TT)]
        stored = [sem(f"stored{t}") for t in range(TT)]
        block = ctx.enter_context(nc.Block())

        @block.sync
        def _(sp):
            for t in range(TT):
                sp.dma_start(hb[:, t, :], A["h_scratch"][t * P:(t + 1) * P, :]).then_inc(h_in[t], 16)
            for t in range(TT):
                sp.wait_ge(added, t + 1)
                sp.dma_start(A["out"][t * P:(t + 1) * P, :], res[:, t, :]).then_inc(stored[t], 16)
            for t in range(TT):
                sp.wait_ge(stored[t], 16)

        @block.vector
        def _(dve):
            for t in range(TT):
                nc.vector.tensor_tensor(part[:, t, :], acc[:, t, :], g2[:], ALU.mult).then_inc(scaled, 1)
            for t in range(TT):
                dve.wait_ge(h_in[t], 16)
                dve.wait_ge(scaled, t + 1)
                nc.vector.tensor_tensor(res[:, t, :], part[:, t, :], hb[:, t, :], ALU.add).then_inc(added, 1)


def scales(nc, C, mods):
    with ExitStack() as ctx:
        block = ctx.enter_context(nc.Block())

        @block.vector
        def _(dve):
            V = nc.vector
            for i, name in enumerate(("norm1_g", "norm2_g")):
                a = COLS[name][0]
                V.scalar_tensor_tensor(C["scales"][:, i, :], mods[:, 2 * i + 1, :], 1.0,
                                       C["cols"][:, a:a + 8], ALU.add, ALU.mult)
            V.tensor_scalar(C["subln"][:], column(C, "subln_g")(0), 1.0 - LAM_INIT, None, ALU.mult)


def program(nc, A, stop=None):
    with ExitStack() as ctx:
        C = constants(nc, ctx, A["cols"])
        sb, _, _ = phase_tools(nc, ctx, "main")
        h = sb("h", [P, TT, D])
        hT = sb("hT", [P, DK, SEQ])
        load(nc, "x", [(h[:], A["x"].rearrange("(t p) d -> p t d", p=P))])
        mods = sb("mods", [P, MODS, DK])
        g1 = sb("g1", [P, D])
        g2 = sb("g2", [P, D])
        C["scales"] = sb("scales", [P, 2, DK])
        C["subln"] = sb("subln", [P, 1])
        block1(nc, C, h, hT, A, Modulation(nc, C, A, mods, g1, g2))
        scales(nc, C, mods)
        block2(nc, C, h, hT, mods, g1, g2, A)


def lay_out(i):
    def one(name):
        return np.asarray(i[name])[0]

    def vec(x):
        return np.asarray(x).reshape(-1, P).T

    def tok(w, width):
        k, n = w.shape
        return np.ascontiguousarray(w.reshape(k // P, P, n // width, width).transpose(2, 1, 0, 3))

    def states(x):
        return x.reshape(STILES, P).T

    a = {"x": np.asarray(i["x"])[0], "mem": np.asarray(i["mem"])[0]}
    step = np.repeat(one("ssm_log_step")[:, None], STATES, axis=1)
    cols = {
        "att_q_g": vec(np.tile(one("att_q_g"), 2)), "att_k_g": vec(np.tile(one("att_k_g"), 2)),
        "ssm_d": vec(one("ssm_d").reshape(-1)),
        "lam": np.concatenate([states(one("ssm_lam_re")), states(one("ssm_lam_im")), states(step)], axis=1),
        "norm1_g": vec(one("norm1_g_2")), "norm2_g": vec(one("norm2_g_2")), "b_gate": vec(one("b_gate_2")),
        "b_ada": vec(one("b_ada_2")), "subln_g": vec(one("subln_g_2")), "c": vec(i["c_2"]),
    }
    for name in COLS:
        if name not in cols:
            cols[name] = vec(one(name))
    a["cols"] = np.ascontiguousarray(np.concatenate([cols[n] for n in COLS], axis=1))
    w_in = one("w_in")
    a["w_in"] = tok(w_in, BANK)
    dist = np.arange(P)[:, None] + (SEQ - P) - np.arange(SEQ)[None, :]
    bucket = np.clip(dist, -(CHUNK - 1), REL_MAX) + CHUNK - 1
    a["bias"] = np.ascontiguousarray(one("rel_bias")[:, bucket])
    bc = [one(n).reshape(STILES, P, GROUP).transpose(1, 0, 2) for n in ("ssm_b_re", "ssm_b_im")]
    bc += [one(n).transpose(0, 2, 1).reshape(STILES, P, GROUP).transpose(1, 0, 2) for n in ("ssm_c_re", "ssm_c_im")]
    a["ssm_bc"] = np.ascontiguousarray(np.stack(bc))
    a["w_glu"] = tok(one("ssm_w_glu"), P)
    a["w_out"] = tok(one("w_out"), BANK)
    for n in ("w_mem_q", "w_mem_k", "w_mem_v", "w_mem_o"):
        a[n] = tok(one(n), BANK)

    def experts(u):
        return np.ascontiguousarray(u.reshape(KEYS, P, DK, P).transpose(0, 3, 2, 1))

    def keys(k):
        return np.ascontiguousarray(k.reshape(HALVES, KEYS, P).transpose(2, 0, 1))
    a["w_peer_q"], a["peer_keys"] = tok(one("w_peer_q"), BANK), keys(one("peer_keys"))
    a["peer_u"], a["peer_v"] = experts(one("peer_u")), one("peer_v").reshape(KEYS, P, D)
    a["w_query_2"], a["sub_keys_2"] = tok(one("w_query_2"), BANK), keys(one("sub_keys_2"))
    a["expert_u_2"], a["expert_v_2"] = experts(one("expert_u_2")), one("expert_v_2").reshape(KEYS, P, D)

    w2 = one("w_in_2")
    s = np.cumsum([0, DIL_W, DIL_W, DIL_W, DIFF_W, DIFF_W, DIFF_W, 2 * D])
    a["w_qk_2"] = tok(np.concatenate([w2[:, s[0]:s[2]], w2[:, s[3]:s[5]]], axis=1), BANK)
    a["w_va_2"] = tok(w2[:, s[2]:s[3]], DIL_W // 2)
    a["w_vb_2"] = tok(w2[:, s[5]:s[6]], BANK)
    a["w_gate_2"] = tok(w2[:, s[6]:s[7]], BANK)
    a["w_proj_a_2"], a["w_proj_b_2"] = tok(one("w_proj_a_2"), BANK), tok(one("w_proj_b_2"), BANK)
    a["w_out_2"], a["w_ada"] = tok(one("w_out_2"), BANK), tok(one("w_ada_2"), BANK)
    b_ada = one("b_ada_2").reshape(6, D)
    a["ada_rows"] = np.ascontiguousarray(np.stack([b_ada[2], b_ada[5]]))
    a["positions"] = np.asarray(i["positions_2"])[0]
    half = np.arange(0, HEAD, 2, dtype=np.float32) / np.float32(HEAD)
    inv_freq = (np.float32(1.0) / (np.float32(10000.0) ** half)).astype(np.float32)
    gains = [np.tile(one(n), w // HEAD) for n, w in (("qn_a_2", DIL_W), ("kn_a_2", DIL_W), ("qn_b_2", DIFF_W),
                                                     ("kn_b_2", DIFF_W))]
    lams = [one(n) for n in ("lam_q1_2", "lam_k1_2", "lam_q2_2", "lam_k2_2")]
    a["rows"] = np.concatenate(gains + [inv_freq] + lams)
    q = np.arange(SEQ)[:, None]
    k = np.arange(SEQ)[None, :]
    masks = np.full((SEQ, 2 * SEQ + 3 * P), MASKED, np.float32)
    allowed = [((q - k) % r == 0) & (np.abs(q - k) <= w // 2) for w, r in DIL]
    masks[:, 0:SEQ] = np.where(allowed[1], 0.0, MASKED)
    masks[:, SEQ:2 * SEQ] = np.where(allowed[2], 0.0, MASKED)
    for t in range(TT):
        a0, a1 = max(0, t - 1) * P, min(TT, t + 2) * P
        rows = slice(t * P, (t + 1) * P)
        masks[rows, 2 * SEQ:2 * SEQ + a1 - a0] = np.where(allowed[0][rows, a0:a1], 0.0, MASKED)
    a["masks"] = np.ascontiguousarray(masks.reshape(TT, P, -1).transpose(1, 0, 2))
    return a


def build(nc, arrays):
    A = {n: nc.dram_tensor(f"in_{n}", x.shape, mybir.dt.from_np(x.dtype), kind="ExternalInput").ap()
         for n, x in arrays.items()}
    A["gates"] = nc.dram_tensor("gates", (KEYS // EGROUP, P, SEQ // PIECE, EGROUP, PIECE), F32).ap()
    A["h_scratch"] = nc.dram_tensor("h_scratch", (SEQ, D), F32).ap()
    A["out"] = nc.dram_tensor("out_0", (SEQ, D), F32, kind="ExternalOutput").ap()
    program(nc, A)


def kernel(**inputs):
    import concourse.bacc as bacc
    from concourse.bass_utils import run_bass_kernel_spmd
    arrays = lay_out(inputs)
    nc = bacc.Bacc("TRN2", target_bir_lowering=False, num_devices=1)
    build(nc, arrays)
    r = run_bass_kernel_spmd(nc, [{f"in_{n}": x for n, x in arrays.items()}], core_ids=[0])
    return r.results[0]["out_0"].reshape(1, SEQ, D)
```
